# Optimizing a Trainium2 kernel written in Bass

```python
import math
import jax
import jax.numpy as jnp
from jax import lax
import numpy as np

D_MODEL = 1024
BATCH = 1
SEQ = 512
DEPTH = 1
DEC_BATCH = 8
DEC_SEQ = 4
PAST_LEN = 4096
PAGE_SIZE = 128

SB_HEADS = 8
SB_HEAD_DIM = 64
SB_WIDTH = SB_HEADS * SB_HEAD_DIM
SB_Q_BLOCK = 128
SB_BIAS_INIT = -6.0
HG_HEADS = 8
HG_DK = 64
HG_DV = 64
HG_WIDTH_K = HG_HEADS * HG_DK
HG_WIDTH_V = HG_HEADS * HG_DV
HG_CHUNK = 32
N_GROUPS = 4
EXPERTS_PER_GROUP = 8
N_EXPERTS = N_GROUPS * EXPERTS_PER_GROUP
TOP_K = 2
D_FF_EXPERT = 512
MOE_BLOCK = 64
RMS_EPS = 1e-6
D_IN = 3 * SB_WIDTH + 2 * HG_WIDTH_K + 2 * HG_WIDTH_V + 2 * D_MODEL

kernel_name = "hybrid_stickbreak_hgrn2_hmoe_step"

def rms_norm(x, w):
    xf = x.astype(jnp.float32)
    y = xf * lax.rsqrt(jnp.mean(xf * xf, axis=-1, keepdims=True) + RMS_EPS)
    return (y * w.astype(jnp.float32)).astype(x.dtype)

def mixer_inputs(x, norm1_w, w_in, q_norm_w, k_norm_w, lb):
    B, T, _ = x.shape
    h = rms_norm(x, norm1_w) @ w_in
    sizes = (SB_WIDTH, SB_WIDTH, SB_WIDTH, HG_WIDTH_K, HG_WIDTH_K, HG_WIDTH_V, HG_WIDTH_V, D_MODEL)
    pts = []
    acc = 0
    for s in sizes:
        acc += s
        pts.append(acc)
    q_sb, k_sb, v_sb, q_hg, f_hg, i_hg, g_hg, gate_a, gate_b = jnp.split(h, pts, axis=-1)
    q_sb = rms_norm(q_sb.reshape(B, T, SB_HEADS, SB_HEAD_DIM), q_norm_w)
    k_sb = rms_norm(k_sb.reshape(B, T, SB_HEADS, SB_HEAD_DIM), k_norm_w)
    v_sb = v_sb.reshape(B, T, SB_HEADS, SB_HEAD_DIM)
    f = lb + (1.0 - lb) * jax.nn.sigmoid(f_hg.astype(jnp.float32))
    log_f = jnp.log(f).reshape(B, T, HG_HEADS, HG_DK)
    k_hg = (1.0 - f).reshape(B, T, HG_HEADS, HG_DK)
    q_hg = q_hg.astype(jnp.float32).reshape(B, T, HG_HEADS, HG_DK)
    i_hg = i_hg.astype(jnp.float32).reshape(B, T, HG_HEADS, HG_DV)
    return q_sb, k_sb, v_sb, q_hg, log_f, k_hg, i_hg, g_hg, gate_a, gate_b

def stick_breaking_weights(z, mask):
    log_keep = jnp.where(mask, jax.nn.log_sigmoid(-z), 0.0)
    remain = lax.cumsum(log_keep, axis=z.ndim - 1, reverse=True)
    return jnp.exp(jnp.where(mask, z + remain, -jnp.inf))

def sb_prompt(q, k, v, bias):
    B, T, H, Dh = q.shape
    scale = Dh ** -0.5
    b = bias.astype(jnp.float32)[None, :, None, None]
    outs = []
    for blk in range(T // SB_Q_BLOCK):
        lo = blk * SB_Q_BLOCK
        hi = lo + SB_Q_BLOCK
        z = jnp.einsum('bqhd,bkhd->bhqk', q[:, lo:hi], k[:, :hi]).astype(jnp.float32) * scale + b
        mask = jnp.arange(hi)[None, :] < jnp.arange(lo, hi)[:, None]
        a = stick_breaking_weights(z, mask).astype(v.dtype)
        outs.append(jnp.einsum('bhqk,bkhd->bqhd', a, v[:, :hi]))
    return jnp.concatenate(outs, axis=1)

def sb_decode(q, k_new, v_new, k_past, v_past, bias):
    Tq = q.shape[1]
    P = k_past.shape[1]
    scale = q.shape[-1] ** -0.5
    z_past = jnp.einsum('bqhd,bkhd->bhqk', q, k_past).astype(jnp.float32)
    z_new = jnp.einsum('bqhd,bkhd->bhqk', q, k_new).astype(jnp.float32)
    z = jnp.concatenate([z_past, z_new], axis=-1) * scale + bias.astype(jnp.float32)[None, :, None, None]
    mask = jnp.concatenate([jnp.ones((Tq, P), dtype=bool),
                            jnp.arange(Tq)[None, :] < jnp.arange(Tq)[:, None]], axis=-1)
    a = stick_breaking_weights(z, mask).astype(v_new.dtype)
    return (jnp.einsum('bhqk,bkhd->bqhd', a[..., :P], v_past)
            + jnp.einsum('bhqk,bkhd->bqhd', a[..., P:], v_new))

def hgrn2_chunked(q, log_f, k, v, s0):
    B, T, H, Dk = q.shape
    Dv = v.shape[-1]
    c = HG_CHUNK if T % HG_CHUNK == 0 else T
    n = T // c

    def to_chunks(a):
        return a.reshape(B, n, c, H, a.shape[-1]).transpose(1, 0, 3, 2, 4)

    causal = jnp.tril(jnp.ones((c, c), dtype=bool))

    def step(s, inp):
        qc, gc, kc, vc = inp
        g_cum = jnp.cumsum(gc, axis=2)
        g_last = g_cum[:, :, -1:, :]
        q_dec = qc * jnp.exp(g_cum)
        k_dec = kc * jnp.exp(-g_cum)
        scores = jnp.where(causal, jnp.einsum('bhtk,bhsk->bhts', q_dec, k_dec), 0.0)
        o = jnp.einsum('bhtk,bhkv->bhtv', q_dec, s) + jnp.einsum('bhts,bhsv->bhtv', scores, vc)
        s_new = (jnp.exp(g_last[:, :, 0, :])[..., None] * s
                 + jnp.einsum('bhsk,bhsv->bhkv', kc * jnp.exp(g_last - g_cum), vc))
        return s_new, o

    s_fin, o = lax.scan(step, s0, (to_chunks(q), to_chunks(log_f), to_chunks(k), to_chunks(v)))
    o = o.transpose(1, 0, 3, 2, 4).reshape(B, T, H, Dv)
    return o, s_fin

def mixer_output(x, o_sb, o_hg, g_hg, gate_a, gate_b, hg_norm_w, w_branch_a, w_branch_b, w_out):
    B, T, _ = x.shape
    y_b = (rms_norm(o_hg, hg_norm_w).reshape(B, T, HG_WIDTH_V)
           * jax.nn.silu(g_hg.astype(jnp.float32))).astype(x.dtype)
    ya = o_sb.reshape(B, T, SB_WIDTH) @ w_branch_a
    yb = y_b @ w_branch_b
    merged = jax.nn.sigmoid(gate_a) * ya + jax.nn.sigmoid(gate_b) * yb
    return x + merged @ w_out

def hier_moe(x2d, w_gr, b_gr, w_er, b_er, w_g, w_u, w_d):
    n_tok, d = x2d.shape
    g_logits = (x2d @ w_gr).astype(jnp.float32) + b_gr.astype(jnp.float32)
    g_prob = jax.nn.softmax(g_logits, axis=-1)
    p_group, g_idx = lax.top_k(g_prob, 1)
    e_logits = (x2d @ w_er).astype(jnp.float32) + b_er.astype(jnp.float32)
    e_logits = e_logits.reshape(n_tok, N_GROUPS, EXPERTS_PER_GROUP)[jnp.arange(n_tok), g_idx[:, 0]]
    e_prob = jax.nn.softmax(e_logits, axis=-1)
    w_top, e_loc = lax.top_k(e_prob, TOP_K)
    w_top = p_group * w_top / jnp.sum(w_top, axis=-1, keepdims=True)
    e_glob = g_idx * EXPERTS_PER_GROUP + e_loc

    n_assign = n_tok * TOP_K
    e_flat = e_glob.reshape(-1)
    w_flat = w_top.reshape(-1)
    tok_flat = jnp.repeat(jnp.arange(n_tok, dtype=jnp.int32), TOP_K)
    order = jnp.argsort(e_flat)
    e_sorted = e_flat[order]
    counts = jnp.bincount(e_flat, length=N_EXPERTS)
    starts = jnp.cumsum(counts) - counts
    padded = ((counts + MOE_BLOCK - 1) // MOE_BLOCK) * MOE_BLOCK
    pad_ends = jnp.cumsum(padded)
    pad_starts = pad_ends - padded
    dest = pad_starts[e_sorted] + (jnp.arange(n_assign) - starts[e_sorted])
    n_blocks = -(-(n_assign + N_EXPERTS * (MOE_BLOCK - 1)) // MOE_BLOCK)
    n_rows = n_blocks * MOE_BLOCK
    row_tok = jnp.zeros((n_rows,), jnp.int32).at[dest].set(tok_flat[order])
    row_w = jnp.zeros((n_rows,), jnp.float32).at[dest].set(w_flat[order])
    block_exp = jnp.clip(jnp.searchsorted(pad_ends, jnp.arange(n_blocks) * MOE_BLOCK, side='right'),
                         0, N_EXPERTS - 1)

    def run_block(args):
        toks, e = args
        xb = x2d[toks]
        hb = jax.nn.silu(xb @ w_g[e]) * (xb @ w_u[e])
        return hb @ w_d[e]

    out = lax.map(run_block, (row_tok.reshape(n_blocks, MOE_BLOCK), block_exp))
    contrib = (out.reshape(n_rows, d).astype(jnp.float32) * row_w[:, None]).astype(x2d.dtype)
    return jnp.zeros((n_tok, d), x2d.dtype).at[row_tok].add(contrib)

def channel_mixer(x, norm2_w, w_gr, b_gr, w_er, b_er, w_g, w_u, w_d):
    B, T, d = x.shape
    h = rms_norm(x, norm2_w).reshape(B * T, d)
    return x + hier_moe(h, w_gr, b_gr, w_er, b_er, w_g, w_u, w_d).reshape(B, T, d)

def setup_inputs(seed: int = 0) -> dict:
    key = jax.random.key(seed)
    ks = jax.random.split(key, 24)
    f32 = jnp.float32
    n_pages = PAST_LEN // PAGE_SIZE
    n_used = DEC_BATCH * n_pages
    n_pool = n_used + n_used // 4

    def nrm(k, shape, scale):
        return jax.random.normal(k, shape, f32) * scale

    return {
        "x_prompt": nrm(ks[0], (BATCH, SEQ, D_MODEL), 1.0),
        "x_sample": nrm(ks[1], (DEC_BATCH, DEC_SEQ, D_MODEL), 1.0),
        "cache_k": nrm(ks[2], (DEPTH, n_pool, PAGE_SIZE, SB_HEADS, SB_HEAD_DIM), 1.0),
        "cache_v": nrm(ks[3], (DEPTH, n_pool, PAGE_SIZE, SB_HEADS, SB_HEAD_DIM), 1.0),
        "page_table": jax.random.permutation(ks[4], n_pool)[:n_used].reshape(DEC_BATCH, n_pages).astype(jnp.int32),
        "state_hgrn": nrm(ks[5], (DEPTH, DEC_BATCH, HG_HEADS, HG_DK, HG_DV), 0.5),
        "norm1_w": 1.0 + nrm(ks[6], (DEPTH, D_MODEL), 0.01),
        "w_in": nrm(ks[7], (DEPTH, D_MODEL, D_IN), D_MODEL ** -0.5),
        "q_norm_w": 1.0 + nrm(ks[8], (DEPTH, SB_HEAD_DIM), 0.01),
        "k_norm_w": 1.0 + nrm(ks[9], (DEPTH, SB_HEAD_DIM), 0.01),
        "sb_bias": SB_BIAS_INIT + nrm(ks[23], (DEPTH, SB_HEADS), 0.1),
        "lb_logits": nrm(ks[10], (DEPTH + 1, HG_WIDTH_K), 0.1),
        "hg_norm_w": 1.0 + nrm(ks[11], (DEPTH, HG_DV), 0.01),
        "w_branch_a": nrm(ks[12], (DEPTH, SB_WIDTH, D_MODEL), SB_WIDTH ** -0.5),
        "w_branch_b": nrm(ks[13], (DEPTH, HG_WIDTH_V, D_MODEL), HG_WIDTH_V ** -0.5),
        "w_out": nrm(ks[14], (DEPTH, D_MODEL, D_MODEL), D_MODEL ** -0.5),
        "norm2_w": 1.0 + nrm(ks[15], (DEPTH, D_MODEL), 0.01),
        "w_group_router": nrm(ks[16], (DEPTH, D_MODEL, N_GROUPS), D_MODEL ** -0.5),
        "b_group_router": nrm(ks[17], (DEPTH, N_GROUPS), 0.01),
        "w_expert_router": nrm(ks[18], (DEPTH, D_MODEL, N_EXPERTS), D_MODEL ** -0.5),
        "b_expert_router": nrm(ks[19], (DEPTH, N_EXPERTS), 0.01),
        "w_gate_exp": nrm(ks[20], (DEPTH, N_EXPERTS, D_MODEL, D_FF_EXPERT), D_MODEL ** -0.5),
        "w_up_exp": nrm(ks[21], (DEPTH, N_EXPERTS, D_MODEL, D_FF_EXPERT), D_MODEL ** -0.5),
        "w_down_exp": nrm(ks[22], (DEPTH, N_EXPERTS, D_FF_EXPERT, D_MODEL), D_FF_EXPERT ** -0.5),
    }

def reference(x_prompt, x_sample, cache_k, cache_v, page_table, state_hgrn, norm1_w, w_in, q_norm_w,
              k_norm_w, sb_bias, lb_logits, hg_norm_w, w_branch_a, w_branch_b, w_out, norm2_w, w_group_router,
              b_group_router, w_expert_router, b_expert_router, w_gate_exp, w_up_exp, w_down_exp):
    xp = x_prompt
    xs = x_sample
    B = xp.shape[0]
    Bd = xs.shape[0]
    n_pages = page_table.shape[1]
    lbs = jnp.cumsum(jax.nn.softmax(lb_logits.astype(jnp.float32), axis=0), axis=0)
    kp_l, vp_l, sp_l, ks_l, vs_l, ss_l = [], [], [], [], [], []
    for l in range(DEPTH):
        lb = lbs[l]
        q, k, v, hq, hf, hk, hi, hg, ga, gb = mixer_inputs(xp, norm1_w[l], w_in[l], q_norm_w[l], k_norm_w[l], lb)
        o_sb = sb_prompt(q, k, v, sb_bias[l])
        o_hg, s_p = hgrn2_chunked(hq, hf, hk, hi, jnp.zeros((B, HG_HEADS, HG_DK, HG_DV), jnp.float32))
        xp = mixer_output(xp, o_sb, o_hg, hg, ga, gb, hg_norm_w[l], w_branch_a[l], w_branch_b[l], w_out[l])
        xp = channel_mixer(xp, norm2_w[l], w_group_router[l], b_group_router[l], w_expert_router[l],
                           b_expert_router[l], w_gate_exp[l], w_up_exp[l], w_down_exp[l])
        kp_l.append(k)
        vp_l.append(v)
        sp_l.append(s_p)
        q, k, v, hq, hf, hk, hi, hg, ga, gb = mixer_inputs(xs, norm1_w[l], w_in[l], q_norm_w[l], k_norm_w[l], lb)
        k_past = cache_k[l][page_table].reshape(Bd, n_pages * PAGE_SIZE, SB_HEADS, SB_HEAD_DIM)
        v_past = cache_v[l][page_table].reshape(Bd, n_pages * PAGE_SIZE, SB_HEADS, SB_HEAD_DIM)
        o_sb = sb_decode(q, k, v, k_past, v_past, sb_bias[l])
        o_hg, s_s = hgrn2_chunked(hq, hf, hk, hi, state_hgrn[l].astype(jnp.float32))
        xs = mixer_output(xs, o_sb, o_hg, hg, ga, gb, hg_norm_w[l], w_branch_a[l], w_branch_b[l], w_out[l])
        xs = channel_mixer(xs, norm2_w[l], w_group_router[l], b_group_router[l], w_expert_router[l],
                           b_expert_router[l], w_gate_exp[l], w_up_exp[l], w_down_exp[l])
        ks_l.append(k)
        vs_l.append(v)
        ss_l.append(s_s)
    new_k_prompt = jnp.stack(kp_l, axis=0)
    new_v_prompt = jnp.stack(vp_l, axis=0)
    new_hgrn_prompt = jnp.stack(sp_l, axis=0)
    new_k_sample = jnp.stack(ks_l, axis=0)
    new_v_sample = jnp.stack(vs_l, axis=0)
    new_hgrn_sample = jnp.stack(ss_l, axis=0)
    return (xp, xs, new_k_prompt, new_v_prompt, new_hgrn_prompt, new_k_sample, new_v_sample, new_hgrn_sample)


_drawn_inputs = setup_inputs


def setup_inputs(seed=0):
    import zlib

    import numpy as np

    out = dict(_drawn_inputs(seed))
    spreads = {}
    factors = {'norm1_w': 2.885,
     'q_norm_w': 8.0,
     'k_norm_w': 5.229,
     'sb_bias': 13.775,
     'hg_norm_w': 7.348,
     'norm2_w': 3.977,
     'b_group_router': 41.04,
     'b_expert_router': 3.963}
    for name, (base, spread) in spreads.items():
        noise = np.random.default_rng([zlib.crc32(name.encode()), seed]).standard_normal(out[name].shape)
        drawn = base * np.exp(spread * noise) if base else spread * noise
        out[name] = jnp.asarray(drawn.astype(out[name].dtype))
    for name, factor in factors.items():
        out[name] = (out[name] * factor).astype(out[name].dtype)
    return out
```

```python
from contextlib import ExitStack

import concourse.bass as bass
from concourse import mybir

F32 = mybir.dt.float32
I32 = mybir.dt.int32
U32 = mybir.dt.uint32
ALU = mybir.AluOpType
ACT = mybir.ActivationFunctionType
AX_X = mybir.AxisListType.X

P = 128
D = 1024
KD = D // P
SEQ = 512
NB = 8
TQ = 4
TS = NB * TQ
T = SEQ + TS
TH = T // 2
NT = 5
ROWS = [P] * 4 + [TS]
H = 8
DH = 64
CT = H * DH // P
W = H * DH
PAGE = 128
NPAGES = 32
GP = 4
NGRP = NPAGES // GP
CHUNK = 32
NE = 32
NG = 4
EG = NE // NG
FF = 512
FJ = FF // P
BLK = 64
KMAX = T // BLK
NOVF = 2 * T // BLK
NBLK = NE + NOVF
SCALE = float(DH) ** -0.5
EPS = 1e-6
BIG = 1e30
AZ = 1280
SB_OFF = [0, 512, 1024, 896]
SB_LEN = [512, 384, 256, 128]


class Chain:

    def __init__(self, eng, sem):
        self.eng, self.sem, self.n, self.base = eng, sem, 0, 0

    def __call__(self, ins):
        ins.then_inc(self.sem, 1)
        self.n += 1

    def wait(self):
        self.eng.wait_ge(self.sem, self.base + self.n)


def hybrid_step(nc, a):
    ctx = ExitStack()
    with ctx:
        def sb(name, shape, dt=F32):
            return ctx.enter_context(nc.sbuf_tensor(name, shape, dt))

        signals = {}

        def S(name):
            if name not in signals:
                signals[name] = ctx.enter_context(nc.semaphore(name))
            return signals[name]

        ps = ctx.enter_context(nc.psum_tensor("ps", [P, 8, 512], F32))
        xg_dram = nc.dram_tensor("expert_rows", [NBLK * BLK, D], F32).ap()
        yg_dram = nc.dram_tensor("expert_outs", [NBLK * BLK, D], F32).ap()

        ident = sb("ident", [P, P])
        ones = sb("ones", [P, P])
        tri_ge = sb("tri_ge", [P, P])
        headones = sb("headones", [P, P])
        mask_lt = sb("mask_lt", [P, P])
        neg_lt = sb("neg_lt", [P, P])
        tri_le = sb("tri_le", [P, P])
        chk_le = sb("chk_le", [P, P])
        chk_gt = sb("chk_gt", [P, P])
        sq_le = sb("sq_le", [TS, TS])
        sq_gt = sb("sq_gt", [TS, TS])
        new_m = sb("new_m", [TS, 256])
        new_neg = sb("new_neg", [TS, 256])
        in_b = sb("in_b", [TS, NB])
        w1c = sb("w1c", [P, KD])
        qkg = sb("qkg", [P, 3])
        bias8 = sb("bias8", [P, H])
        bias32 = sb("bias32", [P, 32])
        ss = sb("ss", [P, 8])
        rstd = sb("rstd", [P, 8])
        ss2 = sb("ss2", [P, 8])
        rstd2 = sb("rstd2", [P, 8])

        hT = sb("hT", [P, KD, T])
        osbT = sb("osbT", [P, CT, T])
        ybT = sb("ybT", [P, CT, T])
        ARENA = 40960
        arena = sb("arena", [P, ARENA])

        def carve(off, *dims):
            n = 1
            for d in dims:
                n *= d
            assert off + n <= ARENA, (off, dims)
            v = arena[:, off:off + n]
            if len(dims) == 2:
                v = v.rearrange("p (a b) -> p a b", a=dims[0])
            if len(dims) == 3:
                v = v.rearrange("p (a b c) -> p a b c", a=dims[0], b=dims[1])
            return v

        wring = carve(0, 3, KD, 512)
        qT = carve(12288, CT, T)
        kT = carve(14464, CT, T)
        vtok = carve(16640, NT, W)
        hqT = carve(19200, CT, T)
        ftok = carve(21376, NT, W)
        itok = carve(23936, NT, W)
        gT = carve(26496, CT, T)
        A0 = 28672
        xt = carve(A0, NT, D)
        kout = carve(A0 + 5120, NT, W)
        sq = carve(A0 + 7680, CT, T)
        rs = carve(A0 + 9856, CT, T)
        a_z = carve(A0, AZ)
        a_e = carve(A0 + 1280, AZ)
        a_ln = carve(A0 + 2560, AZ)
        a_t = carve(A0 + 3840, AZ)
        a_L = carve(A0 + 8960, AZ)
        a_A = carve(A0 + 5120, 2, AZ)

        state = carve(0, 8, CT, P)
        state0 = carve(4096, NB, CT, P)
        ib = carve(8192, NB, W)
        g0 = A0
        lbr = carve(g0, 2, W)
        lb = carve(g0 + 1024, W)
        oml = carve(g0 + 1536, W)
        ktok = carve(g0 + 2048, W)
        g_e = carve(g0 + 2560, W)
        g_en = carve(g0 + 3072, W)
        g_e2 = carve(g0 + 3584, W)
        qd = carve(g0 + 4096, CT, P)
        kd = carve(g0 + 4608, CT, P)
        kdec = carve(g0 + 5120, W)
        scm = carve(g0 + 5632, H, P)

        d_kt = carve(0, 2, GP, 512)
        D0 = 4096
        d_z = carve(D0, 2, 128)
        d_e = carve(D0 + 256, 2, 128)
        d_ln = carve(D0 + 512, 2, 128)
        d_t = carve(D0 + 768, 2, 128)
        d_L = carve(D0 + 1024, 2, 128)
        d_R = carve(D0 + 1280, 4, 128)
        d_A = carve(D0 + 1792, 4, 128)
        qblk = carve(D0 + 2304, NB, 32)
        obase = carve(D0 + 2560, CT, 64)
        n_z = carve(D0 + 2816, 256)
        n_e = carve(D0 + 3072, 256)
        n_t = carve(D0 + 3328, 256)
        n_L = carve(D0 + 3584, 256)
        carry0 = carve(D0 + 3840, NB, 32)
        n_s = carve(D0 + 4096, 256)
        vring = carve(16384, NGRP, GP, 512)
        kring = carve(32768, 4, GP, 512)

        gw = carve(0, 2, KD, 512)
        wab = carve(8192, 2, CT, D)
        mrg = carve(16384, KD, T)
        m_sa = carve(20736, 2, T)
        m_sb = carve(21824, 2, T)
        x2 = carve(22912, NT, D)
        wo = carve(0, KD, D)
        h2 = carve(8192, NT, D)
        h2T = carve(13312, 2, KD, P)
        w2r = carve(15360, D)
        wr = carve(20736, KD, 36)
        sqj = carve(13312, D)

        we = [carve(28672, 3, 4096), carve(0, 3, 4096)]
        M0 = 12288
        xg = carve(M0, 2, D)
        xgT = carve(M0 + 2048, 2, KD, BLK)
        m_s = carve(M0 + 3072, 2, FJ * BLK)
        m_h = carve(M0 + 3584, 2, FJ, BLK)
        m_y = carve(M0 + 4096, 2, D)
        wgv = [w[:, 0, :].rearrange("p (k f) -> p k f", k=KD) for w in we]
        wuv = [w[:, 1, :].rearrange("p (k f) -> p k f", k=KD) for w in we]
        wdv = [w[:, 2, :].rearrange("p (k f) -> p k f", k=FJ) for w in we]
        yg = carve(0, 4, D)

        route = carve(21056, 1536)
        tab = sb("tab", [P, 32], I32)
        slot_i = sb("slot_i", [P, 2 * NT], I32)
        wts = sb("wts", [P, 2 * NT])

        x_tok = [a["x_prompt"][0, P * i:P * i + P, :] for i in range(4)] + [
            a["x_sample"].rearrange("b q d -> (b q) d")]
        w_in = a["w_in"][0].rearrange("(p k) n -> p k n", k=KD)
        w_br = [a[n][0].rearrange("(c p) n -> p c n", p=P) for n in ("w_branch_a", "w_branch_b")]

        CHUNKS = [("cols", qT), ("cols", kT), ("rows", vtok), ("cols", hqT), ("rows", ftok), ("rows", itok),
                  ("cols", gT)]
        JOBS = [(c, j) for c, (kind, _) in enumerate(CHUNKS) for j in range(4 if kind == "cols" else NT)]
        CHUNK_END = [max(n for n, (c, _) in enumerate(JOBS) if c == cc) + 1 for cc in range(len(CHUNKS))]
        QKV = CHUNK_END[2]
        KV_BANK = [5, 6, 7, 0]
        GATE_CHUNKS = [7, 9, 8, 10]

        def flat(v):
            return v.rearrange("p a b -> p (a b)")

        def each(v, n):
            return v.rearrange("p (a b) -> p a b", a=n)

        def diag3(off):
            return each(arena[:, off:off + 1536], 3)[:, :, 0:P]

        ps_attn = ps[:, 0:3, :].rearrange("p b c -> p (b c)")[:, 0:AZ]
        ps_h2 = ps[:, 4:6, :].rearrange("p b (k m) -> p (b k) m", k=4)
        kout_flat = kout.rearrange("p a b -> p (a b)")
        a_z_off, a_L_off = A0, A0 + 8960
        LOSS_STEPS = 6

        taken = [0]

        def small(n, rows=None):
            o = taken[0]
            taken[0] += n
            assert taken[0] <= 1536
            return route[:, o:o + n]

        gcol_i, ecol_i = small(NE).bitcast(I32), small(NE).bitcast(I32)
        gcol, ecol, r_b36, r_lg = small(NE), small(NE), small(NG + NE), small(NG + NE)
        r_gl, r_gm, r_gi, r_em, r_ei = small(8), small(8), small(8).bitcast(U32), small(8), small(8).bitcast(U32)
        r_ng, r_gf, r_ge, r_gs, r_e2, r_gap, r_t1 = (small(k) for k in (1, 1, NG, 1, 1, 1, 1))
        r_m, r_n, r_el, r_j = small(NE), small(NE), small(NE), small(NE)
        r_O = small(NE * NT)
        r_Ok = small(2 * NT * NE).rearrange("p (a b) -> p a b", a=2 * NT)
        r_rank, r_ov, r_cnt, r_base, r_ind, r_incl = (small(k) for k in (NE * NT, P, P, NE, NOVF, 1))
        r_EI, r_RK, r_BK = small(2 * NT), small(2 * NT), small(2 * NT)

        block = ctx.enter_context(nc.Block())

        @block.sync
        def _(sp):
            for i in range(NT):
                sp.dma_start(xt[0:ROWS[i], i, :], x_tok[i]).then_inc(S("x_loaded"), 16)
            for c in range(len(CHUNKS)):
                if c >= 3:
                    sp.wait_ge(S("projected"), CHUNK_END[c - 3])
                sp.dma_start(wring[:, c % 3], w_in[:, :, 512 * c:512 * c + 512]).then_inc(S(f"w_in_{c % 3}"), 16)
                if c == 5:
                    sp.wait_ge(S("projection_out"), QKV)
                    sp.dma_start(a["new_v_prompt"][0, 0].rearrange("(i p) h d -> p i (h d)", p=P),
                                 vtok[:, 0:4, :]).then_inc(S("kv_stored"), 16)
                    sp.dma_start(a["new_v_sample"][0].rearrange("b q h d -> (b q) (h d)"),
                                 vtok[0:TS, 4, :]).then_inc(S("kv_stored"), 16)
                    sp.wait_ge(S("k_rows"), NT)
                    sp.dma_start(a["new_k_prompt"][0, 0].rearrange("(i p) h d -> p i (h d)", p=P),
                                 kout[:, 0:4, :]).then_inc(S("kv_stored"), 16)
                    sp.dma_start(a["new_k_sample"][0].rearrange("b q h d -> (b q) (h d)"),
                                 kout[0:TS, 4, :]).then_inc(S("kv_stored"), 16)
            sp.wait_ge(S("projected"), len(JOBS))
            sp.wait_ge(S("states_zero"), 1)
            st_in = a["state_hgrn"][0].rearrange("b (c e) k v -> e k b c v", e=2)
            st_out = a["new_hgrn_sample"][0].rearrange("b (c e) k v -> e k b c v", e=2)
            for e in range(2):
                for b in range(NB):
                    sp.dma_start(state0[64 * e:64 * e + 64, b, :, 64 * e:64 * e + 64],
                                 st_in[e, :, b]).then_inc(S("states_loaded"), 16)
            sp.wait_ge(S("chunk_states"), 16)
            p_out = a["new_hgrn_prompt"][0, 0].rearrange("(c e) k v -> e k c v", e=2)
            for e in range(2):
                sp.dma_start(p_out[e], state[64 * e:64 * e + 64, 0, :, 64 * e:64 * e + 64]
                             ).then_inc(S("states_stored"), 16)
            sp.wait_ge(S("sample_states"), NB)
            for e in range(2):
                for b in range(NB):
                    sp.dma_start(st_out[e, :, b], state0[64 * e:64 * e + 64, b, :, 64 * e:64 * e + 64]
                                 ).then_inc(S("states_stored"), 16)

            sp.wait_ge(S("yb"), 1)
            sp.wait_ge(S("new_rows"), 4)

            def page_loads(b, g):
                n = b * NGRP + g
                pages = [sp.value_load(a["page_table"][bass.ds(b, 1), NPAGES - 1 - GP * g - j:NPAGES - GP * g - j],
                                       min_val=0, max_val=a["cache_k"].shape[1] - 1) for j in range(GP)]
                for what, ring, slot, free, lag, per in (("cache_k", kring, g % 4, "page_turned", 4, GP),
                                                         ("cache_v", vring, g, "values_summed", NGRP, 1)):
                    if not (isinstance(n, int) and n < lag):
                        sp.wait_ge(S(free), (n - lag + 1) * per)
                    for j, page in enumerate(pages):
                        sp.dma_start(ring[:, slot, j, :],
                                     a[what][0, bass.ds(page, 1)].rearrange("a s h d -> (a s) (h d)")
                                     ).then_inc(S(f"{what}_{slot}"), 16)

            for g in range(NGRP):
                page_loads(0, g)
            with sp.Fori(1, NB) as b:
                for g in range(NGRP):
                    page_loads(b, g)

            sp.wait_ge(S("decoded"), NB)
            for e in range(2):
                sp.dma_start(wab[:, e], w_br[e]).then_inc(S("w_branches"), 16)
            for n, c in enumerate(GATE_CHUNKS):
                if n >= 2:
                    sp.wait_ge(S("branch_products"), 16)
                sp.dma_start(gw[:, n % 2], w_in[:, :, 512 * c:512 * c + 512]).then_inc(S(f"w_gate_{n % 2}"), 16)
            for i in range(NT):
                sp.dma_start(x2[0:ROWS[i], i, :], x_tok[i]).then_inc(S("x_again"), 16)
            def expert_rows(n, u):
                if not (isinstance(n, int) and n < 2):
                    sp.wait_ge(S("rows_turned"), n - 1)
                sp.dma_start(xg[0:BLK, u, :], xg_dram[bass.ds(n * BLK, BLK), :]).then_inc(S(f"rows_{u}"), 16)

            def expert_weights(n, u, e):
                late = not (isinstance(n, int) and n < 2)
                if late:
                    sp.wait_ge(S("gate_up"), n - 1)
                sp.dma_start(wgv[u], a["w_gate_exp"][0, bass.ds(e, 1)].rearrange("a (p k) f -> (a p) k f", k=KD)
                             ).then_inc(S(f"w_gate_exp_{u}"), 16)
                sp.dma_start(wuv[u], a["w_up_exp"][0, bass.ds(e, 1)].rearrange("a (p k) f -> (a p) k f", k=KD)
                             ).then_inc(S(f"w_up_exp_{u}"), 16)
                if not (isinstance(n, int) and n == 0):
                    expert_rows(n, u)
                if late:
                    sp.wait_ge(S("down"), n - 1)
                sp.dma_start(wdv[u], a["w_down_exp"][0, bass.ds(e, 1)].rearrange("a (p j) d -> (a p) j d", j=FJ)
                             ).then_inc(S(f"w_down_exp_{u}"), 16)

            expert_weights(0, 0, 0)
            sp.wait_ge(S("branch_products"), 32)
            sp.dma_start(wo[:, :, :], a["w_out"][0].rearrange("(k p) n -> p k n", p=P)).then_inc(S("w_out"), 16)
            sp.wait_ge(S("h2_scattered"), 32 * NT)
            sp.wait_ge(S("logits"), NT)
            expert_rows(0, 0)
            expert_weights(1, 1, 1)
            with sp.Fori(1, NE // 2) as it:
                for u in range(2):
                    expert_weights(2 * it + u, u, 2 * it + u)
            sp.wait_ge(S("down"), NE)
            novf = sp.value_load(tab[0:1, NOVF:NOVF + 1], min_val=0, max_val=NOVF)
            with sp.Fori(0, NOVF) as i:
                e = sp.value_load(tab[0:1, bass.ds(i, 1)], min_val=0, max_val=NE - 1)
                with sp.If(i < novf):
                    sp.wait_ge(S("extra_down"), i)
                    sp.dma_start(wgv[0], a["w_gate_exp"][0, bass.ds(e, 1)].rearrange("a (p k) f -> (a p) k f", k=KD)
                                 ).then_inc(S("extra_loaded"), 16)
                    sp.dma_start(wuv[0], a["w_up_exp"][0, bass.ds(e, 1)].rearrange("a (p k) f -> (a p) k f", k=KD)
                                 ).then_inc(S("extra_loaded"), 16)
                    sp.dma_start(wdv[0], a["w_down_exp"][0, bass.ds(e, 1)].rearrange("a (p j) d -> (a p) j d", j=FJ)
                                 ).then_inc(S("extra_loaded"), 16)
                    sp.dma_start(xg[0:BLK, 0, :], xg_dram[bass.ds((NE + i) * BLK, BLK), :]).then_inc(S("extra_loaded"), 16)
                with sp.Else():
                    sp.nop()
                sp.nop()
            for i in range(NT):
                sp.wait_ge(S("y_rows"), i + 1)
                dst = a["y_prompt"][0, P * i:P * i + P, :] if i < 4 else a["y_sample"].rearrange("b q d -> (b q) d")
                sp.dma_start(dst, x2[0:ROWS[i], i, :]).then_inc(S("y_stored"), 16)
            sp.wait_ge(S("y_stored"), 16 * NT)
            sp.wait_ge(S("kv_stored"), 64)
            sp.wait_ge(S("states_stored"), 16 * (2 + 2 * NB))

        @block.gpsimd
        def _(pool):
            chain = Chain(pool, S("pool_chain"))

            def select(v, pattern, op, fill, base, cm):
                chain(nc.gpsimd.affine_select(out=v, in_=v, compare_op=op, fill=fill, base=base, pattern=pattern,
                                              channel_multiplier=cm))

            for t, v in ((ident, 0.0), (ones, 1.0), (tri_ge, 1.0), (headones, 1.0), (mask_lt, 1.0), (neg_lt, 0.0),
                         (tri_le, 1.0), (chk_le, 1.0), (chk_gt, 1.0), (sq_le, 1.0), (sq_gt, 1.0), (new_m, 1.0),
                         (new_neg, 0.0), (in_b, 1.0)):
                chain(nc.gpsimd.memset(t[:, :], v))
            chain(nc.gpsimd.memset(flat(ybT), 0.0))
            chain.wait()
            select(ident[:, :], [[-1, P]], ALU.not_equal, 1.0, 0, 1)
            select(tri_ge[:, :], [[-1, P]], ALU.is_ge, 0.0, 0, 1)
            select(mask_lt[:, :], [[1, P]], ALU.is_gt, 0.0, 0, -1)
            select(neg_lt[:, :], [[1, P]], ALU.is_gt, -BIG, 0, -1)
            select(tri_le[:, :], [[1, P]], ALU.is_ge, 0.0, 0, -1)
            select(chk_le[:, :], [[1, P]], ALU.is_ge, 0.0, 0, -1)
            select(chk_gt[:, :], [[-1, P]], ALU.is_gt, 0.0, 0, 1)
            select(sq_le[:, :], [[1, TS]], ALU.is_ge, 0.0, 0, -1)
            select(sq_gt[:, :], [[-1, TS]], ALU.is_gt, 0.0, 0, 1)
            select(each(headones[:, :], 2), [[-64, 2], [0, 64]], ALU.is_ge, 0.0, 0, 1)
            select(in_b[:, :], [[-TQ, NB]], ALU.is_ge, 0.0, 0, 1)
            new4 = [v[:, :].rearrange("p (c b e q) -> p c b e q", c=CT, b=NB, e=2) for v in (new_m, new_neg)]
            for c in range(CT):
                for v, fill in zip(new4, (0.0, -BIG)):
                    select(v[:, c], [[-TQ, NB], [0, 2], [0, TQ]], ALU.is_ge, fill, 0, 1)
            chain.wait()
            select(each(headones[:, :], 2), [[64, 2], [0, 64]], ALU.is_ge, 0.0, 63, -1)
            select(each(chk_le[:, :], 4), [[-CHUNK, 4], [0, CHUNK]], ALU.is_ge, 0.0, 0, 1)
            select(each(chk_gt[:, :], 4), [[CHUNK, 4], [0, CHUNK]], ALU.is_ge, 0.0, CHUNK - 1, -1)
            select(each(sq_le[:, :], NB), [[-TQ, NB], [0, TQ]], ALU.is_ge, 0.0, 0, 1)
            select(each(sq_gt[:, :], NB), [[TQ, NB], [0, TQ]], ALU.is_ge, 0.0, TQ - 1, -1)
            select(in_b[:, :], [[TQ, NB]], ALU.is_ge, 0.0, TQ - 1, -1)
            for c in range(CT):
                for v, fill in zip(new4, (0.0, -BIG)):
                    select(v[:, c], [[TQ, NB], [0, 2], [1, TQ]], ALU.is_gt, fill, 0, -1)
            chain.wait()
            nc.gpsimd.memset(ss[:, :], 0.0).then_inc(S("constants"), 1)
            pool.wait_ge(S("projected"), QKV)
            full = NBLK * BLK // P
            pool.dma_start(xg_dram[0:full * P, :].rearrange("(n p) d -> p n d", p=P),
                           flat(ybT)[:, 0:D].unsqueeze(1).to_broadcast([P, full, D])).then_inc(S("rows_zeroed"), 16)
            pool.dma_start(xg_dram[full * P:NBLK * BLK, :], flat(ybT)[0:NBLK * BLK - full * P, 0:D]
                           ).then_inc(S("rows_zeroed"), 16)
            extra = yg_dram[NE * BLK:NBLK * BLK, :].rearrange("(n p) d -> p n d", p=BLK)
            pool.dma_start(extra, flat(ybT)[0:BLK, 0:D].unsqueeze(1).to_broadcast([BLK, NOVF, D])
                           ).then_inc(S("rows_zeroed"), 16)
            pool.wait_ge(S("projected"), len(JOBS))
            nc.gpsimd.memset(arena[:, 0:8192], 0.0).then_inc(S("states_zero"), 1)
            pool.wait_ge(S("x2"), 1)
            chain(nc.gpsimd.iota(gcol_i, pattern=[[1, NG], [0, EG]], base=0, channel_multiplier=0))
            chain(nc.gpsimd.iota(ecol_i, pattern=[[1, NE]], base=0, channel_multiplier=0))
            chain.wait()
            nc.gpsimd.tensor_copy(gcol, gcol_i).then_inc(S("counters"), 1)
            nc.gpsimd.tensor_copy(ecol, ecol_i).then_inc(S("counters"), 1)
            pool.wait_ge(S("rows_zeroed"), 48)
            pool.wait_ge(S("slots"), 1)
            for i in range(NT):
                for k in range(2):
                    pool.indirect_dma_start(
                        out=xg_dram, out_offset=bass.IndirectOffsetOnAxis(
                            ap=slot_i[0:ROWS[i], 2 * i + k:2 * i + k + 1].bitcast(U32), axis=0),
                        in_=h2[0:ROWS[i], i, :], in_offset=None).then_inc(S("h2_scattered"), 16)
            pool.wait_ge(S("extra_table"), 1)
            novf = pool.value_load(tab[0:1, NOVF:NOVF + 1], min_val=0, max_val=NOVF)
            pool.wait_ge(S("out_stored_0"), 16 * NE // 2)
            pool.wait_ge(S("out_stored_1"), 16 * NE // 2)
            pool.wait_ge(S("extra_stored"), novf * 16)
            pool.sem_inc(S("pool_passed"), 1)
            for i in range(NT):
                if i >= 2:
                    pool.wait_ge(S("y_rows"), i - 1)
                for k in range(2):
                    pool.indirect_dma_start(
                        out=yg[0:ROWS[i], 2 * (i % 2) + k, :], out_offset=None, in_=yg_dram,
                        in_offset=bass.IndirectOffsetOnAxis(
                            ap=slot_i[0:ROWS[i], 2 * i + k:2 * i + k + 1].bitcast(U32), axis=0)
                    ).then_inc(S(f"y_gathered_{i % 2}"), 16)

        @block.tensor
        def _(pe):
            mm = nc.tensor.matmul
            turn = nc.tensor.transpose

            pe.wait_ge(S("constants"), 1)
            for i, r in enumerate(ROWS):
                pe.wait_ge(S("x_normed"), i + 1)
                for kk in range(2):
                    n = 2 * i + kk
                    if n >= 4:
                        pe.wait_ge(S("hT"), n - 3)
                    for c in range(4):
                        cols = xt[0:r, i, :].rearrange("p (m k) -> p k m", k=KD)[:, 4 * kk + c, :]
                        last = turn(ps[:, 4 + n % 4, P * c:P * c + r], cols, ident[0:r, 0:r])
                    last.then_inc(S("x_turned"), 1)
            pe.wait_ge(S("hT"), 2 * NT)

            def project(n):
                c, j = JOBS[n]
                bank = 4 + 2 * (n % 2)
                if j == 0:
                    pe.wait_ge(S(f"w_in_{c % 3}"), 16 * (c // 3 + 1))
                if n >= 2:
                    pe.wait_ge(S("projection_out"), n - 1)
                for k in range(KD):
                    if CHUNKS[c][0] == "cols":
                        for hf in range(2):
                            last = mm(ps[:, bank + hf, 0:TH], wring[:, c % 3, k, P * j:P * j + P],
                                      hT[:, k, TH * hf:TH * hf + TH], start=k == 0, stop=k == KD - 1)
                    else:
                        last = mm(ps[0:ROWS[j], bank, :], hT[:, k, P * j:P * j + ROWS[j]], wring[:, c % 3, k, :],
                                  start=k == 0, stop=k == KD - 1)
                last.then_inc(S("projected"), 1)

            def head_sums(m):
                pe.wait_ge(S("squares"), m + 1)
                for c in range(CT):
                    if m or c >= 2:
                        pe.wait_ge(S("mean_squares"), 4 * m + max(c - 1, 0))
                    for hf in range(2):
                        last = mm(ps[:, 2 * (c % 2) + hf, 0:TH], headones[:, :], sq[:, c, TH * hf:TH * hf + TH],
                                  start=True, stop=True)
                    last.then_inc(S("head_sums"), 1)

            for n in range(4):
                project(n)
            for n in range(4, 8):
                project(n)
            head_sums(0)
            for n in range(8, QKV):
                project(n)
            head_sums(1)
            pe.wait_ge(S("heads_normed"), 2)
            for i, r in enumerate(ROWS):
                if i >= 4:
                    pe.wait_ge(S("k_rows"), i - 3)
                for c in range(CT):
                    last = turn(ps[0:r, i % 4, P * c:P * c + P], kT[:, c, P * i:P * i + r], ident[:, :])
                last.then_inc(S("k_turned_rows"), 1)

            def attn_scores(h):
                if h:
                    pe.wait_ge(S("attn_args"), h)
                else:
                    pe.wait_ge(S("k_rows"), NT)
                r0 = 64 * (h % 2)
                for s in range(4):
                    o = SB_OFF[s]
                    last = mm(ps[:, o // 512, o % 512:o % 512 + SB_LEN[s]], kT[r0:r0 + 64, h // 2, P * s:P * s + P],
                              qT[r0:r0 + 64, h // 2, P * s:SEQ], start=True, stop=True)
                last.then_inc(S("attn_scores"), 1)

            def attn_remain(h):
                pe.wait_ge(S("attn_losses"), h + 1)
                for s in (0, 1, 3, 2):
                    o = SB_OFF[s]
                    bank, c0 = o // 512, o % 512
                    last = mm(ps[:, bank, c0:c0 + SB_LEN[s]], tri_ge[:, :], a_L[:, o:o + SB_LEN[s]],
                              start=True, stop=s == 3)
                    for j in range(s + 1, 4):
                        skip = P * (j - s)
                        last = mm(ps[:, bank, c0 + skip:c0 + SB_LEN[s]], ones[:, :],
                                  a_L[:, SB_OFF[j]:SB_OFF[j] + SB_LEN[j]], start=False, stop=j == 3)
                last.then_inc(S("attn_remains"), 1)

            def attn_values(h):
                pe.wait_ge(S("attn_weights"), h + 1)
                r0 = 64 * (h % 2)
                if h % 2 == 0 and h:
                    pe.wait_ge(S("attn_out"), h // 2)
                for s in range(4):
                    last = mm(ps[r0:r0 + 64, 3, P * s:SEQ], vtok[:, s, DH * h:DH * h + DH],
                              a_A[:, h % 2, SB_OFF[s]:SB_OFF[s] + SB_LEN[s]], start=s == 0, stop=s == 3)
                last.then_inc(S("attn_values"), 1)

            n = QKV
            for h in range(H):
                attn_scores(h)
                if n < len(JOBS):
                    project(n)
                    n += 1
                if h == 0 or h == 4:
                    project(n)
                    n += 1
                attn_remain(h)
                if n < len(JOBS):
                    project(n)
                    n += 1
                attn_values(h)
            assert n == len(JOBS)

            for i in range(5):
                r, prompt = ROWS[i], i < 4
                le, gt = (chk_le, chk_gt) if prompt else (sq_le, sq_gt)
                pe.wait_ge(S("log_f"), i + 1)
                if i:
                    pe.wait_ge(S("chunk_states"), 4 * i)
                    pe.wait_ge(S("o_read"), i)
                    pe.wait_ge(S("decayed"), 3 * i)
                else:
                    pe.wait_ge(S("attn_args"), H)
                for c in range(CT):
                    mm(ps[:, 0, r * c:r * c + r], ftok[0:r, i, P * c:P * c + P], le[0:r, 0:r], start=True, stop=True)
                mm(ps[0:r, 1, :], gt[0:r, 0:r], ftok[0:r, i, :], start=True, stop=True)
                for c in range(CT):
                    last = turn(ps[:, 2, r * c:r * c + r], ktok[0:r, P * c:P * c + P], ident[0:r, 0:r])
                last.then_inc(S("decay_sums"), 1)
                pe.wait_ge(S("decayed"), 3 * i + 3)
                if i:
                    pe.wait_ge(S("hg_masked"), 2 * i)
                else:
                    pe.wait_ge(S("attn_out"), CT)
                    pe.wait_ge(S("projection_out"), len(JOBS))
                for e in range(2):
                    for c in range(CT):
                        last = mm(ps[0:r, 3 + e, r * c:r * c + r], kd[64 * e:64 * e + 64, c, 0:r],
                                  qd[64 * e:64 * e + 64, c, 0:r], start=True, stop=True)
                last.then_inc(S("hg_scores"), 1)
                if prompt:
                    for k in range(4):
                        for c in range(CT):
                            last = mm(ps[:, KV_BANK[k], P * c:P * c + P], kdec[CHUNK * k:CHUNK * k + CHUNK, P * c:P * c + P],
                                      itok[CHUNK * k:CHUNK * k + CHUNK, i, P * c:P * c + P], start=True, stop=True)
                        last.then_inc(S("chunk_kv"), 1)
                pe.wait_ge(S("hg_masked"), 2 * i + 2)
                for c in range(CT):
                    for e in range(2):
                        mm(ps[64 * e:64 * e + 64, 1, r * c:r * c + r], itok[0:r, i, P * c + 64 * e:P * c + 64 * e + 64],
                           scm[0:r, 4 * e + c, 0:r], start=c == 0, stop=False, skip_group_check=True)
                if prompt:
                    for k in range(4):
                        if i or k:
                            pe.wait_ge(S("chunk_states"), 4 * i + k)
                        else:
                            pe.wait_ge(S("states_zero"), 1)
                        for c in range(CT):
                            last = mm(ps[:, 1, P * c + CHUNK * k:P * c + CHUNK * k + CHUNK], state[:, (4 * i + k) % 8, c, :],
                                      qd[:, c, CHUNK * k:CHUNK * k + CHUNK], start=False, stop=True, skip_group_check=True)
                    last.then_inc(S("hg_out"), 1)
                else:
                    pe.wait_ge(S("states_loaded"), 32 * NB)
                    for b in range(NB):
                        for c in range(CT):
                            last = mm(ps[:, 1, TS * c + TQ * b:TS * c + TQ * b + TQ], state0[:, b, c, :],
                                      qd[:, c, TQ * b:TQ * b + TQ], start=False, stop=True, skip_group_check=True)
                    last.then_inc(S("hg_out"), 1)
                    pe.wait_ge(S("ib"), 1)
                    for b in range(NB):
                        if b >= 4:
                            pe.wait_ge(S("sample_states"), b - 3)
                        for c in range(CT):
                            last = mm(ps[:, KV_BANK[b % 4], P * c:P * c + P], kdec[0:r, P * c:P * c + P],
                                      ib[0:r, b, P * c:P * c + P], start=True, stop=True)
                        last.then_inc(S("sample_kv"), 1)
            pe.wait_ge(S("sample_states"), NB)
            head_sums(2)

            pe.wait_ge(S("q_blocks"), 1)
            for c in range(CT):
                last = mm(ps[0:TS, 4, 64 * c:64 * c + 64], kT[:, c, SEQ:T], qblk[:, :, 8 * c:8 * c + 8],
                          start=True, stop=True)
            last.then_inc(S("new_products"), 1)
            pe.wait_ge(S("new_rows"), 2)
            mm(ps[0:TS, 5, 0:256], tri_ge[0:TS, 0:TS], n_L[0:TS, :], start=True, stop=True).then_inc(S("new_products"), 1)
            pe.wait_ge(S("new_act"), 4)
            for c in range(CT):
                last = mm(ps[:, 6, 64 * c:64 * c + 64], vtok[0:TS, 4, P * c:P * c + P],
                          n_e[0:TS, 64 * c:64 * c + 64], start=True, stop=True)
            last.then_inc(S("new_products"), 1)

            def turn_keys(b, g):
                n = b * NGRP + g
                pe.wait_ge(S(f"cache_k_{g % 4}"), (b * 2 + g // 4 + 1) * 16 * GP)
                for j in range(GP):
                    if g or not isinstance(b, int):
                        pe.wait_ge(S("kT_act" if j < 2 else "kT_dve"), 2 * n - 1 + j % 2)
                    for c in range(CT):
                        last = turn(ps[:, j, P * c:P * c + P], kring[:, g % 4, j, P * c:P * c + P], ident[:, :])
                    last.then_inc(S("page_turned"), 1)

            def page_scores(b, g):
                n = b * NGRP + g
                pe.wait_ge(S("kT_act"), 2 * n + 2)
                pe.wait_ge(S("kT_dve"), 2 * n + 2)
                if not isinstance(n, int) or n >= 2:
                    pe.wait_ge(S("page_args"), n - 1)
                for j in range(GP):
                    for c in range(CT):
                        last = mm(ps[:, 4 + g % 2, 32 * j + 8 * c:32 * j + 8 * c + 8], d_kt[:, g % 2, j, P * c:P * c + P],
                                  qblk[:, bass.ds(b, 1), 8 * c:8 * c + 8], start=True, stop=True)
                last.then_inc(S("page_scores"), 1)

            def page_remains(b, g):
                n = b * NGRP + g
                pe.wait_ge(S("page_sums"), n + 1)
                mm(ps[:, 4 + g % 2, 128:256], tri_ge[:, :], d_L[:, g % 2, :], start=True, stop=False)
                mm(ps[:, 4 + g % 2, 128:256], ones[:, :], d_R[:, g % 4, :], start=False, stop=True
                   ).then_inc(S("page_remains"), 1)

            def page_values(b, g):
                n = b * NGRP + g
                pe.wait_ge(S(f"cache_v_{g}"), (b + 1) * 16 * GP)
                pe.wait_ge(S("page_weights"), n + 1)
                if g == 0 and isinstance(b, int) and b == 0:
                    pe.wait_ge(S("new_rows"), 4)
                elif g == 0:
                    pe.wait_ge(S("decoded"), b)
                for j in range(GP):
                    for c in range(CT):
                        last = mm(ps[:, 6, 8 * c:8 * c + 8], vring[:, g, j, P * c:P * c + P],
                                  d_A[:, g % 4, 32 * j + 8 * c:32 * j + 8 * c + 8],
                                  start=g == 0 and j == 0 and c == 0, stop=g == NGRP - 1 and j == GP - 1,
                                  skip_group_check=True)
                last.then_inc(S("values_summed"), 1)

            def before(b, g, lag):
                return (b, g - lag) if g >= lag else (b - 1, g - lag + NGRP)

            def decode_steps(b):
                for g in range(NGRP):
                    turn_keys(b, g)
                    for lag, part in ((1, page_scores), (2, page_remains), (3, page_values)):
                        if g >= lag or not isinstance(b, int):
                            part(*before(b, g, lag))

            pe.wait_ge(S("mean_squares"), 3 * CT)
            decode_steps(0)
            with pe.Fori(1, NB) as b:
                decode_steps(b)
            page_scores(NB - 1, NGRP - 1)
            page_remains(NB - 1, NGRP - 2)
            page_values(NB - 1, NGRP - 3)
            page_remains(NB - 1, NGRP - 1)
            page_values(NB - 1, NGRP - 2)
            page_values(NB - 1, NGRP - 1)

            pe.wait_ge(S("w_branches"), 32)
            pe.wait_ge(S("decoded"), NB)
            for m in range(KD):
                for e in range(4):
                    n = 4 * m + e
                    bank = 2 * (n % 4)
                    if m:
                        pe.wait_ge(S("gates_read" if e < 2 else "branches_read"), 2 * m - 1 + e % 2)
                    if e < 2 and m % 4 == 0:
                        pe.wait_ge(S(f"w_gate_{e}"), 16 * (m // 4 + 1))
                    for k in range(KD if e < 2 else CT):
                        for hf in range(2):
                            cols = slice(TH * hf, TH * hf + TH)
                            if e < 2:
                                last = mm(ps[:, bank + hf, 0:TH], gw[:, e, k, P * (m % 4):P * (m % 4) + P], hT[:, k, cols],
                                          start=k == 0, stop=k == KD - 1)
                            else:
                                last = mm(ps[:, bank + hf, 0:TH], wab[:, e - 2, k, P * m:P * m + P],
                                          (osbT, ybT)[e - 2][:, k, cols], start=k == 0, stop=k == CT - 1)
                    last.then_inc(S("branch_products"), 1)
            pe.wait_ge(S("merged"), KD)
            pe.wait_ge(S("w_out"), 16)
            for i, r in enumerate(ROWS):
                if i >= 2:
                    pe.wait_ge(S("x2"), i - 1)
                for k in range(KD):
                    for hf in range(2):
                        last = mm(ps[0:r, 2 * (i % 2) + hf, :], mrg[:, k, P * i:P * i + r], wo[:, k, 512 * hf:512 * hf + 512],
                                  start=k == 0, stop=k == KD - 1)
                last.then_inc(S("mixed"), 1)
            pe.wait_ge(S("w_router"), 32)
            for i, r in enumerate(ROWS):
                pe.wait_ge(S("h2"), i + 1)
                if i:
                    pe.wait_ge(S("h2_cols"), i)
                for k in range(KD):
                    cols = h2[0:r, i, :].rearrange("p (m k) -> p k m", k=KD)[:, k, :]
                    last = turn(ps[:, 4 + k // 4, P * (k % 4):P * (k % 4) + r], cols, ident[0:r, 0:r])
                last.then_inc(S("h2_turned"), 1)
                pe.wait_ge(S("h2_cols"), i + 1)
                if i:
                    pe.wait_ge(S("logits_read"), i)
                for k in range(KD):
                    last = mm(ps[0:r, 6, 0:NG + NE], h2T[:, i % 2, k, 0:r], wr[:, k, :], start=k == 0, stop=k == KD - 1)
                last.then_inc(S("logits"), 1)
            pe.wait_ge(S("chosen"), NT)
            for i, r in enumerate(ROWS):
                for j in range(i + 1):
                    lhs = mask_lt[0:r, 0:r] if j == i else ones[0:ROWS[j], 0:r]
                    mm(ps[0:r, 7, NE * i:NE * i + NE], lhs, r_O[0:ROWS[j], NE * j:NE * j + NE], start=j == 0, stop=j == i)
            for j, r in enumerate(ROWS):
                last = mm(ps[0:NE, 6, 0:P], r_O[0:r, NE * j:NE * j + NE], ones[0:r, :], start=j == 0, stop=j == NT - 1)
            last.then_inc(S("list_sums"), 1)
            pe.wait_ge(S("extra_blocks"), 1)
            mm(ps[:, 5, 0:NE], r_ov[0:NE, :], mask_lt[0:NE, 0:NE], start=True, stop=True)
            mm(ps[0:NE, 5, NE:NE + 1], tri_le[0:NE, 0:NE], r_ov[0:NE, 0:1], start=True, stop=True)
            mm(ps[:, 5, NE + 1:NE + 2], ones[0:NE, :], r_ov[0:NE, 0:1], start=True, stop=True
               ).then_inc(S("list_sums"), 1)
            pe.wait_ge(S("extra_after"), 1)
            mm(ps[:, 4, 0:NOVF], ones[0:NE, :], r_ind[0:NE, :], start=True, stop=True).then_inc(S("list_sums"), 1)

            def rows_to_cols(n, u):
                pe.wait_ge(S(f"rows_{u}"), rows_count(n, u))
                if not (isinstance(n, int) and n < 1):
                    pe.wait_ge(S("xg_cols"), n)
                pe.sem_inc(S("pe_passed"), 1)
                for k in range(KD):
                    cols = xg[0:BLK, u, :].rearrange("p (m k) -> p k m", k=KD)[:, k, :]
                    last = turn(ps[:, 0, BLK * k:BLK * k + BLK], cols, ident[0:BLK, 0:BLK])
                last.then_inc(S("rows_turned"), 1)

            def rows_count(n, u):
                return 16 * (n // 2 + 1) if isinstance(n, int) else 16 + (n - u) * 8

            def gate_up(n, u):
                pe.wait_ge(S("xg_cols"), n + 1)
                if not (isinstance(n, int) and n < 2):
                    pe.wait_ge(S("hidden"), n - 1)
                for e, wv in enumerate((wgv[u], wuv[u])):
                    pe.wait_ge(S(f"{('w_gate_exp', 'w_up_exp')[e]}_{u}"), rows_count(n, u))
                    cols = wv.rearrange("p k (m j) -> p k j m", j=FJ)
                    for j in range(FJ):
                        for k in range(KD):
                            last = mm(ps[:, 1 + 2 * u + e, BLK * j:BLK * j + BLK], cols[:, k, j, :], xgT[:, u, k, :],
                                      start=k == 0, stop=k == KD - 1)
                last.then_inc(S("gate_up"), 1)

            def down(n, u):
                pe.wait_ge(S("hidden"), n + 1)
                pe.wait_ge(S(f"w_down_exp_{u}"), rows_count(n, u))
                if not (isinstance(n, int) and n < 1):
                    pe.wait_ge(S("y_act"), n)
                    pe.wait_ge(S("y_dve"), n)
                for hf in range(2):
                    for j in range(FJ):
                        last = mm(ps[0:BLK, 5 + hf, :], m_h[:, u, j, :], wdv[u][:, j, 512 * hf:512 * hf + 512],
                                  start=j == 0, stop=j == FJ - 1)
                last.then_inc(S("down"), 1)

            rows_to_cols(0, 0)
            gate_up(0, 0)
            rows_to_cols(1, 1)
            gate_up(1, 1)
            down(0, 0)
            with pe.Fori(1, NE // 2) as it:
                for u in range(2):
                    rows_to_cols(2 * it + u, u)
                    gate_up(2 * it + u, u)
                    down(2 * it + u - 1, 1 - u)
            down(NE - 1, 1)
            novf = pe.value_load(tab[0:1, NOVF:NOVF + 1], min_val=0, max_val=NOVF)
            with pe.Fori(0, NOVF) as i:
                with pe.If(i < novf):
                    pe.wait_ge(S("extra_loaded"), (i + 1) * 64)
                    pe.sem_inc(S("pe_passed"), 1)
                    for k in range(KD):
                        cols = xg[0:BLK, 0, :].rearrange("p (m k) -> p k m", k=KD)[:, k, :]
                        last = turn(ps[:, 0, BLK * k:BLK * k + BLK], cols, ident[0:BLK, 0:BLK])
                    last.then_inc(S("extra_turned"), 1)
                    pe.wait_ge(S("extra_cols"), i + 1)
                    for e, wv in enumerate((wgv[0], wuv[0])):
                        cols = wv.rearrange("p k (m j) -> p k j m", j=FJ)
                        for j in range(FJ):
                            for k in range(KD):
                                last = mm(ps[:, 1 + e, BLK * j:BLK * j + BLK], cols[:, k, j, :], xgT[:, 0, k, :],
                                          start=k == 0, stop=k == KD - 1)
                    last.then_inc(S("extra_gate_up"), 1)
                    pe.wait_ge(S("extra_hidden"), i + 1)
                    for hf in range(2):
                        for j in range(FJ):
                            last = mm(ps[0:BLK, 5 + hf, :], m_h[:, 0, j, :], wdv[0][:, j, 512 * hf:512 * hf + 512],
                                      start=j == 0, stop=j == FJ - 1)
                    last.then_inc(S("extra_down"), 1)
                with pe.Else():
                    pe.nop()
                pe.nop()

        @block.scalar
        def _(act):
            fn = nc.scalar.activation

            def load(dst, src, signal):
                act.dma_start(dst, src).then_inc(S(signal), 16)

            load(w1c[:, :], a["norm1_w"][0].rearrange("(p k) -> p k", k=KD), "small_loaded")
            for j, name in enumerate(("q_norm_w", "k_norm_w", "hg_norm_w")):
                for e in range(2):
                    load(qkg[64 * e:64 * e + 64, j:j + 1], a[name][0].rearrange("(p o) -> p o", o=1), "small_loaded")
            load(bias8[:, :], a["sb_bias"].to_broadcast([P, H]), "small_loaded")

            act.wait_ge(S("constants"), 1)
            act.wait_ge(S("x_loaded"), 16 * NT)
            for i, r in enumerate(ROWS):
                if i:
                    act.wait_ge(S("row_squares"), i)
                fn(kout_flat[0:r, 0:D], xt[0:r, i, :], ACT.Square, accum_out=ss[0:r, i:i + 1]).then_inc(S("row_squares"), 1)
            act.wait_ge(S("row_inverses"), 1)
            fn(rstd[:, 0:NT], rstd[:, 0:NT], ACT.Sqrt).then_inc(S("row_scales"), 1)

            def projection_out(n):
                c, j = JOBS[n]
                kind, dst = CHUNKS[c]
                bank = 4 + 2 * (n % 2)
                act.wait_ge(S("projected"), n + 1)
                if kind == "cols":
                    fn(each(dst[:, j, :], 2), ps[:, bank:bank + 2, 0:TH], ACT.Copy).then_inc(S("projection_out"), 1)
                else:
                    r = ROWS[j]
                    fn(dst[0:r, j, :], ps[0:r, bank, :], ACT.Copy).then_inc(S("projection_out"), 1)

            def head_roots(m):
                act.wait_ge(S("head_inverses"), m + 1)
                fn(flat(rs), flat(rs), ACT.Sqrt).then_inc(S("head_scales"), 1)

            for n in range(8):
                projection_out(n)
            head_roots(0)
            for n in range(8, QKV):
                projection_out(n)
            head_roots(1)

            n = QKV
            for h in range(H):
                act.wait_ge(S("attn_scores"), h + 1)
                if h:
                    act.wait_ge(S("attn_losses"), h)
                    act.wait_ge(S("attn_weights"), h)
                fn(a_z, ps_attn, ACT.Identity, scale=SCALE, bias=bias8[:, h:h + 1]).then_inc(S("attn_z"), 1)
                act.wait_ge(S("attn_z"), h + 1)
                fn(a_e, a_z, ACT.Abs).then_inc(S("attn_softplus"), 1)
                act.wait_ge(S("attn_softplus"), 3 * h + 1)
                fn(a_e, a_e, ACT.Exp, scale=-1.0).then_inc(S("attn_softplus"), 1)
                act.wait_ge(S("attn_softplus"), 3 * h + 2)
                fn(a_ln, a_e, ACT.Ln, bias=1.0).then_inc(S("attn_softplus"), 1)
                for _ in range(2 if h in (0, 4) else 1):
                    if n < len(JOBS):
                        projection_out(n)
                        n += 1
                act.wait_ge(S("attn_args"), h + 1)
                if h < 2:
                    act.wait_ge(S("kv_stored"), 64)
                else:
                    act.wait_ge(S("attn_values"), h - 1)
                fn(a_A[:, h % 2, :], a_z, ACT.Exp).then_inc(S("attn_weights"), 1)
                if n < len(JOBS):
                    projection_out(n)
                    n += 1

            act.wait_ge(S("attn_values"), H)
            load(lbr[:, :, :], a["lb_logits"].rearrange("(o r) c -> o r c", o=1).to_broadcast([P, 2, W]), "lb_loaded")
            act.wait_ge(S("lb_shifted"), 1)
            fn(lbr[:, :, :], lbr[:, :, :], ACT.Exp).then_inc(S("lb_exp"), 1)
            act.wait_ge(S("projection_out"), len(JOBS))
            for i, r in enumerate(ROWS):
                fn(ftok[0:r, i, :], ftok[0:r, i, :], ACT.Exp, scale=-1.0).then_inc(S("f_exp"), 1)
            for i, r in enumerate(ROWS):
                act.wait_ge(S("f"), i + 1)
                fn(ftok[0:r, i, :], ftok[0:r, i, :], ACT.Ln).then_inc(S("log_f"), 1)
                act.wait_ge(S("decay_sums"), i + 1)
                fn(g_e[:, 0:CT * r], ps[:, 0, 0:CT * r], ACT.Exp).then_inc(S("decays"), 1)
                fn(g_en[:, 0:CT * r], ps[:, 0, 0:CT * r], ACT.Exp, scale=-1.0).then_inc(S("decays"), 1)
                fn(g_e2[0:r, :], ps[0:r, 1, :], ACT.Exp).then_inc(S("decays"), 1)
            act.wait_ge(S("decayed"), 3 * NT)
            fn(flat(hqT), flat(gT), ACT.Sigmoid).then_inc(S("g_sigmoid"), 1)
            head_roots(2)

            act.wait_ge(S("new_rows"), 1)
            fn(n_e[0:TS, :], n_z[0:TS, :], ACT.Abs).then_inc(S("new_act"), 1)
            act.wait_ge(S("new_act"), 1)
            fn(n_e[0:TS, :], n_e[0:TS, :], ACT.Exp, scale=-1.0).then_inc(S("new_act"), 1)
            act.wait_ge(S("new_act"), 2)
            fn(n_s[0:TS, :], n_e[0:TS, :], ACT.Ln, bias=1.0).then_inc(S("new_act"), 1)
            act.wait_ge(S("new_rows"), 3)
            fn(n_e[0:TS, :], n_z[0:TS, :], ACT.Exp).then_inc(S("new_act"), 1)

            def turned_out(b, g):
                n = b * NGRP + g
                for j in range(2):
                    act.wait_ge(S("page_turned"), 4 * n + j + 1)
                    if not isinstance(n, int) or n >= 2:
                        act.wait_ge(S("page_scores"), n - 1)
                    fn(d_kt[:, g % 2, j, :], ps[:, j, :], ACT.Copy).then_inc(S("kT_act"), 1)

            def softplus_parts(b, g):
                n = b * NGRP + g
                act.wait_ge(S("page_z"), n + 1)
                fn(d_e[:, g % 2, :], d_z[:, g % 2, :], ACT.Abs).then_inc(S("page_softplus"), 1)
                act.wait_ge(S("page_softplus"), 3 * n + 1)
                fn(d_e[:, g % 2, :], d_e[:, g % 2, :], ACT.Exp, scale=-1.0).then_inc(S("page_softplus"), 1)
                act.wait_ge(S("page_softplus"), 3 * n + 2)
                fn(d_ln[:, g % 2, :], d_e[:, g % 2, :], ACT.Ln, bias=1.0).then_inc(S("page_softplus"), 1)

            def page_weights(b, g):
                n = b * NGRP + g
                act.wait_ge(S("page_args"), n + 1)
                if not isinstance(n, int) or n >= 4:
                    act.wait_ge(S("values_summed"), n - 3)
                fn(d_A[:, g % 4, :], d_z[:, g % 2, :], ACT.Exp).then_inc(S("page_weights"), 1)

            def before(b, g, lag):
                return (b, g - lag) if g >= lag else (b - 1, g - lag + NGRP)

            def decode_steps(b):
                for g in range(NGRP):
                    turned_out(b, g)
                    for lag, part in ((1, softplus_parts), (2, page_weights)):
                        if g >= lag or not isinstance(b, int):
                            part(*before(b, g, lag))

            decode_steps(0)
            with act.Fori(1, NB) as b:
                decode_steps(b)
            softplus_parts(NB - 1, NGRP - 1)
            page_weights(NB - 1, NGRP - 2)
            page_weights(NB - 1, NGRP - 1)

            for m in range(KD):
                for e, dst in enumerate((m_sa, m_sb)):
                    act.wait_ge(S("branch_products"), 4 * m + e + 1)
                    if m >= 2:
                        act.wait_ge(S("merged"), m - 1)
                    elif m == 0:
                        act.wait_ge(S("decoded"), NB)
                    fn(each(dst[:, m % 2, :], 2), ps[:, 2 * e:2 * e + 2, 0:TH], ACT.Sigmoid).then_inc(S("gates_read"), 1)
            act.wait_ge(S("branch_products"), 4 * KD)
            load(w2r[:, :], a["norm2_w"].to_broadcast([P, D]), "w2_loaded")
            act.wait_ge(S("merged"), KD)
            load(wr[:, :, 0:NG], a["w_group_router"][0].rearrange("(p k) n -> p k n", k=KD), "w_router")
            load(wr[:, :, NG:NG + NE], a["w_expert_router"][0].rearrange("(p k) n -> p k n", k=KD), "w_router")
            act.wait_ge(S("route_zero"), 1)
            load(r_b36[:, 0:NG], a["b_group_router"].to_broadcast([P, NG]), "b_router")
            load(r_b36[:, NG:NG + NE], a["b_expert_router"].to_broadcast([P, NE]), "b_router")
            for i, r in enumerate(ROWS):
                act.wait_ge(S("x2"), i + 1)
                if i:
                    act.wait_ge(S("row_squares"), NT + i)
                fn(sqj[0:r, :], x2[0:r, i, :], ACT.Square, accum_out=ss2[0:r, i:i + 1]).then_inc(S("row_squares"), 1)
                act.wait_ge(S("row_inverses"), 2 + i)
                fn(rstd2[0:r, i:i + 1], rstd2[0:r, i:i + 1], ACT.Sqrt).then_inc(S("row_scales"), 1)
            for i, r in enumerate(ROWS):
                act.wait_ge(S("group_max"), i + 1)
                fn(r_ge[0:r, :], r_gl[0:r, 0:NG], ACT.Exp, bias=r_ng[0:r, :], accum_out=r_gs[0:r, :]
                   ).then_inc(S("group_sum"), 1)
                act.wait_ge(S("expert_gap"), i + 1)
                fn(r_e2[0:r, :], r_gap[0:r, :], ACT.Exp).then_inc(S("expert_ratio"), 1)

            def slot_count(n, u):
                return 16 * (n // 2 + 1) if isinstance(n, int) else 16 + (n - u) * 8

            def silu(n, u):
                act.wait_ge(S("gate_up"), n + 1)
                if not (isinstance(n, int) and n < 2):
                    act.wait_ge(S("hidden"), n - 1)
                fn(m_s[:, u, :], ps[:, 1 + 2 * u, 0:FJ * BLK], ACT.Silu).then_inc(S("silu"), 1)

            def y_out(n, u):
                act.wait_ge(S("down"), n + 1)
                if not (isinstance(n, int) and n < 2):
                    act.wait_ge(S(f"out_stored_{u}"), slot_count(n, u) - 16)
                fn(m_y[0:BLK, u, 0:512], ps[0:BLK, 5, :], ACT.Copy).then_inc(S("y_act"), 1)
                act.wait_ge(S("y_act"), n + 1)
                act.wait_ge(S("y_dve"), n + 1)
                act.dma_start(yg_dram[bass.ds(n * BLK, BLK), :], m_y[0:BLK, u, :]).then_inc(S(f"out_stored_{u}"), 16)

            silu(0, 0)
            silu(1, 1)
            y_out(0, 0)
            with act.Fori(1, NE // 2) as it:
                for u in range(2):
                    silu(2 * it + u, u)
                    y_out(2 * it + u - 1, 1 - u)
            y_out(NE - 1, 1)
            for u in range(2):
                act.wait_ge(S(f"out_stored_{u}"), 8 * NE)
            novf = act.value_load(tab[0:1, NOVF:NOVF + 1], min_val=0, max_val=NOVF)
            with act.Fori(0, NOVF) as i:
                with act.If(i < novf):
                    act.wait_ge(S("extra_gate_up"), i + 1)
                    fn(m_s[:, 0, :], ps[:, 1, 0:FJ * BLK], ACT.Silu).then_inc(S("extra_silu"), 1)
                    act.wait_ge(S("extra_down"), i + 1)
                    act.wait_ge(S("extra_stored"), i * 16)
                    fn(m_y[0:BLK, 0, 0:512], ps[0:BLK, 5, :], ACT.Copy).then_inc(S("extra_y_act"), 1)
                    act.wait_ge(S("extra_y_act"), i + 1)
                    act.wait_ge(S("extra_y_dve"), i + 1)
                    act.dma_start(yg_dram[bass.ds((NE + i) * BLK, BLK), :], m_y[0:BLK, 0, :]).then_inc(S("extra_stored"), 16)
                with act.Else():
                    act.nop()
                act.nop()

        @block.vector
        def _(dve):
            v = nc.vector
            chain = Chain(dve, S("vector_chain"))
            stt = v.scalar_tensor_tensor

            def over(m, r, n, k):
                return m[0:r, 0:k].unsqueeze(1).to_broadcast([r, n, k])

            dve.wait_ge(S("row_squares"), NT)
            chain(v.tensor_scalar(rstd[:, 0:NT], ss[:, 0:NT], 1.0 / D, EPS, ALU.mult, ALU.add))
            chain.wait()
            v.reciprocal(rstd[:, 0:NT], rstd[:, 0:NT]).then_inc(S("row_inverses"), 1)
            dve.wait_ge(S("row_scales"), 1)
            for i, r in enumerate(ROWS):
                v.tensor_scalar(xt[0:r, i, :], xt[0:r, i, :], rstd[0:r, i:i + 1], None, ALU.mult).then_inc(S("x_normed"), 1)
            dve.wait_ge(S("small_loaded"), 128)
            chain(v.tensor_copy(bias32[:, :].rearrange("p (h q) -> p h q", q=TQ), bias8[:, :].unsqueeze(2).to_broadcast([P, H, TQ])))
            for i, r in enumerate(ROWS):
                for kk in range(2):
                    n = 2 * i + kk
                    dve.wait_ge(S("x_turned"), n + 1)
                    v.tensor_tensor(hT[:, 4 * kk:4 * kk + 4, P * i:P * i + r], each(ps[:, 4 + n % 4, :], 4)[:, :, 0:r],
                                    w1c[:, 4 * kk:4 * kk + 4].unsqueeze(2).to_broadcast([P, 4, r]), ALU.mult
                                    ).then_inc(S("hT"), 1)

            def head_norm(m, xT):
                if m:
                    dve.wait_ge(S("head_sums"), 4 * m)
                v.tensor_tensor(flat(sq), flat(xT), flat(xT), ALU.mult).then_inc(S("squares"), 1)
                for c in range(CT):
                    dve.wait_ge(S("head_sums"), 4 * m + c + 1)
                    v.tensor_scalar(each(rs[:, c, :], 2), ps[:, 2 * (c % 2):2 * (c % 2) + 2, 0:TH], 1.0 / DH, EPS,
                                    ALU.mult, ALU.add).then_inc(S("mean_squares"), 1)
                dve.wait_ge(S("mean_squares"), 4 * m + 4)
                v.reciprocal(flat(rs), flat(rs)).then_inc(S("head_inverses"), 1)
                dve.wait_ge(S("head_scales"), m + 1)
                stt(out=flat(xT), in0=flat(xT), scalar=qkg[:, m:m + 1], in1=flat(rs), op0=ALU.mult, op1=ALU.mult
                    ).then_inc(S("heads_normed"), 1)

            dve.wait_ge(S("projection_out"), 4)
            head_norm(0, qT)
            dve.wait_ge(S("projection_out"), 8)
            dve.wait_ge(S("heads_normed"), 1)
            head_norm(1, kT)
            for i, r in enumerate(ROWS):
                dve.wait_ge(S("k_turned_rows"), i + 1)
                v.tensor_copy(kout[0:r, i, :], ps[0:r, i % 4, :]).then_inc(S("k_rows"), 1)

            def softplus(z, e, ln, t, L):
                chain(v.tensor_scalar(t, e, 1.0, -1.0, ALU.add, ALU.add))
                chain.wait()
                chain(v.tensor_tensor(t, e, t, ALU.subtract))

            def attn_pair_out(p):
                dve.wait_ge(S("attn_values"), 2 * p + 2)
                v.tensor_copy(osbT[:, p, 0:SEQ], ps[:, 3, :]).then_inc(S("attn_out"), 1)

            for h in range(H):
                dve.wait_ge(S("attn_softplus"), 3 * h + 2)
                softplus(a_z, a_e, a_ln, a_t, a_L)
                dve.wait_ge(S("attn_softplus"), 3 * h + 3)
                chain(stt(out=a_L, in0=a_z, scalar=0.0, in1=a_ln, op0=ALU.max, op1=ALU.add))
                chain.wait()
                chain(v.tensor_tensor(a_L, a_L, a_t, ALU.add))
                chain.wait()
                chain(v.tensor_tensor(diag3(a_L_off), diag3(a_L_off), over(mask_lt, P, 3, P), ALU.mult))
                v.tensor_tensor(a_L[:, 896:1024], a_L[:, 896:1024], mask_lt[:, :], ALU.mult).then_inc(S("attn_losses"), 1)
                dve.wait_ge(S("attn_remains"), h + 1)
                chain(v.tensor_tensor(a_z, a_z, ps_attn, ALU.subtract))
                chain.wait()
                chain(v.tensor_tensor(diag3(a_z_off), diag3(a_z_off), over(neg_lt, P, 3, P), ALU.add))
                v.tensor_tensor(a_z[:, 896:1024], a_z[:, 896:1024], neg_lt[:, :], ALU.add).then_inc(S("attn_args"), 1)
                if h % 2 == 0 and h:
                    attn_pair_out(h // 2 - 1)
            attn_pair_out(CT - 1)

            dve.wait_ge(S("lb_loaded"), 16)
            chain(v.tensor_tensor(oml, lbr[:, 0, :], lbr[:, 1, :], ALU.max))
            chain.wait()
            chain(v.tensor_tensor(lbr[:, 0, :], lbr[:, 0, :], oml, ALU.subtract))
            v.tensor_tensor(lbr[:, 1, :], lbr[:, 1, :], oml, ALU.subtract).then_inc(S("lb_shifted"), 1)
            dve.wait_ge(S("lb_exp"), 1)
            chain(v.tensor_tensor(oml, lbr[:, 0, :], lbr[:, 1, :], ALU.add))
            chain.wait()
            chain(v.reciprocal(oml, oml))
            chain.wait()
            chain(v.tensor_tensor(lb, lbr[:, 0, :], oml, ALU.mult))
            chain.wait()
            chain(v.tensor_scalar(oml, lb, -1.0, 1.0, ALU.mult, ALU.add))
            dve.wait_ge(S("states_zero"), 1)
            for b in range(NB):
                last = v.tensor_scalar(ib[0:TS, b, :], itok[0:TS, 4, :], in_b[:, b:b + 1], None, ALU.mult)
            last.then_inc(S("ib"), 1)

            def forget(i):
                r = ROWS[i]
                f = ftok[0:r, i, :]
                dve.wait_ge(S("f_exp"), i + 1)
                chain.wait()
                chain(v.tensor_scalar(f, f, 1.0, None, ALU.add))
                chain.wait()
                chain(v.reciprocal(f, f))
                chain.wait()
                chain(v.tensor_tensor(f, f, oml[0:r, :], ALU.mult))
                chain.wait()
                chain(v.tensor_tensor(f, f, lb[0:r, :], ALU.add))
                chain.wait()
                if i:
                    dve.wait_ge(S("decay_sums"), i)
                    dve.wait_ge(S("decayed"), 3 * i)
                v.tensor_scalar(ktok[0:r, :], f, -1.0, 1.0, ALU.mult, ALU.add).then_inc(S("f"), 1)

            def state_update(dst, src, bank, col):
                for c in range(CT):
                    for e in range(2):
                        hs = slice(64 * e, 64 * e + 64)
                        last = stt(out=dst[hs, c, hs], in0=src[hs, c, hs], scalar=g_e[hs, col(c):col(c) + 1],
                                   in1=ps[hs, bank, P * c + 64 * e:P * c + 64 * e + 64], op0=ALU.mult, op1=ALU.add)
                return last

            for i, r in enumerate(ROWS):
                forget(i)
                dve.wait_ge(S("decays"), 3 * i + 3)
                if i:
                    dve.wait_ge(S("hg_out"), i)
                cols = slice(P * i, P * i + r)
                v.tensor_tensor(qd[:, :, 0:r], hqT[:, :, cols], each(g_e[:, 0:CT * r], CT), ALU.mult).then_inc(S("decayed"), 1)
                v.tensor_tensor(kd[:, :, 0:r], each(ps[:, 2, 0:CT * r], CT), each(g_en[:, 0:CT * r], CT), ALU.mult
                                ).then_inc(S("decayed"), 1)
                dve.wait_ge(S("f"), i + 1)
                v.tensor_tensor(kdec[0:r, :], ktok[0:r, :], g_e2[0:r, :], ALU.mult).then_inc(S("decayed"), 1)
                dve.wait_ge(S("hg_scores"), i + 1)
                for e in range(2):
                    v.tensor_tensor(scm[0:r, 4 * e:4 * e + 4, 0:r], each(ps[0:r, 3 + e, 0:CT * r], CT),
                                    over(chk_le if i < 4 else sq_le, r, CT, r), ALU.mult).then_inc(S("hg_masked"), 1)
                if i < 4:
                    for k in range(4):
                        x = 4 * i + k
                        dve.wait_ge(S("chunk_kv"), x + 1)
                        if x:
                            dve.wait_ge(S("chunk_states"), x)
                        state_update(state[:, (x + 1) % 8], state[:, x % 8], KV_BANK[k],
                                     lambda c: P * c + CHUNK * k + CHUNK - 1).then_inc(S("chunk_states"), 1)
                dve.wait_ge(S("hg_out"), i + 1)
                v.tensor_copy(ybT[:, :, cols], each(ps[:, 1, 0:CT * r], CT)).then_inc(S("o_read"), 1) if i else (
                    dve.wait_ge(S("rows_zeroed"), 48),
                    v.tensor_copy(ybT[:, :, cols], each(ps[:, 1, 0:CT * r], CT)).then_inc(S("o_read"), 1))
            for b in range(NB):
                dve.wait_ge(S("sample_kv"), b + 1)
                state_update(state0[:, b], state0[:, b], KV_BANK[b % 4], lambda c: TS * c + TQ * b + TQ - 1
                             ).then_inc(S("sample_states"), 1)
            dve.wait_ge(S("o_read"), NT)
            head_norm(2, ybT)
            dve.wait_ge(S("g_sigmoid"), 1)
            chain(v.tensor_tensor(flat(gT), flat(gT), flat(hqT), ALU.mult))
            chain.wait()
            dve.wait_ge(S("heads_normed"), 3)
            v.tensor_tensor(flat(ybT), flat(ybT), flat(gT), ALU.mult).then_inc(S("yb"), 1)

            dve.wait_ge(S("states_stored"), 16 * (2 + 2 * NB))
            chain(v.memset(flat(qblk), 0.0))
            chain(v.memset(flat(carry0), 0.0))
            chain.wait()
            for e in range(2):
                hs = slice(64 * e, 64 * e + 64)
                for c in range(CT):
                    dst = qblk[hs, :, :].rearrange("p b (c e q) -> p c e b q", c=CT, e=2)[:, c, e]
                    last = v.tensor_copy(dst, qT[hs, c, SEQ:T].rearrange("p (b q) -> p b q", b=NB))
            last.then_inc(S("q_blocks"), 1)
            dve.wait_ge(S("new_products"), 1)
            for c in range(CT):
                z4 = n_z[0:TS, 64 * c:64 * c + 64].rearrange("p (b x) -> p b x", b=NB)
                last = stt(out=z4, in0=ps[0:TS, 4, 64 * c:64 * c + 64].rearrange("p (b x) -> p b x", b=NB), scalar=SCALE,
                           in1=bias32[0:TS, 8 * c:8 * c + 8].unsqueeze(1).to_broadcast([TS, NB, 8]),
                           op0=ALU.mult, op1=ALU.add)
            last.then_inc(S("new_rows"), 1)
            dve.wait_ge(S("new_act"), 3)
            softplus(None, n_e[0:TS, :], None, n_t[0:TS, :], None)
            dve.wait_ge(S("new_rows"), 1)
            chain(stt(out=n_L[0:TS, :], in0=n_z[0:TS, :], scalar=0.0, in1=n_s[0:TS, :], op0=ALU.max, op1=ALU.add))
            chain.wait()
            chain(v.tensor_tensor(n_L[0:TS, :], n_L[0:TS, :], n_t[0:TS, :], ALU.add))
            chain.wait()
            v.tensor_tensor(n_L[0:TS, :], n_L[0:TS, :], new_m[:, :], ALU.mult).then_inc(S("new_rows"), 1)
            dve.wait_ge(S("new_rows"), 2)
            for b in range(NB):
                chain(v.tensor_copy(carry0[0:TS, b, :].rearrange("p (c x) -> p c x", c=CT),
                                    n_L[0:TS, :].rearrange("p (c b x) -> p b c x", c=CT, b=NB)[:, b]))
            dve.wait_ge(S("new_products"), 2)
            chain(v.tensor_tensor(n_z[0:TS, :], n_z[0:TS, :], ps[0:TS, 5, 0:256], ALU.subtract))
            chain.wait()
            v.tensor_tensor(n_z[0:TS, :], n_z[0:TS, :], new_neg[:, :], ALU.add).then_inc(S("new_rows"), 1)
            dve.wait_ge(S("new_products"), 3)
            v.tensor_copy(flat(obase), ps[:, 6, 0:256]).then_inc(S("new_rows"), 1)
            dve.wait_ge(S("new_rows"), 4)

            def turned_out(b, g):
                n = b * NGRP + g
                for j in range(2, GP):
                    dve.wait_ge(S("page_turned"), 4 * n + j + 1)
                    if not isinstance(n, int) or n >= 2:
                        dve.wait_ge(S("page_scores"), n - 1)
                    v.tensor_copy(d_kt[:, g % 2, j, :], ps[:, j, :]).then_inc(S("kT_dve"), 1)

            def losses(b, g):
                n = b * NGRP + g
                z, e, t, L = (x[:, g % 2, :] for x in (d_z, d_e, d_t, d_L))
                dve.wait_ge(S("page_scores"), n + 1)
                if not isinstance(n, int) or n >= 2:
                    dve.wait_ge(S("page_weights"), n - 1)
                stt(out=each(z, GP), in0=each(ps[:, 4 + g % 2, 0:128], GP), scalar=SCALE,
                    in1=bias32[:, :].unsqueeze(1).to_broadcast([P, GP, 32]), op0=ALU.mult, op1=ALU.add
                    ).then_inc(S("page_z"), 1)
                if g == 0:
                    chain(v.tensor_copy(d_R[:, 0, 0:32], carry0[:, bass.ds(b, 1), :].rearrange("p o c -> p (o c)")))
                dve.wait_ge(S("page_softplus"), 3 * n + 2)
                softplus(None, e, None, t, None)
                dve.wait_ge(S("page_softplus"), 3 * n + 3)
                chain(stt(out=L, in0=z, scalar=0.0, in1=d_ln[:, g % 2, :], op0=ALU.max, op1=ALU.add))
                chain.wait()
                chain(v.tensor_tensor(L, L, t, ALU.add))
                chain.wait()
                R = d_R[:, g % 4, :]
                for j in range(GP - 1):
                    add = v.tensor_tensor(R[:, 32 * j + 32:32 * j + 64], R[:, 32 * j:32 * j + 32], L[:, 32 * j:32 * j + 32],
                                          ALU.add)
                    if j < GP - 2:
                        chain(add)
                        chain.wait()
                add.then_inc(S("page_sums"), 1)
                dve.wait_ge(S("page_sums"), n + 1)
                if g < NGRP - 1:
                    chain(v.tensor_tensor(d_R[:, (g + 1) % 4, 0:32], R[:, 96:128], L[:, 96:128], ALU.add))

            def args(b, g):
                n = b * NGRP + g
                dve.wait_ge(S("page_remains"), n + 1)
                v.tensor_tensor(d_z[:, g % 2, :], d_z[:, g % 2, :], ps[:, 4 + g % 2, 128:256], ALU.subtract
                                ).then_inc(S("page_args"), 1)

            def decoded(b):
                dve.wait_ge(S("values_summed"), (b + 1) * NGRP)
                for e in range(2):
                    hs = slice(64 * e, 64 * e + 64)
                    got = ps[hs, 6, 0:32].rearrange("p (c e q) -> p e c q", c=CT, e=2)[:, e]
                    new = obase[hs, :, :].rearrange("p c (b e q) -> p e c b q", b=NB, e=2)[:, e, :, bass.ds(b, 1), :]
                    out = osbT[hs, :, SEQ:T].rearrange("p c (b q) -> p c b q", b=NB)[:, :, bass.ds(b, 1), :]
                    last = v.tensor_tensor(out, got.unsqueeze(2), new, ALU.add)
                last.then_inc(S("decoded"), 1)

            def before(b, g, lag):
                return (b, g - lag) if g >= lag else (b - 1, g - lag + NGRP)

            def decode_steps(b):
                chain.base, chain.n = chain_base(b), 0
                for g in range(NGRP):
                    turned_out(b, g)
                    for lag, part in ((1, losses), (2, args)):
                        if g >= lag or not isinstance(b, int):
                            part(*before(b, g, lag))
                    if g == 3 and not isinstance(b, int):
                        decoded(b - 1)
                per_loop.append(chain.n)

            per_loop = []
            chain_base = lambda b: chain.n + chain.base
            decode_steps(0)
            start = chain.base + chain.n
            steady = per_loop[0] + LOSS_STEPS
            chain_base = lambda b: start + (b - 1) * steady
            with dve.Fori(1, NB) as b:
                decode_steps(b)
            assert per_loop[1] == steady, per_loop
            chain.base, chain.n = start + (NB - 1) * steady, 0
            losses(NB - 1, NGRP - 1)
            args(NB - 1, NGRP - 2)
            args(NB - 1, NGRP - 1)
            decoded(NB - 1)

            for m in range(KD):
                dve.wait_ge(S("branch_products"), 4 * m + 3)
                dve.wait_ge(S("gates_read"), 2 * m + 2)
                v.tensor_tensor(each(mrg[:, m, :], 2), each(m_sa[:, m % 2, :], 2), ps[:, 4:6, 0:TH], ALU.mult
                                ).then_inc(S("branches_read"), 1)
                dve.wait_ge(S("branch_products"), 4 * m + 4)
                v.tensor_tensor(each(m_sb[:, m % 2, :], 2), each(m_sb[:, m % 2, :], 2), ps[:, 6:8, 0:TH], ALU.mult
                                ).then_inc(S("branches_read"), 1)
                dve.wait_ge(S("branches_read"), 2 * m + 2)
                v.tensor_tensor(mrg[:, m, :], mrg[:, m, :], m_sb[:, m % 2, :], ALU.add).then_inc(S("merged"), 1)
            dve.wait_ge(S("merged"), KD)
            v.memset(route, 0.0).then_inc(S("route_zero"), 1)
            dve.wait_ge(S("x_again"), 16 * NT)
            for i, r in enumerate(ROWS):
                dve.wait_ge(S("mixed"), i + 1)
                v.tensor_tensor(each(x2[0:r, i, :], 2), each(x2[0:r, i, :], 2), ps[0:r, 2 * (i % 2):2 * (i % 2) + 2, :],
                                ALU.add).then_inc(S("x2"), 1)
                dve.wait_ge(S("row_squares"), NT + i + 1)
                chain(v.tensor_scalar(rstd2[0:r, i:i + 1], ss2[0:r, i:i + 1], 1.0 / D, EPS, ALU.mult, ALU.add))
                chain.wait()
                v.reciprocal(rstd2[0:r, i:i + 1], rstd2[0:r, i:i + 1]).then_inc(S("row_inverses"), 1)
                dve.wait_ge(S("row_scales"), 2 + i)
                dve.wait_ge(S("w2_loaded"), 16)
                dve.wait_ge(S("x2"), i + 1)
                stt(out=h2[0:r, i, :], in0=x2[0:r, i, :], scalar=rstd2[0:r, i:i + 1], in1=w2r[0:r, :],
                    op0=ALU.mult, op1=ALU.mult).then_inc(S("h2"), 1)
            dve.wait_ge(S("b_router"), 32)
            dve.wait_ge(S("counters"), 2)
            for i, r in enumerate(ROWS):
                dve.wait_ge(S("h2_turned"), i + 1)
                if i >= 2:
                    dve.wait_ge(S("logits"), i - 1)
                v.tensor_copy(h2T[:, i % 2, :, 0:r], ps_h2[:, :, 0:r]).then_inc(S("h2_cols"), 1)
                dve.wait_ge(S("logits"), i + 1)

                def step(ins):
                    chain(ins)
                    chain.wait()

                g, x = slice(0, r), slice(NG, NG + NE)
                v.tensor_tensor(r_lg[g, :], ps[g, 6, 0:NG + NE], r_b36[g, :], ALU.add).then_inc(S("logits_read"), 1)
                dve.wait_ge(S("logits_read"), i + 1)
                chain(v.memset(r_gl[g, NG:8], -BIG))
                step(v.tensor_copy(r_gl[g, 0:NG], r_lg[g, 0:NG]))
                step(v.max(r_gm[g, :], r_gl[g, :]))
                chain(v.max_index(r_gi[g, :], r_gm[g, :], r_gl[g, :]))
                v.tensor_scalar(r_ng[g, :], r_gm[g, 0:1], -1.0, None, ALU.mult).then_inc(S("group_max"), 1)
                chain.wait()
                step(v.tensor_copy(r_gf[g, :], r_gi[g, 0:1]))
                step(v.tensor_scalar(r_m[g, :], gcol[g, :], r_gf[g, :], None, ALU.is_equal))
                chain(v.tensor_scalar(r_n[g, :], r_m[g, :], BIG, -BIG, ALU.mult, ALU.add))
                step(v.tensor_tensor(r_el[g, :], r_lg[g, x], r_m[g, :], ALU.mult))
                step(v.tensor_tensor(r_el[g, :], r_el[g, :], r_n[g, :], ALU.add))
                step(v.max(r_em[g, :], r_el[g, :]))
                chain(v.max_index(r_ei[g, :], r_em[g, :], r_el[g, :]))
                v.tensor_tensor(r_gap[g, :], r_em[g, 1:2], r_em[g, 0:1], ALU.subtract).then_inc(S("expert_gap"), 1)
                chain.wait()
                step(v.tensor_copy(r_EI[g, 2 * i:2 * i + 2], r_ei[g, 0:2]))
                for k in range(2):
                    chain(v.tensor_scalar(r_Ok[g, 2 * i + k, :], ecol[g, :], r_EI[g, 2 * i + k:2 * i + k + 1], None, ALU.is_equal))
                chain.wait()
                v.tensor_tensor(r_O[g, NE * i:NE * i + NE], r_Ok[g, 2 * i, :], r_Ok[g, 2 * i + 1, :], ALU.add
                                ).then_inc(S("chosen"), 1)
                dve.wait_ge(S("group_sum"), i + 1)
                dve.wait_ge(S("expert_ratio"), i + 1)
                step(v.tensor_scalar(r_t1[g, :], r_e2[g, :], 1.0, None, ALU.add))
                step(v.tensor_tensor(r_t1[g, :], r_t1[g, :], r_gs[g, :], ALU.mult))
                step(v.reciprocal(wts[g, 2 * i:2 * i + 1], r_t1[g, :]))
                step(v.tensor_tensor(wts[g, 2 * i + 1:2 * i + 2], wts[g, 2 * i:2 * i + 1], r_e2[g, :], ALU.mult))
            dve.wait_ge(S("list_sums"), 1)
            step(v.tensor_copy(r_cnt[0:NE, :], ps[0:NE, 6, 0:P]))
            step(v.tensor_scalar(r_ov[0:NE, :], r_cnt[0:NE, :], float(BLK), None, ALU.is_gt))
            for k in range(2, KMAX + 1):
                add = stt(out=r_ov[0:NE, :], in0=r_cnt[0:NE, :], scalar=float(BLK * k), in1=r_ov[0:NE, :],
                          op0=ALU.is_gt, op1=ALU.add)
                if k < KMAX:
                    step(add)
            add.then_inc(S("extra_blocks"), 1)
            chain(v.tensor_copy(r_rank[:, :], ps[:, 7, 0:NE * NT]) if False else v.tensor_copy(r_rank[:, 0:NE * 4], ps[:, 7, 0:NE * 4]))
            chain(v.tensor_copy(r_rank[0:TS, NE * 4:NE * 5], ps[0:TS, 7, NE * 4:NE * 5]))
            dve.wait_ge(S("list_sums"), 2)
            chain(v.tensor_copy(r_base[:, :], ps[:, 5, 0:NE]))
            chain(v.tensor_copy(r_incl[0:NE, :], ps[0:NE, 5, NE:NE + 1]))
            chain(v.tensor_copy(tab[0:1, NOVF:NOVF + 1], ps[0:1, 5, NE + 1:NE + 2]))
            chain.wait()
            v.tensor_scalar(r_ind[0:NE, :], ecol[0:NE, 0:NOVF], r_incl[0:NE, :], None, ALU.is_ge).then_inc(S("extra_after"), 1)
            for i, r in enumerate(ROWS):
                for k in range(2):
                    col = slice(2 * i + k, 2 * i + k + 1)
                    step(v.tensor_tensor_reduce(r_j[0:r, :], r_Ok[0:r, 2 * i + k, :], r_rank[0:r, NE * i:NE * i + NE], 1.0, 0.0,
                                                ALU.mult, ALU.add, r_RK[0:r, col]))
                    step(v.tensor_tensor_reduce(r_j[0:r, :], r_Ok[0:r, 2 * i + k, :], r_base[0:r, :], 1.0, 0.0,
                                                ALU.mult, ALU.add, r_BK[0:r, col]))
            step(v.tensor_tensor(r_BK, r_BK, r_EI, ALU.subtract))
            step(v.tensor_scalar(r_BK, r_BK, float(BLK), float((NE - 1) * BLK), ALU.mult, ALU.add))
            step(stt(out=r_BK, in0=r_RK, scalar=float(BLK), in1=r_BK, op0=ALU.is_ge, op1=ALU.mult))
            step(v.tensor_tensor(r_RK, r_RK, r_BK, ALU.add))
            step(stt(out=r_RK, in0=r_EI, scalar=float(BLK), in1=r_RK, op0=ALU.mult, op1=ALU.add))
            v.tensor_copy(slot_i[:, :], r_RK).then_inc(S("slots"), 1)
            dve.wait_ge(S("list_sums"), 3)
            step(v.tensor_scalar(r_ov[0:1, 0:NOVF], ps[0:1, 4, 0:NOVF], float(NE - 1), None, ALU.min))
            v.tensor_copy(tab[0:1, 0:NOVF], r_ov[0:1, 0:NOVF]).then_inc(S("extra_table"), 1)

            def cols_out(n, u):
                dve.wait_ge(S("rows_turned"), n + 1)
                if not (isinstance(n, int) and n < 2):
                    dve.wait_ge(S("gate_up"), n - 1)
                v.tensor_copy(flat(xgT[:, u]), ps[:, 0, :]).then_inc(S("xg_cols"), 1)

            def hidden(n, u):
                dve.wait_ge(S("silu"), n + 1)
                if not (isinstance(n, int) and n < 2):
                    dve.wait_ge(S("down"), n - 1)
                v.tensor_tensor(flat(m_h[:, u]), m_s[:, u, :], ps[:, 2 + 2 * u, 0:FJ * BLK], ALU.mult).then_inc(S("hidden"), 1)

            def y_out(n, u):
                dve.wait_ge(S("down"), n + 1)
                if not (isinstance(n, int) and n < 2):
                    dve.wait_ge(S(f"out_stored_{u}"), (n - u) * 8)
                v.tensor_copy(m_y[0:BLK, u, 512:D], ps[0:BLK, 6, :]).then_inc(S("y_dve"), 1)

            cols_out(0, 0)
            hidden(0, 0)
            cols_out(1, 1)
            hidden(1, 1)
            y_out(0, 0)
            with dve.Fori(1, NE // 2) as it:
                for u in range(2):
                    cols_out(2 * it + u, u)
                    hidden(2 * it + u, u)
                    y_out(2 * it + u - 1, 1 - u)
            y_out(NE - 1, 1)
            dve.wait_ge(S("extra_table"), 1)
            novf = dve.value_load(tab[0:1, NOVF:NOVF + 1], min_val=0, max_val=NOVF)
            with dve.Fori(0, NOVF) as i:
                with dve.If(i < novf):
                    dve.wait_ge(S("extra_turned"), i + 1)
                    v.tensor_copy(flat(xgT[:, 0]), ps[:, 0, :]).then_inc(S("extra_cols"), 1)
                    dve.wait_ge(S("extra_silu"), i + 1)
                    v.tensor_tensor(flat(m_h[:, 0]), m_s[:, 0, :], ps[:, 2, 0:FJ * BLK], ALU.mult).then_inc(S("extra_hidden"), 1)
                    dve.wait_ge(S("extra_down"), i + 1)
                    dve.wait_ge(S("extra_stored"), i * 16)
                    v.tensor_copy(m_y[0:BLK, 0, 512:D], ps[0:BLK, 6, :]).then_inc(S("extra_y_dve"), 1)
                with dve.Else():
                    dve.nop()
                dve.nop()
            for i, r in enumerate(ROWS):
                dve.wait_ge(S(f"y_gathered_{i % 2}"), 32 * (i // 2 + 1))
                step(stt(out=x2[0:r, i, :], in0=yg[0:r, 2 * (i % 2), :], scalar=wts[0:r, 2 * i:2 * i + 1], in1=x2[0:r, i, :],
                         op0=ALU.mult, op1=ALU.add))
                stt(out=x2[0:r, i, :], in0=yg[0:r, 2 * (i % 2) + 1, :], scalar=wts[0:r, 2 * i + 1:2 * i + 2], in1=x2[0:r, i, :],
                    op0=ALU.mult, op1=ALU.add).then_inc(S("y_rows"), 1)


_INS = ["x_prompt", "x_sample", "cache_k", "cache_v", "page_table", "state_hgrn", "norm1_w", "w_in", "q_norm_w",
        "k_norm_w", "sb_bias", "lb_logits", "hg_norm_w", "w_branch_a", "w_branch_b", "w_out", "norm2_w",
        "w_group_router", "b_group_router", "w_expert_router", "b_expert_router", "w_gate_exp", "w_up_exp",
        "w_down_exp"]
_OUTS = [("y_prompt", (1, SEQ, D)), ("y_sample", (NB, TQ, D)), ("new_k_prompt", (1, 1, SEQ, H, DH)),
         ("new_v_prompt", (1, 1, SEQ, H, DH)), ("new_hgrn_prompt", (1, 1, H, DH, DH)),
         ("new_k_sample", (1, NB, TQ, H, DH)), ("new_v_sample", (1, NB, TQ, H, DH)),
         ("new_hgrn_sample", (1, NB, H, DH, DH))]


def kernel(**inputs):
    import numpy as _np
    import concourse.bacc as _bacc
    from concourse import mybir as _mybir
    from concourse.bass_utils import run_bass_kernel_spmd as _run

    nc = _bacc.Bacc("TRN2", target_bir_lowering=False, num_devices=1)
    arrays, aps = {}, {}
    for name in _INS:
        x = _np.ascontiguousarray(inputs[name])
        arrays[f"in_{name}"] = x
        aps[name] = nc.dram_tensor(f"in_{name}", x.shape, _mybir.dt.from_np(x.dtype), kind="ExternalInput").ap()
    for name, shape in _OUTS:
        aps[name] = nc.dram_tensor(name, shape, F32, kind="ExternalOutput").ap()
    hybrid_step(nc, aps)
    r = _run(nc, [arrays], core_ids=[0])
    return tuple(r.results[0][name] for name, _ in _OUTS)
```

```python
from contextlib import ExitStack

import concourse.bass as bass
from concourse import mybir

F32 = mybir.dt.float32
I32 = mybir.dt.int32
U32 = mybir.dt.uint32
ALU = mybir.AluOpType
ACT = mybir.ActivationFunctionType
AX_X = mybir.AxisListType.X

P = 128
D = 1024
KD = D // P
SEQ = 512
NB = 8
TQ = 4
TS = NB * TQ
T = SEQ + TS
TH = T // 2
NT = 5
ROWS = [P] * 4 + [TS]
H = 8
DH = 64
CT = H * DH // P
W = H * DH
PAGE = 128
NPAGES = 32
GP = 4
NGRP = NPAGES // GP
CHUNK = 32
NE = 32
NG = 4
EG = NE // NG
FF = 512
FJ = FF // P
BLK = 64
KMAX = T // BLK
NOVF = 2 * T // BLK
NBLK = NE + NOVF
SCALE = float(DH) ** -0.5
EPS = 1e-6
BIG = 1e30
AZ = 1280
SB_OFF = [0, 512, 1024, 896]
SB_LEN = [512, 384, 256, 128]


class Chain:

    def __init__(self, eng, sem):
        self.eng, self.sem, self.n, self.base = eng, sem, 0, 0

    def __call__(self, ins):
        ins.then_inc(self.sem, 1)
        self.n += 1

    def wait(self):
        self.eng.wait_ge(self.sem, self.base + self.n)


def hybrid_step(nc, a):
    ctx = ExitStack()
    with ctx:
        def sb(name, shape, dt=F32):
            return ctx.enter_context(nc.sbuf_tensor(name, shape, dt))

        signals = {}

        def S(name):
            if name not in signals:
                signals[name] = ctx.enter_context(nc.semaphore(name))
            return signals[name]

        ps = ctx.enter_context(nc.psum_tensor("ps", [P, 8, 512], F32))
        xg_dram = nc.dram_tensor("expert_rows", [NBLK * BLK, D], F32).ap()
        yg_dram = nc.dram_tensor("expert_outs", [NBLK * BLK, D], F32).ap()

        ident = sb("ident", [P, P])
        ones = sb("ones", [P, P])
        tri_ge = sb("tri_ge", [P, P])
        headones = sb("headones", [P, P])
        mask_lt = sb("mask_lt", [P, P])
        neg_lt = sb("neg_lt", [P, P])
        tri_le = sb("tri_le", [P, P])
        chk_le = sb("chk_le", [P, P])
        chk_gt = sb("chk_gt", [P, P])
        sq_le = sb("sq_le", [TS, TS])
        sq_gt = sb("sq_gt", [TS, TS])
        new_m = sb("new_m", [TS, 256])
        new_neg = sb("new_neg", [TS, 256])
        in_b = sb("in_b", [TS, NB])
        w1c = sb("w1c", [P, KD])
        qkg = sb("qkg", [P, 3])
        bias8 = sb("bias8", [P, H])
        bias32 = sb("bias32", [P, 32])
        eps = sb("eps", [P, 1])
        ss = sb("ss", [P, 8])
        rstd = sb("rstd", [P, 8])
        ss2 = sb("ss2", [P, 8])
        rstd2 = sb("rstd2", [P, 8])

        hT = sb("hT", [P, KD, T])
        osbT = sb("osbT", [P, CT, T])
        ybT = sb("ybT", [P, CT, T])
        ARENA = 40960
        arena = sb("arena", [P, ARENA])

        def carve(off, *dims):
            n = 1
            for d in dims:
                n *= d
            assert off + n <= ARENA, (off, dims)
            v = arena[:, off:off + n]
            if len(dims) == 2:
                v = v.rearrange("p (a b) -> p a b", a=dims[0])
            if len(dims) == 3:
                v = v.rearrange("p (a b c) -> p a b c", a=dims[0], b=dims[1])
            return v

        wring = carve(0, 3, KD, 512)
        qT = carve(12288, CT, T)
        kT = carve(14464, CT, T)
        vtok = carve(16640, NT, W)
        hqT = carve(19200, CT, T)
        ftok = carve(21376, NT, W)
        itok = carve(23936, NT, W)
        gT = carve(26496, CT, T)
        A0 = 28672
        xt = carve(A0, NT, D)
        kout = carve(A0 + 5120, NT, W)
        sq = [carve(A0 + 7680, CT, T)] * 2 + [carve(A0, CT, T)]
        rs = [carve(A0 + 9856, CT, T)] * 2 + [carve(A0 + 2176, CT, T)]
        a_z = carve(A0, AZ)
        a_e = carve(A0 + 1280, AZ)
        a_ln = carve(A0 + 2560, AZ)
        a_t = carve(A0 + 3840, AZ)
        a_L = carve(A0 + 8960, AZ)
        a_A = carve(A0 + 5120, 2, AZ)

        state = carve(0, 8, CT, P)
        state0 = carve(4096, NB, CT, P)
        ib = carve(8192, NB, W)
        g0 = A0
        lbr = carve(g0, 2, W)
        lb = carve(g0 + 1024, W)
        oml = carve(g0 + 1536, W)
        ktok = carve(g0 + 2048, W)
        g_e = carve(g0 + 2560, W)
        g_en = carve(g0 + 3072, W)
        g_e2 = carve(g0 + 3584, W)
        qd = carve(g0 + 4096, CT, P)
        kd = carve(g0 + 4608, CT, P)
        kdec = carve(g0 + 5120, W)
        scm = carve(g0 + 5632, H, P)

        d_kt = carve(0, 2, GP, 512)
        D0 = 4096
        d_z = carve(D0, 2, 128)
        d_e = carve(D0 + 256, 2, 128)
        d_ln = carve(D0 + 512, 2, 128)
        d_t = carve(D0 + 768, 2, 128)
        d_L = carve(D0 + 1024, 2, 128)
        d_R = carve(D0 + 1280, 4, 128)
        d_A = carve(D0 + 1792, 4, 128)
        qblk = carve(D0 + 2304, NB, 32)
        obase = carve(D0 + 2560, CT, 64)
        n_z = carve(D0 + 2816, 256)
        n_e = carve(D0 + 3072, 256)
        n_t = carve(D0 + 3328, 256)
        n_L = carve(D0 + 3584, 256)
        carry0 = carve(D0 + 3840, NB, 32)
        n_s = carve(D0 + 4096, 256)
        d_o = carve(D0 + 4352, 512)
        vring = carve(17664, 4, GP, 512)
        kring = carve(36864, 2, GP, 512)
        pages = carve(36352, NB * NPAGES).bitcast(I32)

        mrg = carve(0, KD, T)
        m_sa = carve(4352, 2, T)
        m_sb = carve(5440, 2, T)
        wab = [carve(9472, CT, D), carve(13568, CT, D)]
        x2 = carve(17664, NT, D)
        gw = [[carve(25856 + 4096 * i + 2048 * e, KD, 256) for e in range(2)] for i in range(2)]
        WO_PARTS = [(22784, 3), (34048, 4), (6528, 1)]
        wo = [arena[:, o + D * k:o + D * k + D] for o, n in WO_PARTS for k in range(n)]
        h2 = carve(12288, NT, D)
        h2T = carve(25856, 2, KD, P)
        w2r = carve(27904, D)
        wr = carve(28928, KD, 36)
        sqj = carve(29216, D)

        M0 = 22784
        xg = carve(M0, 2, D)
        xgT = carve(M0 + 2048, 2, KD, BLK)
        m_s = carve(M0 + 3072, 2, FF)
        m_hr = carve(M0 + 4096, 2, FF)
        m_h = carve(M0 + 5120, 2, FJ, BLK)
        m_y = carve(M0 + 5632, 2, D)
        wgv = [carve(0, KD, FF), carve(12288, KD, FF)]
        wuv = [carve(4096, KD, FF), carve(30464, KD, FF)]
        wdv = [carve(8192, FJ, D), carve(34560, FJ, D)]
        yg = carve(0, 4, D)

        route = carve(38656, 1536)
        tab = sb("tab", [P, 32], I32)
        slot_i = sb("slot_i", [P, 2 * NT], I32)
        wts = sb("wts", [P, 2 * NT])

        x_tok = [a["x_prompt"][0, P * i:P * i + P, :] for i in range(4)] + [
            a["x_sample"].rearrange("b q d -> (b q) d")]
        w_in = a["w_in"][0].rearrange("(p k) n -> p k n", k=KD)
        w_br = [a[n][0].rearrange("(c p) n -> p c n", p=P) for n in ("w_branch_a", "w_branch_b")]

        CHUNKS = [("cols", qT), ("cols", kT), ("rows", vtok), ("cols", hqT), ("rows", ftok), ("rows", itok),
                  ("cols", gT)]
        JOBS = [(c, j) for c, (kind, _) in enumerate(CHUNKS) for j in range(4 if kind == "cols" else NT)]
        CHUNK_END = [max(n for n, (c, _) in enumerate(JOBS) if c == cc) + 1 for cc in range(len(CHUNKS))]
        QKV = CHUNK_END[2]
        KV_BANK = [5, 6, 7, 0]
        GATE_AT = [7 * 512, 9 * 512]

        def flat(v):
            return v.rearrange("p a b -> p (a b)")

        def each(v, n):
            return v.rearrange("p (a b) -> p a b", a=n)

        def diag3(off):
            return each(arena[:, off:off + 1536], 3)[:, :, 0:P]

        ps_attn = ps[:, 0:3, :].rearrange("p b c -> p (b c)")[:, 0:AZ]
        ps_h2 = ps[:, 4:6, :].rearrange("p b (k m) -> p (b k) m", k=4)
        kout_flat = kout.rearrange("p a b -> p (a b)")
        a_z_off, a_L_off = A0, A0 + 8960
        LOSS_STEPS = 6

        taken = [0]

        def small(n, rows=None):
            o = taken[0]
            taken[0] += n
            assert taken[0] <= 1536
            return route[:, o:o + n]

        gcol_i, ecol_i = small(NE).bitcast(I32), small(NE).bitcast(I32)
        gcol, ecol, r_b36, r_lg = small(NE), small(NE), small(NG + NE), small(NG + NE)
        r_gl, r_gm, r_gi, r_em, r_ei = small(8), small(8), small(8).bitcast(U32), small(8), small(8).bitcast(U32)
        r_ng, r_gf, r_ge, r_gs, r_e2, r_gap, r_t1 = (small(k) for k in (1, 1, NG, 1, 1, 1, 1))
        r_m, r_n, r_el, r_j = small(NE), small(NE), small(NE), small(NE)
        r_O = small(NE * NT)
        r_Ok = small(2 * NT * NE).rearrange("p (a b) -> p a b", a=2 * NT)
        r_rank, r_ov, r_cnt, r_base, r_ind, r_incl = (small(k) for k in (NE * NT, P, P, NE, NOVF, 1))
        r_EI, r_RK, r_BK = small(2 * NT), small(2 * NT), small(2 * NT)

        def extra_stage(i, k):
            return 4 * i + 4 + k

        block = ctx.enter_context(nc.Block())

        @block.sync
        def _(sp):
            for i in range(NT):
                sp.dma_start(xt[0:ROWS[i], i, :], x_tok[i]).then_inc(S("x_loaded"), 16)
            for c in range(len(CHUNKS)):
                if c >= 3:
                    sp.wait_ge(S("projected"), CHUNK_END[c - 3])
                sp.dma_start(wring[:, c % 3], w_in[:, :, 512 * c:512 * c + 512]).then_inc(S(f"w_in_{c % 3}"), 16)
                if c == 5:
                    sp.wait_ge(S("projection_out"), QKV)
                    sp.dma_start(a["new_v_prompt"][0, 0].rearrange("(i p) h d -> p i (h d)", p=P),
                                 vtok[:, 0:4, :]).then_inc(S("kv_stored"), 16)
                    sp.dma_start(a["new_v_sample"][0].rearrange("b q h d -> (b q) (h d)"),
                                 vtok[0:TS, 4, :]).then_inc(S("kv_stored"), 16)
                    sp.wait_ge(S("k_rows"), NT)
                    sp.dma_start(a["new_k_prompt"][0, 0].rearrange("(i p) h d -> p i (h d)", p=P),
                                 kout[:, 0:4, :]).then_inc(S("kv_stored"), 16)
                    sp.dma_start(a["new_k_sample"][0].rearrange("b q h d -> (b q) (h d)"),
                                 kout[0:TS, 4, :]).then_inc(S("kv_stored"), 16)
            sp.wait_ge(S("projected"), len(JOBS))
            sp.wait_ge(S("states_zero"), 1)
            st_in = a["state_hgrn"][0].rearrange("b (c e) k v -> e k b c v", e=2)
            st_out = a["new_hgrn_sample"][0].rearrange("b (c e) k v -> e k b c v", e=2)
            for e in range(2):
                for b in range(NB):
                    sp.dma_start(state0[64 * e:64 * e + 64, b, :, 64 * e:64 * e + 64],
                                 st_in[e, :, b]).then_inc(S("states_loaded"), 16)
            def pages_of(b, g):
                return [sp.value_load(pages[0:1, bass.ds(b * NPAGES + NPAGES - 1 - GP * g - j, 1)],
                                      min_val=0, max_val=a["cache_k"].shape[1] - 1) for j in range(GP)]

            def key_loads(b, g):
                n = b * NGRP + g
                for j, page in enumerate(pages_of(b, g)):
                    if not (isinstance(n, int) and n < 2):
                        sp.wait_ge(S("page_turned"), GP * (n - 2) + j + 1)
                    sp.dma_start(kring[:, g % 2, j, :], a["cache_k"][0, bass.ds(page, 1)].rearrange("a s h d -> (a s) (h d)")
                                 ).then_inc(S(f"cache_k_{g % 2}"), 16)

            def value_loads(b, g):
                n = b * NGRP + g
                numbers = pages_of(b, g)
                if not (isinstance(n, int) and n < 4):
                    sp.wait_ge(S("values_summed"), n - 3)
                for j, page in enumerate(numbers):
                    sp.dma_start(vring[:, g % 4, j, :], a["cache_v"][0, bass.ds(page, 1)].rearrange("a s h d -> (a s) (h d)")
                                 ).then_inc(S(f"cache_v_{g % 4}"), 16)

            def before(b, g, lag):
                return (b, g - lag) if g >= lag else (b - 1, g - lag + NGRP)

            sp.dma_start(pages[0:1, :], a["page_table"].rearrange("(o b) n -> o (b n)", o=1)).then_inc(S("page_table"), 16)
            sp.wait_ge(S("page_table"), 16)
            for g in range(2):
                key_loads(0, g)
            sp.wait_ge(S("chunk_states"), 16)
            p_out = a["new_hgrn_prompt"][0, 0].rearrange("(c e) k v -> e k c v", e=2)
            for e in range(2):
                sp.dma_start(p_out[e], state[64 * e:64 * e + 64, 0, :, 64 * e:64 * e + 64]
                             ).then_inc(S("states_stored"), 16)
            sp.wait_ge(S("sample_states"), NB)
            for e in range(2):
                for b in range(NB):
                    sp.dma_start(st_out[e, :, b], state0[64 * e:64 * e + 64, b, :, 64 * e:64 * e + 64]
                                 ).then_inc(S("states_stored"), 16)

            sp.wait_ge(S("yb"), 1)
            sp.wait_ge(S("new_rows"), 4)
            for g in range(2, NGRP):
                value_loads(0, g - 2)
                key_loads(0, g)
            def gate_loads(q):
                for e in range(2):
                    c0 = GATE_AT[e] + 256 * q
                    sp.dma_start(gw[q % 2][e], w_in[:, :, c0:c0 + 256]).then_inc(S(f"w_gate_{q % 2}"), 16)

            with sp.Fori(1, NB) as b:
                for g in range(NGRP):
                    value_loads(*before(b, g, 2))
                    key_loads(b, g)
            for g in (NGRP - 2, NGRP - 1):
                value_loads(NB - 1, g)
            for e in range(2):
                sp.dma_start(wab[e], w_br[e]).then_inc(S("w_branches"), 16)
            for q in range(2):
                gate_loads(q)

            sp.wait_ge(S("values_summed"), NB * NGRP)
            for i in range(NT):
                sp.dma_start(x2[0:ROWS[i], i, :], x_tok[i]).then_inc(S("x_again"), 16)
            w_out = a["w_out"][0].rearrange("(k p) n -> p k n", p=P)
            k = 0
            for o, n in WO_PARTS:
                if o == WO_PARTS[-1][0]:
                    sp.wait_ge(S("decoded"), NB)
                sp.dma_start(each(arena[:, o:o + D * n], n), w_out[:, k:k + n]).then_inc(S("w_out"), 16)
                k += n
            for q in range(2, KD // 2):
                sp.wait_ge(S("branch_products"), 8 * (q - 1))
                gate_loads(q)
            def expert_rows(n, u):
                if not (isinstance(n, int) and n < 2):
                    sp.wait_ge(S("rows_turned"), n - 1)
                sp.dma_start(xg[0:BLK, u, :], xg_dram[bass.ds(n * BLK, BLK), :]).then_inc(S(f"rows_{u}"), 16)

            def expert_weights(n, u, e):
                if not (isinstance(n, int) and n == 0):
                    expert_rows(n, u)
                late = not (isinstance(n, int) and n < 2)
                if late:
                    sp.wait_ge(S("gate_up"), n - 1)
                sp.dma_start(wgv[u], a["w_gate_exp"][0, bass.ds(e, 1)].rearrange("a (p k) f -> (a p) k f", k=KD)
                             ).then_inc(S(f"w_gate_exp_{u}"), 16)
                sp.dma_start(wuv[u], a["w_up_exp"][0, bass.ds(e, 1)].rearrange("a (p k) f -> (a p) k f", k=KD)
                             ).then_inc(S(f"w_up_exp_{u}"), 16)
                if late:
                    sp.wait_ge(S("down"), n - 1)
                sp.dma_start(wdv[u], a["w_down_exp"][0, bass.ds(e, 1)].rearrange("a (p j) d -> (a p) j d", j=FJ)
                             ).then_inc(S(f"w_down_exp_{u}"), 16)

            sp.wait_ge(S("mixed"), NT)
            expert_weights(0, 0, 0)
            sp.wait_ge(S("h2_scattered"), 32 * NT)
            sp.wait_ge(S("logits"), NT)
            expert_rows(0, 0)
            expert_weights(1, 1, 1)
            with sp.Fori(1, NE // 2) as it:
                for u in range(2):
                    expert_weights(2 * it + u, u, 2 * it + u)
            sp.wait_ge(S("down"), NE)
            novf = sp.value_load(tab[0:1, NOVF:NOVF + 1], min_val=0, max_val=NOVF)
            with sp.Fori(0, NOVF) as i:
                e = sp.value_load(tab[0:1, bass.ds(i, 1)], min_val=0, max_val=NE - 1)
                with sp.If(i < novf):
                    sp.wait_ge(S("extra_products"), extra_stage(i, 0))
                    sp.dma_start(wgv[0], a["w_gate_exp"][0, bass.ds(e, 1)].rearrange("a (p k) f -> (a p) k f", k=KD)
                                 ).then_inc(S("extra_loaded"), 16)
                    sp.dma_start(wuv[0], a["w_up_exp"][0, bass.ds(e, 1)].rearrange("a (p k) f -> (a p) k f", k=KD)
                                 ).then_inc(S("extra_loaded"), 16)
                    sp.dma_start(wdv[0], a["w_down_exp"][0, bass.ds(e, 1)].rearrange("a (p j) d -> (a p) j d", j=FJ)
                                 ).then_inc(S("extra_loaded"), 16)
                    sp.dma_start(xg[0:BLK, 0, :], xg_dram[bass.ds((NE + i) * BLK, BLK), :]).then_inc(S("extra_loaded"), 16)
                with sp.Else():
                    sp.nop()
                sp.nop()
            for i in range(NT):
                sp.wait_ge(S("y_rows"), i + 1)
                dst = a["y_prompt"][0, P * i:P * i + P, :] if i < 4 else a["y_sample"].rearrange("b q d -> (b q) d")
                sp.dma_start(dst, x2[0:ROWS[i], i, :]).then_inc(S("y_stored"), 16)
            sp.wait_ge(S("y_stored"), 16 * NT)
            sp.wait_ge(S("kv_stored"), 64)
            sp.wait_ge(S("states_stored"), 16 * (2 + 2 * NB))

        @block.gpsimd
        def _(pool):
            chain = Chain(pool, S("pool_chain"))

            def select(v, pattern, op, fill, base, cm):
                chain(nc.gpsimd.affine_select(out=v, in_=v, compare_op=op, fill=fill, base=base, pattern=pattern,
                                              channel_multiplier=cm))

            for t, v in ((ident, 0.0), (ones, 1.0), (tri_ge, 1.0), (headones, 1.0), (mask_lt, 1.0), (neg_lt, 0.0),
                         (tri_le, 1.0), (chk_le, 1.0), (chk_gt, 1.0), (sq_le, 1.0), (sq_gt, 1.0), (new_m, 1.0),
                         (new_neg, 0.0), (in_b, 1.0), (eps, EPS)):
                chain(nc.gpsimd.memset(t[:, :], v))
            chain(nc.gpsimd.memset(flat(ybT), 0.0))
            chain.wait()
            select(ident[:, :], [[-1, P]], ALU.not_equal, 1.0, 0, 1)
            select(tri_ge[:, :], [[-1, P]], ALU.is_ge, 0.0, 0, 1)
            select(mask_lt[:, :], [[1, P]], ALU.is_gt, 0.0, 0, -1)
            select(neg_lt[:, :], [[1, P]], ALU.is_gt, -BIG, 0, -1)
            select(tri_le[:, :], [[1, P]], ALU.is_ge, 0.0, 0, -1)
            select(chk_le[:, :], [[1, P]], ALU.is_ge, 0.0, 0, -1)
            select(chk_gt[:, :], [[-1, P]], ALU.is_gt, 0.0, 0, 1)
            select(sq_le[:, :], [[1, TS]], ALU.is_ge, 0.0, 0, -1)
            select(sq_gt[:, :], [[-1, TS]], ALU.is_gt, 0.0, 0, 1)
            select(each(headones[:, :], 2), [[-64, 2], [0, 64]], ALU.is_ge, 0.0, 0, 1)
            select(in_b[:, :], [[-TQ, NB]], ALU.is_ge, 0.0, 0, 1)
            new4 = [v[:, :].rearrange("p (c b e q) -> p c b e q", c=CT, b=NB, e=2) for v in (new_m, new_neg)]
            for c in range(CT):
                for v, fill in zip(new4, (0.0, -BIG)):
                    select(v[:, c], [[-TQ, NB], [0, 2], [0, TQ]], ALU.is_ge, fill, 0, 1)
            chain.wait()
            select(each(headones[:, :], 2), [[64, 2], [0, 64]], ALU.is_ge, 0.0, 63, -1)
            select(each(chk_le[:, :], 4), [[-CHUNK, 4], [0, CHUNK]], ALU.is_ge, 0.0, 0, 1)
            select(each(chk_gt[:, :], 4), [[CHUNK, 4], [0, CHUNK]], ALU.is_ge, 0.0, CHUNK - 1, -1)
            select(each(sq_le[:, :], NB), [[-TQ, NB], [0, TQ]], ALU.is_ge, 0.0, 0, 1)
            select(each(sq_gt[:, :], NB), [[TQ, NB], [0, TQ]], ALU.is_ge, 0.0, TQ - 1, -1)
            select(in_b[:, :], [[TQ, NB]], ALU.is_ge, 0.0, TQ - 1, -1)
            for c in range(CT):
                for v, fill in zip(new4, (0.0, -BIG)):
                    select(v[:, c], [[TQ, NB], [0, 2], [1, TQ]], ALU.is_gt, fill, 0, -1)
            chain.wait()
            nc.gpsimd.memset(ss[:, :], 0.0).then_inc(S("constants"), 1)
            pool.wait_ge(S("projected"), QKV)
            full = NBLK * BLK // P
            pool.dma_start(xg_dram[0:full * P, :].rearrange("(n p) d -> p n d", p=P),
                           flat(ybT)[:, 0:D].unsqueeze(1).to_broadcast([P, full, D])).then_inc(S("rows_zeroed"), 16)
            pool.dma_start(xg_dram[full * P:NBLK * BLK, :], flat(ybT)[0:NBLK * BLK - full * P, 0:D]
                           ).then_inc(S("rows_zeroed"), 16)
            extra = yg_dram[NE * BLK:NBLK * BLK, :].rearrange("(n p) d -> p n d", p=BLK)
            pool.dma_start(extra, flat(ybT)[0:BLK, 0:D].unsqueeze(1).to_broadcast([BLK, NOVF, D])
                           ).then_inc(S("rows_zeroed"), 16)
            pool.wait_ge(S("projected"), len(JOBS))
            nc.gpsimd.memset(arena[:, 0:8192], 0.0).then_inc(S("states_zero"), 1)
            pool.wait_ge(S("x2"), 1)
            chain(nc.gpsimd.iota(gcol_i, pattern=[[1, NG], [0, EG]], base=0, channel_multiplier=0))
            chain(nc.gpsimd.iota(ecol_i, pattern=[[1, NE]], base=0, channel_multiplier=0))
            chain.wait()
            nc.gpsimd.tensor_copy(gcol, gcol_i).then_inc(S("counters"), 1)
            nc.gpsimd.tensor_copy(ecol, ecol_i).then_inc(S("counters"), 1)
            pool.wait_ge(S("rows_zeroed"), 48)
            pool.wait_ge(S("slots"), 1)
            for i in range(NT):
                for k in range(2):
                    pool.indirect_dma_start(
                        out=xg_dram, out_offset=bass.IndirectOffsetOnAxis(
                            ap=slot_i[0:ROWS[i], 2 * i + k:2 * i + k + 1].bitcast(U32), axis=0),
                        in_=h2[0:ROWS[i], i, :], in_offset=None).then_inc(S("h2_scattered"), 16)
            pool.wait_ge(S("extra_table"), 1)
            novf = pool.value_load(tab[0:1, NOVF:NOVF + 1], min_val=0, max_val=NOVF)
            pool.wait_ge(S("out_stored_0"), 16 * NE // 2)
            pool.wait_ge(S("out_stored_1"), 16 * NE // 2)
            pool.wait_ge(S("extra_stored"), novf * 16 + 16)
            pool.sem_inc(S("pool_passed"), 1)
            for i in range(NT):
                if i >= 2:
                    pool.wait_ge(S("y_rows"), i - 1)
                for k in range(2):
                    pool.indirect_dma_start(
                        out=yg[0:ROWS[i], 2 * (i % 2) + k, :], out_offset=None, in_=yg_dram,
                        in_offset=bass.IndirectOffsetOnAxis(
                            ap=slot_i[0:ROWS[i], 2 * i + k:2 * i + k + 1].bitcast(U32), axis=0)
                    ).then_inc(S(f"y_gathered_{i % 2}"), 16)

        @block.tensor
        def _(pe):
            mm = nc.tensor.matmul
            turn = nc.tensor.transpose

            pe.wait_ge(S("constants"), 1)
            for i, r in enumerate(ROWS):
                pe.wait_ge(S("x_normed"), i + 1)
                for kk in range(2):
                    n = 2 * i + kk
                    if n >= 4:
                        pe.wait_ge(S("hT"), n - 3)
                    for c in range(4):
                        cols = xt[0:r, i, :].rearrange("p (m k) -> p k m", k=KD)[:, 4 * kk + c, :]
                        last = turn(ps[:, 4 + n % 4, P * c:P * c + r], cols, ident[0:r, 0:r])
                    last.then_inc(S("x_turned"), 1)
            pe.wait_ge(S("hT"), 2 * NT)

            def project(n):
                c, j = JOBS[n]
                bank = 4 + 2 * (n % 2)
                if j == 0:
                    pe.wait_ge(S(f"w_in_{c % 3}"), 16 * (c // 3 + 1))
                if n >= 2:
                    pe.wait_ge(S("projection_out"), n - 1)
                for k in range(KD):
                    if CHUNKS[c][0] == "cols":
                        for hf in range(2):
                            last = mm(ps[:, bank + hf, 0:TH], wring[:, c % 3, k, P * j:P * j + P],
                                      hT[:, k, TH * hf:TH * hf + TH], start=k == 0, stop=k == KD - 1)
                    else:
                        last = mm(ps[0:ROWS[j], bank, :], hT[:, k, P * j:P * j + ROWS[j]], wring[:, c % 3, k, :],
                                  start=k == 0, stop=k == KD - 1)
                last.then_inc(S("projected"), 1)

            def head_sums(m):
                pe.wait_ge(S("squares"), m + 1)
                for c in range(CT):
                    if m or c >= 2:
                        pe.wait_ge(S("head_roots"), 4 * m + max(c - 1, 0))
                    for hf in range(2):
                        last = mm(ps[:, 2 * (c % 2) + hf, 0:TH], headones[:, :], sq[m][:, c, TH * hf:TH * hf + TH],
                                  start=True, stop=True)
                    last.then_inc(S("head_sums"), 1)

            for n in range(4):
                project(n)
            for n in range(4, 8):
                project(n)
            head_sums(0)
            for n in range(8, QKV):
                project(n)
            head_sums(1)
            pe.wait_ge(S("heads_normed"), 2 * CT)
            for i, r in enumerate(ROWS):
                if i >= 4:
                    pe.wait_ge(S("k_rows"), i - 3)
                for c in range(CT):
                    last = turn(ps[0:r, i % 4, P * c:P * c + P], kT[:, c, P * i:P * i + r], ident[:, :])
                last.then_inc(S("k_turned_rows"), 1)

            def attn_scores(h):
                if h:
                    pe.wait_ge(S("attn_args"), h)
                else:
                    pe.wait_ge(S("k_rows"), NT)
                r0 = 64 * (h % 2)
                for s in range(4):
                    o = SB_OFF[s]
                    last = mm(ps[:, o // 512, o % 512:o % 512 + SB_LEN[s]], kT[r0:r0 + 64, h // 2, P * s:P * s + P],
                              qT[r0:r0 + 64, h // 2, P * s:SEQ], start=True, stop=True)
                last.then_inc(S("attn_scores"), 1)

            def attn_remain(h):
                pe.wait_ge(S("attn_losses"), h + 1)
                for s in (0, 1, 3, 2):
                    o = SB_OFF[s]
                    bank, c0 = o // 512, o % 512
                    last = mm(ps[:, bank, c0:c0 + SB_LEN[s]], tri_ge[:, :], a_L[:, o:o + SB_LEN[s]],
                              start=True, stop=s == 3)
                    for j in range(s + 1, 4):
                        skip = P * (j - s)
                        last = mm(ps[:, bank, c0 + skip:c0 + SB_LEN[s]], ones[:, :],
                                  a_L[:, SB_OFF[j]:SB_OFF[j] + SB_LEN[j]], start=False, stop=j == 3)
                last.then_inc(S("attn_remains"), 1)

            def attn_values(h):
                pe.wait_ge(S("attn_weights"), h + 1)
                r0 = 64 * (h % 2)
                if h % 2 == 0 and h:
                    pe.wait_ge(S("attn_out"), h // 2)
                for s in range(4):
                    last = mm(ps[r0:r0 + 64, 3, P * s:SEQ], vtok[:, s, DH * h:DH * h + DH],
                              a_A[:, h % 2, SB_OFF[s]:SB_OFF[s] + SB_LEN[s]], start=s == 0, stop=s == 3)
                last.then_inc(S("attn_values"), 1)

            n = QKV
            for h in range(H):
                attn_scores(h)
                if n < len(JOBS):
                    project(n)
                    n += 1
                if h == 0 or h == 4:
                    project(n)
                    n += 1
                attn_remain(h)
                if n < len(JOBS):
                    project(n)
                    n += 1
                attn_values(h)
            assert n == len(JOBS)

            for i in range(5):
                r, prompt = ROWS[i], i < 4
                le, gt = (chk_le, chk_gt) if prompt else (sq_le, sq_gt)
                pe.wait_ge(S("log_f"), i + 1)
                if i:
                    pe.wait_ge(S("chunk_states"), 4 * i)
                    pe.wait_ge(S("o_read"), i)
                    pe.wait_ge(S("decayed"), 3 * i)
                else:
                    pe.wait_ge(S("attn_args"), H)
                for c in range(CT):
                    mm(ps[:, 0, r * c:r * c + r], ftok[0:r, i, P * c:P * c + P], le[0:r, 0:r], start=True, stop=True)
                mm(ps[0:r, 1, :], gt[0:r, 0:r], ftok[0:r, i, :], start=True, stop=True)
                for c in range(CT):
                    last = turn(ps[:, 2, r * c:r * c + r], ktok[0:r, P * c:P * c + P], ident[0:r, 0:r])
                last.then_inc(S("decay_sums"), 1)
                pe.wait_ge(S("decayed"), 3 * i + 3)
                if i:
                    pe.wait_ge(S("hg_masked"), 2 * i)
                else:
                    pe.wait_ge(S("attn_out"), CT)
                    pe.wait_ge(S("projection_out"), len(JOBS))
                for e in range(2):
                    for c in range(CT):
                        last = mm(ps[0:r, 3 + e, r * c:r * c + r], kd[64 * e:64 * e + 64, c, 0:r],
                                  qd[64 * e:64 * e + 64, c, 0:r], start=True, stop=True)
                last.then_inc(S("hg_scores"), 1)
                if prompt:
                    for k in range(4):
                        for c in range(CT):
                            last = mm(ps[:, KV_BANK[k], P * c:P * c + P], kdec[CHUNK * k:CHUNK * k + CHUNK, P * c:P * c + P],
                                      itok[CHUNK * k:CHUNK * k + CHUNK, i, P * c:P * c + P], start=True, stop=True)
                        last.then_inc(S("chunk_kv"), 1)
                pe.wait_ge(S("hg_masked"), 2 * i + 2)
                for c in range(CT):
                    for e in range(2):
                        mm(ps[64 * e:64 * e + 64, 1, r * c:r * c + r], itok[0:r, i, P * c + 64 * e:P * c + 64 * e + 64],
                           scm[0:r, 4 * e + c, 0:r], start=c == 0, stop=False, skip_group_check=True)
                if prompt:
                    for k in range(4):
                        if i or k:
                            pe.wait_ge(S("chunk_states"), 4 * i + k)
                        else:
                            pe.wait_ge(S("states_zero"), 1)
                        for c in range(CT):
                            last = mm(ps[:, 1, P * c + CHUNK * k:P * c + CHUNK * k + CHUNK], state[:, (4 * i + k) % 8, c, :],
                                      qd[:, c, CHUNK * k:CHUNK * k + CHUNK], start=False, stop=True, skip_group_check=True)
                    last.then_inc(S("hg_out"), 1)
                else:
                    pe.wait_ge(S("states_loaded"), 32 * NB)
                    for b in range(NB):
                        for c in range(CT):
                            last = mm(ps[:, 1, TS * c + TQ * b:TS * c + TQ * b + TQ], state0[:, b, c, :],
                                      qd[:, c, TQ * b:TQ * b + TQ], start=False, stop=True, skip_group_check=True)
                    last.then_inc(S("hg_out"), 1)
                    pe.wait_ge(S("ib"), 1)
                    for b in range(NB):
                        if b >= 4:
                            pe.wait_ge(S("sample_states"), b - 3)
                        for c in range(CT):
                            last = mm(ps[:, KV_BANK[b % 4], P * c:P * c + P], kdec[0:r, P * c:P * c + P],
                                      ib[0:r, b, P * c:P * c + P], start=True, stop=True)
                        last.then_inc(S("sample_kv"), 1)
            pe.wait_ge(S("sample_states"), NB)
            head_sums(2)

            pe.wait_ge(S("q_blocks"), 1)
            for c in range(CT):
                last = mm(ps[0:TS, 4, 64 * c:64 * c + 64], kT[:, c, SEQ:T], qblk[:, :, 8 * c:8 * c + 8],
                          start=True, stop=True)
            last.then_inc(S("new_products"), 1)
            pe.wait_ge(S("new_rows"), 2)
            mm(ps[0:TS, 5, 0:256], tri_ge[0:TS, 0:TS], n_L[0:TS, :], start=True, stop=True).then_inc(S("new_products"), 1)
            pe.wait_ge(S("new_act"), 4)
            for c in range(CT):
                last = mm(ps[:, 6, 64 * c:64 * c + 64], vtok[0:TS, 4, P * c:P * c + P],
                          n_e[0:TS, 64 * c:64 * c + 64], start=True, stop=True)
            last.then_inc(S("new_products"), 1)

            def turn_keys(b, g, j):
                n = b * NGRP + g
                if j == 0:
                    pe.wait_ge(S(f"cache_k_{g % 2}"), (b * 4 + g // 2 + 1) * 16 * GP)
                if g or not isinstance(b, int):
                    pe.wait_ge(S("kT_act" if j < 2 else "kT_dve"), 2 * n - 1 + j % 2)
                for c in range(CT):
                    last = turn(ps[:, j, P * c:P * c + P], kring[:, g % 2, j, P * c:P * c + P], ident[:, :])
                last.then_inc(S("page_turned"), 1)

            def page_scores(b, g, j):
                n = b * NGRP + g
                if j == 0:
                    pe.wait_ge(S("kT_act"), 2 * n + 2)
                    pe.wait_ge(S("kT_dve"), 2 * n + 2)
                    if not isinstance(n, int) or n >= 2:
                        pe.wait_ge(S("page_args"), n - 1)
                for c in range(CT):
                    last = mm(ps[:, 4 + g % 2, 32 * j + 8 * c:32 * j + 8 * c + 8], d_kt[:, g % 2, j, P * c:P * c + P],
                              qblk[:, bass.ds(b, 1), 8 * c:8 * c + 8], start=True, stop=True)
                if j == GP - 1:
                    last.then_inc(S("page_scores"), 1)

            def page_remains(b, g):
                n = b * NGRP + g
                pe.wait_ge(S("page_sums"), n + 1)
                mm(ps[:, 4 + g % 2, 128:256], tri_ge[:, :], d_L[:, g % 2, :], start=True, stop=False)
                mm(ps[:, 4 + g % 2, 128:256], ones[:, :], d_R[:, g % 4, :], start=False, stop=True
                   ).then_inc(S("page_remains"), 1)

            def page_values(b, g, j):
                n = b * NGRP + g
                if j == 0:
                    pe.wait_ge(S(f"cache_v_{g % 4}"), (b * 2 + g // 4 + 1) * 16 * GP)
                    pe.wait_ge(S("page_weights"), n + 1)
                    if g == 0 and isinstance(b, int) and b == 0:
                        pe.wait_ge(S("new_rows"), 4)
                    elif g == 0:
                        pe.wait_ge(S("values_out"), b)
                last = mm(ps[0:32, 6, :], d_A[:, g % 4, 32 * j:32 * j + 32], vring[:, g % 4, j, :],
                          start=g == 0 and j == 0, stop=g == NGRP - 1 and j == GP - 1)
                if j == GP - 1:
                    last.then_inc(S("values_summed"), 1)

            def turn_values(b):
                pe.wait_ge(S("values_out"), b + 1)
                pe.sem_inc(S("pe_passed"), 1)
                for c in range(CT):
                    last = turn(ps[:, 7, 32 * c:32 * c + 32], d_o[0:32, P * c:P * c + P], ident[0:32, 0:32])
                last.then_inc(S("values_turned"), 1)

            def before(b, g, lag):
                return (b, g - lag) if g >= lag else (b - 1, g - lag + NGRP)

            def decode_steps(b):
                for g in range(NGRP):
                    if g == 4 and not isinstance(b, int):
                        turn_values(b - 1)
                    for j in range(GP):
                        if j == 3 and (g >= 2 or not isinstance(b, int)):
                            page_remains(*before(b, g, 2))
                        turn_keys(b, g, j)
                        for lag, part in ((1, page_scores), (3, page_values)):
                            if g >= lag or not isinstance(b, int):
                                part(*before(b, g, lag), j)

            pe.wait_ge(S("head_roots"), 3 * CT)
            decode_steps(0)
            with pe.Fori(1, NB) as b:
                decode_steps(b)
            page_remains(NB - 1, NGRP - 2)
            for j in range(GP):
                page_scores(NB - 1, NGRP - 1, j)
                page_values(NB - 1, NGRP - 3, j)
            page_remains(NB - 1, NGRP - 1)
            for g in (NGRP - 2, NGRP - 1):
                for j in range(GP):
                    page_values(NB - 1, g, j)
            turn_values(NB - 1)

            pe.wait_ge(S("w_branches"), 32)
            pe.wait_ge(S("decoded"), NB)
            for m in range(KD):
                for e in range(4):
                    n = 4 * m + e
                    bank = 2 * (n % 4)
                    if m:
                        pe.wait_ge(S("gates_read" if e < 2 else "branches_read"), 2 * m - 1 + e % 2)
                    if e == 0 and m % 2 == 0:
                        pe.wait_ge(S(f"w_gate_{m // 2 % 2}"), 32 * (m // 4 + 1))
                    for k in range(KD if e < 2 else CT):
                        for hf in range(2):
                            cols = slice(TH * hf, TH * hf + TH)
                            if e < 2:
                                last = mm(ps[:, bank + hf, 0:TH], gw[m // 2 % 2][e][:, k, P * (m % 2):P * (m % 2) + P], hT[:, k, cols],
                                          start=k == 0, stop=k == KD - 1)
                            else:
                                last = mm(ps[:, bank + hf, 0:TH], wab[e - 2][:, k, P * m:P * m + P],
                                          (osbT, ybT)[e - 2][:, k, cols], start=k == 0, stop=k == CT - 1)
                    last.then_inc(S("branch_products"), 1)
            pe.wait_ge(S("merged"), KD)
            pe.wait_ge(S("w_out"), 16 * len(WO_PARTS))
            for i, r in enumerate(ROWS):
                if i >= 2:
                    pe.wait_ge(S("x2"), i - 1)
                for k in range(KD):
                    for hf in range(2):
                        last = mm(ps[0:r, 2 * (i % 2) + hf, :], mrg[:, k, P * i:P * i + r], wo[k][:, 512 * hf:512 * hf + 512],
                                  start=k == 0, stop=k == KD - 1)
                last.then_inc(S("mixed"), 1)
            pe.wait_ge(S("w_router"), 32)
            for i, r in enumerate(ROWS):
                pe.wait_ge(S("h2"), i + 1)
                if i:
                    pe.wait_ge(S("h2_cols"), i)
                for k in range(KD):
                    cols = h2[0:r, i, :].rearrange("p (m k) -> p k m", k=KD)[:, k, :]
                    last = turn(ps[:, 4 + k // 4, P * (k % 4):P * (k % 4) + r], cols, ident[0:r, 0:r])
                last.then_inc(S("h2_turned"), 1)
                pe.wait_ge(S("h2_cols"), i + 1)
                if i:
                    pe.wait_ge(S("logits_read"), i)
                for k in range(KD):
                    last = mm(ps[0:r, 6, 0:NG + NE], h2T[:, i % 2, k, 0:r], wr[:, k, :], start=k == 0, stop=k == KD - 1)
                last.then_inc(S("logits"), 1)
            pe.wait_ge(S("chosen"), NT)
            for i, r in enumerate(ROWS):
                for j in range(i + 1):
                    lhs = mask_lt[0:r, 0:r] if j == i else ones[0:ROWS[j], 0:r]
                    mm(ps[0:r, 7, NE * i:NE * i + NE], lhs, r_O[0:ROWS[j], NE * j:NE * j + NE], start=j == 0, stop=j == i)
            for j, r in enumerate(ROWS):
                last = mm(ps[0:NE, 6, 0:P], r_O[0:r, NE * j:NE * j + NE], ones[0:r, :], start=j == 0, stop=j == NT - 1)
            last.then_inc(S("list_sums"), 1)
            pe.wait_ge(S("extra_blocks"), 1)
            mm(ps[:, 5, 0:NE], r_ov[0:NE, :], mask_lt[0:NE, 0:NE], start=True, stop=True)
            mm(ps[0:NE, 5, NE:NE + 1], tri_le[0:NE, 0:NE], r_ov[0:NE, 0:1], start=True, stop=True)
            mm(ps[:, 5, NE + 1:NE + 2], ones[0:NE, :], r_ov[0:NE, 0:1], start=True, stop=True
               ).then_inc(S("list_sums"), 1)
            pe.wait_ge(S("extra_after"), 1)
            mm(ps[:, 4, 0:NOVF], ones[0:NE, :], r_ind[0:NE, :], start=True, stop=True).then_inc(S("list_sums"), 1)

            def rows_to_cols(n, u):
                pe.wait_ge(S(f"rows_{u}"), rows_count(n, u))
                if not (isinstance(n, int) and n < 1):
                    pe.wait_ge(S("xg_cols"), n)
                pe.sem_inc(S("pe_passed"), 1)
                for k in range(KD):
                    cols = xg[0:BLK, u, :].rearrange("p (m k) -> p k m", k=KD)[:, k, :]
                    last = turn(ps[:, 0, BLK * k:BLK * k + BLK], cols, ident[0:BLK, 0:BLK])
                last.then_inc(S("rows_turned"), 1)

            def rows_count(n, u):
                return 16 * (n // 2 + 1) if isinstance(n, int) else 16 + (n - u) * 8

            def gate_up(n, u):
                pe.wait_ge(S("xg_cols"), n + 1)
                if not (isinstance(n, int) and n < 2):
                    pe.wait_ge(S("hidden"), n - 1)
                for e, wv in enumerate((wgv[u], wuv[u])):
                    pe.wait_ge(S(f"{('w_gate_exp', 'w_up_exp')[e]}_{u}"), rows_count(n, u))
                    for k in range(KD):
                        last = mm(ps[0:BLK, 1 + 2 * u + e, :], xgT[:, u, k, :], wv[:, k, :], start=k == 0, stop=k == KD - 1)
                last.then_inc(S("gate_up"), 1)

            def turn_hidden(n, u):
                pe.wait_ge(S("hidden"), n + 1)
                pe.sem_inc(S("pe_passed"), 1)
                cols = m_hr[0:BLK, u, :].rearrange("p (m j) -> p j m", j=FJ)
                for j in range(FJ):
                    last = turn(ps[:, 7, FJ * BLK * u + BLK * j:FJ * BLK * u + BLK * j + BLK], cols[:, j, :],
                                ident[0:BLK, 0:BLK])
                last.then_inc(S("hidden_turned"), 1)

            def down(n, u):
                pe.wait_ge(S("hidden_cols"), n + 1)
                pe.wait_ge(S(f"w_down_exp_{u}"), rows_count(n, u))
                if not (isinstance(n, int) and n < 1):
                    pe.wait_ge(S("y_act"), n)
                    pe.wait_ge(S("y_dve"), n)
                for hf in range(2):
                    for j in range(FJ):
                        last = mm(ps[0:BLK, 5 + hf, :], m_h[:, u, j, :], wdv[u][:, j, 512 * hf:512 * hf + 512],
                                  start=j == 0, stop=j == FJ - 1)
                last.then_inc(S("down"), 1)

            rows_to_cols(0, 0)
            gate_up(0, 0)
            rows_to_cols(1, 1)
            turn_hidden(0, 0)
            gate_up(1, 1)
            rows_to_cols(2, 0)
            down(0, 0)
            with pe.Fori(1, NE // 2 - 1) as it:
                for u in range(2):
                    turn_hidden(2 * it + u - 1, 1 - u)
                    gate_up(2 * it + u, u)
                    rows_to_cols(2 * it + u + 1, 1 - u)
                    down(2 * it + u - 1, 1 - u)
            turn_hidden(NE - 3, 1)
            gate_up(NE - 2, 0)
            rows_to_cols(NE - 1, 1)
            down(NE - 3, 1)
            turn_hidden(NE - 2, 0)
            gate_up(NE - 1, 1)
            down(NE - 2, 0)
            turn_hidden(NE - 1, 1)
            down(NE - 1, 1)
            pe.sem_inc(S("extra_products"), 4)
            novf = pe.value_load(tab[0:1, NOVF:NOVF + 1], min_val=0, max_val=NOVF)
            with pe.Fori(0, NOVF) as i:
                with pe.If(i < novf):
                    pe.wait_ge(S("extra_loaded"), (i + 1) * 64)
                    pe.sem_inc(S("pe_passed"), 1)
                    for k in range(KD):
                        cols = xg[0:BLK, 0, :].rearrange("p (m k) -> p k m", k=KD)[:, k, :]
                        last = turn(ps[:, 0, BLK * k:BLK * k + BLK], cols, ident[0:BLK, 0:BLK])
                    last.then_inc(S("extra_products"), 1)
                    pe.wait_ge(S("extra_dve"), 4 * i + 1)
                    for e, wv in enumerate((wgv[0], wuv[0])):
                        for k in range(KD):
                            last = mm(ps[0:BLK, 1 + e, :], xgT[:, 0, k, :], wv[:, k, :], start=k == 0, stop=k == KD - 1)
                    last.then_inc(S("extra_products"), 1)
                    pe.wait_ge(S("extra_dve"), 4 * i + 2)
                    pe.sem_inc(S("pe_passed"), 1)
                    cols = m_hr[0:BLK, 0, :].rearrange("p (m j) -> p j m", j=FJ)
                    for j in range(FJ):
                        last = turn(ps[:, 7, BLK * j:BLK * j + BLK], cols[:, j, :], ident[0:BLK, 0:BLK])
                    last.then_inc(S("extra_products"), 1)
                    pe.wait_ge(S("extra_dve"), 4 * i + 3)
                    for hf in range(2):
                        for j in range(FJ):
                            last = mm(ps[0:BLK, 5 + hf, :], m_h[:, 0, j, :], wdv[0][:, j, 512 * hf:512 * hf + 512],
                                      start=j == 0, stop=j == FJ - 1)
                    last.then_inc(S("extra_products"), 1)
                with pe.Else():
                    pe.nop()
                pe.nop()

        @block.scalar
        def _(act):
            fn = nc.scalar.activation

            def load(dst, src, signal):
                act.dma_start(dst, src).then_inc(S(signal), 16)

            load(w1c[:, :], a["norm1_w"][0].rearrange("(p k) -> p k", k=KD), "small_loaded")
            for j, name in enumerate(("q_norm_w", "k_norm_w", "hg_norm_w")):
                for e in range(2):
                    load(qkg[64 * e:64 * e + 64, j:j + 1], a[name][0].rearrange("(p o) -> p o", o=1), "small_loaded")
            load(bias8[:, :], a["sb_bias"].to_broadcast([P, H]), "small_loaded")

            act.wait_ge(S("constants"), 1)
            act.wait_ge(S("x_loaded"), 16 * NT)
            for i, r in enumerate(ROWS):
                if i:
                    act.wait_ge(S("row_squares"), i)
                fn(kout_flat[0:r, 0:D], xt[0:r, i, :], ACT.Square, accum_out=ss[0:r, i:i + 1]).then_inc(S("row_squares"), 1)
            act.wait_ge(S("row_inverses"), 1)
            fn(rstd[:, 0:NT], rstd[:, 0:NT], ACT.Sqrt).then_inc(S("row_scales"), 1)

            def projection_out(n):
                c, j = JOBS[n]
                kind, dst = CHUNKS[c]
                bank = 4 + 2 * (n % 2)
                act.wait_ge(S("projected"), n + 1)
                if kind == "cols":
                    fn(each(dst[:, j, :], 2), ps[:, bank:bank + 2, 0:TH], ACT.Copy).then_inc(S("projection_out"), 1)
                else:
                    r = ROWS[j]
                    fn(dst[0:r, j, :], ps[0:r, bank, :], ACT.Copy).then_inc(S("projection_out"), 1)

            def head_roots(m):
                for c in range(CT):
                    act.wait_ge(S("head_sums"), 4 * m + c + 1)
                    if m == 1:
                        act.wait_ge(S("heads_normed"), c + 1)
                    fn(each(rs[m][:, c, :], 2), ps[:, 2 * (c % 2):2 * (c % 2) + 2, 0:TH], ACT.Sqrt,
                       scale=1.0 / DH, bias=eps[:, :]).then_inc(S("head_roots"), 1)

            for n in range(8):
                projection_out(n)
            head_roots(0)
            for n in range(8, QKV):
                projection_out(n)
            head_roots(1)

            n = QKV
            for h in range(H):
                act.wait_ge(S("attn_scores"), h + 1)
                if h:
                    act.wait_ge(S("attn_losses"), h)
                    act.wait_ge(S("attn_weights"), h)
                fn(a_z, ps_attn, ACT.Identity, scale=SCALE, bias=bias8[:, h:h + 1]).then_inc(S("attn_z"), 1)
                act.wait_ge(S("attn_z"), h + 1)
                fn(a_e, a_z, ACT.Abs).then_inc(S("attn_softplus"), 1)
                act.wait_ge(S("attn_softplus"), 3 * h + 1)
                fn(a_e, a_e, ACT.Exp, scale=-1.0).then_inc(S("attn_softplus"), 1)
                act.wait_ge(S("attn_softplus"), 3 * h + 2)
                fn(a_ln, a_e, ACT.Ln, bias=1.0).then_inc(S("attn_softplus"), 1)
                for _ in range(2 if h in (0, 4) else 1):
                    if n < len(JOBS):
                        projection_out(n)
                        n += 1
                act.wait_ge(S("attn_args"), h + 1)
                if h < 2:
                    act.wait_ge(S("kv_stored"), 64)
                else:
                    act.wait_ge(S("attn_values"), h - 1)
                fn(a_A[:, h % 2, :], a_z, ACT.Exp).then_inc(S("attn_weights"), 1)
                if n < len(JOBS):
                    projection_out(n)
                    n += 1

            act.wait_ge(S("attn_values"), H)
            load(lbr[:, :, :], a["lb_logits"].rearrange("(o r) c -> o r c", o=1).to_broadcast([P, 2, W]), "lb_loaded")
            act.wait_ge(S("lb_shifted"), 1)
            fn(lbr[:, :, :], lbr[:, :, :], ACT.Exp).then_inc(S("lb_exp"), 1)
            act.wait_ge(S("projection_out"), len(JOBS))
            for i, r in enumerate(ROWS):
                fn(ftok[0:r, i, :], ftok[0:r, i, :], ACT.Exp, scale=-1.0).then_inc(S("f_exp"), 1)
            for i, r in enumerate(ROWS):
                act.wait_ge(S("f"), i + 1)
                fn(ftok[0:r, i, :], ftok[0:r, i, :], ACT.Ln).then_inc(S("log_f"), 1)
                act.wait_ge(S("decay_sums"), i + 1)
                fn(g_e[:, 0:CT * r], ps[:, 0, 0:CT * r], ACT.Exp).then_inc(S("decays"), 1)
                fn(g_en[:, 0:CT * r], ps[:, 0, 0:CT * r], ACT.Exp, scale=-1.0).then_inc(S("decays"), 1)
                fn(g_e2[0:r, :], ps[0:r, 1, :], ACT.Exp).then_inc(S("decays"), 1)
            act.wait_ge(S("decayed"), 3 * NT)
            fn(flat(hqT), flat(gT), ACT.Sigmoid).then_inc(S("g_sigmoid"), 1)
            head_roots(2)

            act.wait_ge(S("new_rows"), 1)
            fn(n_e[0:TS, :], n_z[0:TS, :], ACT.Abs).then_inc(S("new_act"), 1)
            act.wait_ge(S("new_act"), 1)
            fn(n_e[0:TS, :], n_e[0:TS, :], ACT.Exp, scale=-1.0).then_inc(S("new_act"), 1)
            act.wait_ge(S("new_act"), 2)
            fn(n_s[0:TS, :], n_e[0:TS, :], ACT.Ln, bias=1.0).then_inc(S("new_act"), 1)
            act.wait_ge(S("new_rows"), 3)
            fn(n_e[0:TS, :], n_z[0:TS, :], ACT.Exp).then_inc(S("new_act"), 1)

            def turned_out(b, g):
                n = b * NGRP + g
                for j in range(2):
                    act.wait_ge(S("page_turned"), 4 * n + j + 1)
                    if not isinstance(n, int) or n >= 2:
                        act.wait_ge(S("page_scores"), n - 1)
                    fn(d_kt[:, g % 2, j, :], ps[:, j, :], ACT.Copy).then_inc(S("kT_act"), 1)

            def softplus_parts(b, g):
                n = b * NGRP + g
                act.wait_ge(S("page_z"), n + 1)
                fn(d_e[:, g % 2, :], d_z[:, g % 2, :], ACT.Abs).then_inc(S("page_softplus"), 1)
                act.wait_ge(S("page_softplus"), 3 * n + 1)
                fn(d_e[:, g % 2, :], d_e[:, g % 2, :], ACT.Exp, scale=-1.0).then_inc(S("page_softplus"), 1)
                act.wait_ge(S("page_softplus"), 3 * n + 2)
                fn(d_ln[:, g % 2, :], d_e[:, g % 2, :], ACT.Ln, bias=1.0).then_inc(S("page_softplus"), 1)

            def page_weights(b, g):
                n = b * NGRP + g
                act.wait_ge(S("page_args"), n + 1)
                if not isinstance(n, int) or n >= 4:
                    act.wait_ge(S("values_summed"), n - 3)
                fn(d_A[:, g % 4, :], d_z[:, g % 2, :], ACT.Exp).then_inc(S("page_weights"), 1)

            def before(b, g, lag):
                return (b, g - lag) if g >= lag else (b - 1, g - lag + NGRP)

            def decode_steps(b):
                for g in range(NGRP):
                    turned_out(b, g)
                    for lag, part in ((2, page_weights), (1, softplus_parts)):
                        if g >= lag or not isinstance(b, int):
                            part(*before(b, g, lag))

            decode_steps(0)
            with act.Fori(1, NB) as b:
                decode_steps(b)
            page_weights(NB - 1, NGRP - 2)
            softplus_parts(NB - 1, NGRP - 1)
            page_weights(NB - 1, NGRP - 1)

            for m in range(KD):
                for e, dst in enumerate((m_sa, m_sb)):
                    act.wait_ge(S("branch_products"), 4 * m + e + 1)
                    if m >= 2:
                        act.wait_ge(S("merged"), m - 1)
                    elif m == 0:
                        act.wait_ge(S("decoded"), NB)
                    fn(each(dst[:, m % 2, :], 2), ps[:, 2 * e:2 * e + 2, 0:TH], ACT.Sigmoid).then_inc(S("gates_read"), 1)
            act.wait_ge(S("branch_products"), 4 * KD)
            load(w2r[:, :], a["norm2_w"].to_broadcast([P, D]), "w2_loaded")
            act.wait_ge(S("merged"), KD)
            load(wr[:, :, 0:NG], a["w_group_router"][0].rearrange("(p k) n -> p k n", k=KD), "w_router")
            load(wr[:, :, NG:NG + NE], a["w_expert_router"][0].rearrange("(p k) n -> p k n", k=KD), "w_router")
            act.wait_ge(S("route_zero"), 1)
            load(r_b36[:, 0:NG], a["b_group_router"].to_broadcast([P, NG]), "b_router")
            load(r_b36[:, NG:NG + NE], a["b_expert_router"].to_broadcast([P, NE]), "b_router")
            for i, r in enumerate(ROWS):
                act.wait_ge(S("x2"), i + 1)
                if i:
                    act.wait_ge(S("row_squares"), NT + i)
                fn(sqj[0:r, :], x2[0:r, i, :], ACT.Square, accum_out=ss2[0:r, i:i + 1]).then_inc(S("row_squares"), 1)
                act.wait_ge(S("row_inverses"), 2 + i)
                fn(rstd2[0:r, i:i + 1], rstd2[0:r, i:i + 1], ACT.Sqrt).then_inc(S("row_scales"), 1)
            for i, r in enumerate(ROWS):
                act.wait_ge(S("group_max"), i + 1)
                fn(r_ge[0:r, :], r_gl[0:r, 0:NG], ACT.Exp, bias=r_ng[0:r, :], accum_out=r_gs[0:r, :]
                   ).then_inc(S("group_sum"), 1)
                act.wait_ge(S("expert_gap"), i + 1)
                fn(r_e2[0:r, :], r_gap[0:r, :], ACT.Exp).then_inc(S("expert_ratio"), 1)

            def slot_count(n, u):
                return 16 * (n // 2 + 1) if isinstance(n, int) else 16 + (n - u) * 8

            def silu(n, u):
                act.wait_ge(S("gate_up"), n + 1)
                if not (isinstance(n, int) and n < 2):
                    act.wait_ge(S("hidden"), n - 1)
                fn(m_s[0:BLK, u, :], ps[0:BLK, 1 + 2 * u, :], ACT.Silu).then_inc(S("silu"), 1)

            def y_out(n, u):
                act.wait_ge(S("down"), n + 1)
                if not (isinstance(n, int) and n < 2):
                    act.wait_ge(S(f"out_stored_{u}"), slot_count(n, u) - 16)
                fn(m_y[0:BLK, u, 0:512], ps[0:BLK, 5, :], ACT.Copy).then_inc(S("y_act"), 1)
                act.wait_ge(S("y_act"), n + 1)
                act.wait_ge(S("y_dve"), n + 1)
                act.dma_start(yg_dram[bass.ds(n * BLK, BLK), :], m_y[0:BLK, u, :]).then_inc(S(f"out_stored_{u}"), 16)

            silu(0, 0)
            silu(1, 1)
            y_out(0, 0)
            with act.Fori(1, NE // 2) as it:
                for u in range(2):
                    silu(2 * it + u, u)
                    y_out(2 * it + u - 1, 1 - u)
            y_out(NE - 1, 1)
            for u in range(2):
                act.wait_ge(S(f"out_stored_{u}"), 8 * NE)
            act.sem_inc(S("extra_stored"), 16)
            novf = act.value_load(tab[0:1, NOVF:NOVF + 1], min_val=0, max_val=NOVF)
            with act.Fori(0, NOVF) as i:
                with act.If(i < novf):
                    act.wait_ge(S("extra_products"), extra_stage(i, 2))
                    fn(m_s[0:BLK, 0, :], ps[0:BLK, 1, :], ACT.Silu).then_inc(S("extra_act"), 1)
                    act.wait_ge(S("extra_products"), extra_stage(i, 4))
                    act.wait_ge(S("extra_stored"), i * 16 + 16)
                    fn(m_y[0:BLK, 0, 0:512], ps[0:BLK, 5, :], ACT.Copy).then_inc(S("extra_act"), 1)
                    act.wait_ge(S("extra_act"), 2 * i + 2)
                    act.wait_ge(S("extra_dve"), 4 * i + 4)
                    act.dma_start(yg_dram[bass.ds((NE + i) * BLK, BLK), :], m_y[0:BLK, 0, :]).then_inc(S("extra_stored"), 16)
                with act.Else():
                    act.nop()
                act.nop()

        @block.vector
        def _(dve):
            v = nc.vector
            chain = Chain(dve, S("vector_chain"))
            stt = v.scalar_tensor_tensor

            def over(m, r, n, k):
                return m[0:r, 0:k].unsqueeze(1).to_broadcast([r, n, k])

            dve.wait_ge(S("row_squares"), NT)
            chain(v.tensor_scalar(rstd[:, 0:NT], ss[:, 0:NT], 1.0 / D, EPS, ALU.mult, ALU.add))
            chain.wait()
            v.reciprocal(rstd[:, 0:NT], rstd[:, 0:NT]).then_inc(S("row_inverses"), 1)
            dve.wait_ge(S("row_scales"), 1)
            for i, r in enumerate(ROWS):
                v.tensor_scalar(xt[0:r, i, :], xt[0:r, i, :], rstd[0:r, i:i + 1], None, ALU.mult).then_inc(S("x_normed"), 1)
            dve.wait_ge(S("small_loaded"), 128)
            chain(v.tensor_copy(bias32[:, :].rearrange("p (h q) -> p h q", q=TQ), bias8[:, :].unsqueeze(2).to_broadcast([P, H, TQ])))
            for i, r in enumerate(ROWS):
                for kk in range(2):
                    n = 2 * i + kk
                    dve.wait_ge(S("x_turned"), n + 1)
                    v.tensor_tensor(hT[:, 4 * kk:4 * kk + 4, P * i:P * i + r], each(ps[:, 4 + n % 4, :], 4)[:, :, 0:r],
                                    w1c[:, 4 * kk:4 * kk + 4].unsqueeze(2).to_broadcast([P, 4, r]), ALU.mult
                                    ).then_inc(S("hT"), 1)

            def head_norm(m, xT):
                if m:
                    dve.wait_ge(S("head_sums"), 4 * m)
                v.tensor_tensor(flat(sq[m]), flat(xT), flat(xT), ALU.mult).then_inc(S("squares"), 1)
                for c in range(CT):
                    dve.wait_ge(S("head_roots"), 4 * m + c + 1)
                    chain(v.reciprocal(rs[m][:, c, :], rs[m][:, c, :]))
                    chain.wait()
                    stt(out=xT[:, c, :], in0=xT[:, c, :], scalar=qkg[:, m:m + 1], in1=rs[m][:, c, :],
                        op0=ALU.mult, op1=ALU.mult).then_inc(S("heads_normed"), 1)

            dve.wait_ge(S("projection_out"), 4)
            head_norm(0, qT)
            dve.wait_ge(S("projection_out"), 8)
            head_norm(1, kT)
            for i, r in enumerate(ROWS):
                dve.wait_ge(S("k_turned_rows"), i + 1)
                v.tensor_copy(kout[0:r, i, :], ps[0:r, i % 4, :]).then_inc(S("k_rows"), 1)

            def softplus(z, e, ln, t, L):
                chain(v.tensor_scalar(t, e, 1.0, -1.0, ALU.add, ALU.add))
                chain.wait()
                chain(v.tensor_tensor(t, e, t, ALU.subtract))

            def attn_pair_out(p):
                dve.wait_ge(S("attn_values"), 2 * p + 2)
                v.tensor_copy(osbT[:, p, 0:SEQ], ps[:, 3, :]).then_inc(S("attn_out"), 1)

            for h in range(H):
                dve.wait_ge(S("attn_softplus"), 3 * h + 2)
                softplus(a_z, a_e, a_ln, a_t, a_L)
                dve.wait_ge(S("attn_softplus"), 3 * h + 3)
                chain(stt(out=a_L, in0=a_z, scalar=0.0, in1=a_ln, op0=ALU.max, op1=ALU.add))
                chain.wait()
                chain(v.tensor_tensor(a_L, a_L, a_t, ALU.add))
                chain.wait()
                chain(v.tensor_tensor(diag3(a_L_off), diag3(a_L_off), over(mask_lt, P, 3, P), ALU.mult))
                v.tensor_tensor(a_L[:, 896:1024], a_L[:, 896:1024], mask_lt[:, :], ALU.mult).then_inc(S("attn_losses"), 1)
                dve.wait_ge(S("attn_remains"), h + 1)
                chain(v.tensor_tensor(a_z, a_z, ps_attn, ALU.subtract))
                chain.wait()
                chain(v.tensor_tensor(diag3(a_z_off), diag3(a_z_off), over(neg_lt, P, 3, P), ALU.add))
                v.tensor_tensor(a_z[:, 896:1024], a_z[:, 896:1024], neg_lt[:, :], ALU.add).then_inc(S("attn_args"), 1)
                if h % 2 == 0 and h:
                    attn_pair_out(h // 2 - 1)
            attn_pair_out(CT - 1)

            dve.wait_ge(S("lb_loaded"), 16)
            chain(v.tensor_tensor(oml, lbr[:, 0, :], lbr[:, 1, :], ALU.max))
            chain.wait()
            chain(v.tensor_tensor(lbr[:, 0, :], lbr[:, 0, :], oml, ALU.subtract))
            v.tensor_tensor(lbr[:, 1, :], lbr[:, 1, :], oml, ALU.subtract).then_inc(S("lb_shifted"), 1)
            dve.wait_ge(S("lb_exp"), 1)
            chain(v.tensor_tensor(oml, lbr[:, 0, :], lbr[:, 1, :], ALU.add))
            chain.wait()
            chain(v.reciprocal(oml, oml))
            chain.wait()
            chain(v.tensor_tensor(lb, lbr[:, 0, :], oml, ALU.mult))
            chain.wait()
            chain(v.tensor_scalar(oml, lb, -1.0, 1.0, ALU.mult, ALU.add))
            dve.wait_ge(S("states_zero"), 1)
            for b in range(NB):
                last = v.tensor_scalar(ib[0:TS, b, :], itok[0:TS, 4, :], in_b[:, b:b + 1], None, ALU.mult)
            last.then_inc(S("ib"), 1)

            def forget(i):
                r = ROWS[i]
                f = ftok[0:r, i, :]
                dve.wait_ge(S("f_exp"), i + 1)
                chain.wait()
                chain(v.tensor_scalar(f, f, 1.0, None, ALU.add))
                chain.wait()
                chain(v.reciprocal(f, f))
                chain.wait()
                chain(v.tensor_tensor(f, f, oml[0:r, :], ALU.mult))
                chain.wait()
                chain(v.tensor_tensor(f, f, lb[0:r, :], ALU.add))
                chain.wait()
                if i:
                    dve.wait_ge(S("decay_sums"), i)
                    dve.wait_ge(S("decayed"), 3 * i)
                v.tensor_scalar(ktok[0:r, :], f, -1.0, 1.0, ALU.mult, ALU.add).then_inc(S("f"), 1)

            def state_update(dst, src, bank, col):
                for c in range(CT):
                    for e in range(2):
                        hs = slice(64 * e, 64 * e + 64)
                        last = stt(out=dst[hs, c, hs], in0=src[hs, c, hs], scalar=g_e[hs, col(c):col(c) + 1],
                                   in1=ps[hs, bank, P * c + 64 * e:P * c + 64 * e + 64], op0=ALU.mult, op1=ALU.add)
                return last

            for i, r in enumerate(ROWS):
                forget(i)
                dve.wait_ge(S("decays"), 3 * i + 3)
                if i:
                    dve.wait_ge(S("hg_out"), i)
                cols = slice(P * i, P * i + r)
                v.tensor_tensor(qd[:, :, 0:r], hqT[:, :, cols], each(g_e[:, 0:CT * r], CT), ALU.mult).then_inc(S("decayed"), 1)
                v.tensor_tensor(kd[:, :, 0:r], each(ps[:, 2, 0:CT * r], CT), each(g_en[:, 0:CT * r], CT), ALU.mult
                                ).then_inc(S("decayed"), 1)
                dve.wait_ge(S("f"), i + 1)
                v.tensor_tensor(kdec[0:r, :], ktok[0:r, :], g_e2[0:r, :], ALU.mult).then_inc(S("decayed"), 1)
                dve.wait_ge(S("hg_scores"), i + 1)
                for e in range(2):
                    v.tensor_tensor(scm[0:r, 4 * e:4 * e + 4, 0:r], each(ps[0:r, 3 + e, 0:CT * r], CT),
                                    over(chk_le if i < 4 else sq_le, r, CT, r), ALU.mult).then_inc(S("hg_masked"), 1)
                if i < 4:
                    for k in range(4):
                        x = 4 * i + k
                        dve.wait_ge(S("chunk_kv"), x + 1)
                        if x:
                            dve.wait_ge(S("chunk_states"), x)
                        state_update(state[:, (x + 1) % 8], state[:, x % 8], KV_BANK[k],
                                     lambda c: P * c + CHUNK * k + CHUNK - 1).then_inc(S("chunk_states"), 1)
                dve.wait_ge(S("hg_out"), i + 1)
                v.tensor_copy(ybT[:, :, cols], each(ps[:, 1, 0:CT * r], CT)).then_inc(S("o_read"), 1) if i else (
                    dve.wait_ge(S("rows_zeroed"), 48),
                    v.tensor_copy(ybT[:, :, cols], each(ps[:, 1, 0:CT * r], CT)).then_inc(S("o_read"), 1))
            for b in range(NB):
                dve.wait_ge(S("sample_kv"), b + 1)
                state_update(state0[:, b], state0[:, b], KV_BANK[b % 4], lambda c: TS * c + TQ * b + TQ - 1
                             ).then_inc(S("sample_states"), 1)
            dve.wait_ge(S("o_read"), NT)
            head_norm(2, ybT)
            dve.wait_ge(S("g_sigmoid"), 1)
            chain(v.tensor_tensor(flat(gT), flat(gT), flat(hqT), ALU.mult))
            chain.wait()
            dve.wait_ge(S("heads_normed"), 3 * CT)
            v.tensor_tensor(flat(ybT), flat(ybT), flat(gT), ALU.mult).then_inc(S("yb"), 1)

            dve.wait_ge(S("states_stored"), 16 * (2 + 2 * NB))
            chain(v.memset(flat(qblk), 0.0))
            chain(v.memset(flat(carry0), 0.0))
            chain.wait()
            for e in range(2):
                hs = slice(64 * e, 64 * e + 64)
                for c in range(CT):
                    dst = qblk[hs, :, :].rearrange("p b (c e q) -> p c e b q", c=CT, e=2)[:, c, e]
                    last = v.tensor_copy(dst, qT[hs, c, SEQ:T].rearrange("p (b q) -> p b q", b=NB))
            last.then_inc(S("q_blocks"), 1)
            dve.wait_ge(S("new_products"), 1)
            for c in range(CT):
                z4 = n_z[0:TS, 64 * c:64 * c + 64].rearrange("p (b x) -> p b x", b=NB)
                last = stt(out=z4, in0=ps[0:TS, 4, 64 * c:64 * c + 64].rearrange("p (b x) -> p b x", b=NB), scalar=SCALE,
                           in1=bias32[0:TS, 8 * c:8 * c + 8].unsqueeze(1).to_broadcast([TS, NB, 8]),
                           op0=ALU.mult, op1=ALU.add)
            last.then_inc(S("new_rows"), 1)
            dve.wait_ge(S("new_act"), 3)
            softplus(None, n_e[0:TS, :], None, n_t[0:TS, :], None)
            dve.wait_ge(S("new_rows"), 1)
            chain(stt(out=n_L[0:TS, :], in0=n_z[0:TS, :], scalar=0.0, in1=n_s[0:TS, :], op0=ALU.max, op1=ALU.add))
            chain.wait()
            chain(v.tensor_tensor(n_L[0:TS, :], n_L[0:TS, :], n_t[0:TS, :], ALU.add))
            chain.wait()
            v.tensor_tensor(n_L[0:TS, :], n_L[0:TS, :], new_m[:, :], ALU.mult).then_inc(S("new_rows"), 1)
            dve.wait_ge(S("new_rows"), 2)
            for b in range(NB):
                chain(v.tensor_copy(carry0[0:TS, b, :].rearrange("p (c x) -> p c x", c=CT),
                                    n_L[0:TS, :].rearrange("p (c b x) -> p b c x", c=CT, b=NB)[:, b]))
            dve.wait_ge(S("new_products"), 2)
            chain(v.tensor_tensor(n_z[0:TS, :], n_z[0:TS, :], ps[0:TS, 5, 0:256], ALU.subtract))
            chain.wait()
            v.tensor_tensor(n_z[0:TS, :], n_z[0:TS, :], new_neg[:, :], ALU.add).then_inc(S("new_rows"), 1)
            dve.wait_ge(S("new_products"), 3)
            v.tensor_copy(flat(obase), ps[:, 6, 0:256]).then_inc(S("new_rows"), 1)
            dve.wait_ge(S("new_rows"), 4)

            def turned_out(b, g):
                n = b * NGRP + g
                for j in range(2, GP):
                    dve.wait_ge(S("page_turned"), 4 * n + j + 1)
                    if not isinstance(n, int) or n >= 2:
                        dve.wait_ge(S("page_scores"), n - 1)
                    v.tensor_copy(d_kt[:, g % 2, j, :], ps[:, j, :]).then_inc(S("kT_dve"), 1)

            def values_out(b):
                dve.wait_ge(S("values_summed"), (b + 1) * NGRP)
                v.tensor_copy(d_o[0:32, :], ps[0:32, 6, :]).then_inc(S("values_out"), 1)

            def losses(b, g, sums_of=None):
                n = b * NGRP + g
                z, e, t, L = (x[:, g % 2, :] for x in (d_z, d_e, d_t, d_L))
                dve.wait_ge(S("page_scores"), n + 1)
                if not isinstance(n, int) or n >= 2:
                    dve.wait_ge(S("page_weights"), n - 1)
                stt(out=each(z, GP), in0=each(ps[:, 4 + g % 2, 0:128], GP), scalar=SCALE,
                    in1=bias32[:, :].unsqueeze(1).to_broadcast([P, GP, 32]), op0=ALU.mult, op1=ALU.add
                    ).then_inc(S("page_z"), 1)
                if sums_of is not None:
                    values_out(sums_of)
                if g == 0:
                    chain(v.tensor_copy(d_R[:, 0, 0:32], carry0[:, bass.ds(b, 1), :].rearrange("p o c -> p (o c)")))
                dve.wait_ge(S("page_softplus"), 3 * n + 2)
                softplus(None, e, None, t, None)
                dve.wait_ge(S("page_softplus"), 3 * n + 3)
                chain(stt(out=L, in0=z, scalar=0.0, in1=d_ln[:, g % 2, :], op0=ALU.max, op1=ALU.add))
                chain.wait()
                chain(v.tensor_tensor(L, L, t, ALU.add))
                chain.wait()
                R = d_R[:, g % 4, :]
                for j in range(GP - 1):
                    add = v.tensor_tensor(R[:, 32 * j + 32:32 * j + 64], R[:, 32 * j:32 * j + 32], L[:, 32 * j:32 * j + 32],
                                          ALU.add)
                    if j < GP - 2:
                        chain(add)
                        chain.wait()
                add.then_inc(S("page_sums"), 1)
                dve.wait_ge(S("page_sums"), n + 1)
                if g < NGRP - 1:
                    chain(v.tensor_tensor(d_R[:, (g + 1) % 4, 0:32], R[:, 96:128], L[:, 96:128], ALU.add))

            def args(b, g):
                n = b * NGRP + g
                dve.wait_ge(S("page_remains"), n + 1)
                v.tensor_tensor(d_z[:, g % 2, :], d_z[:, g % 2, :], ps[:, 4 + g % 2, 128:256], ALU.subtract
                                ).then_inc(S("page_args"), 1)

            def decoded(b):
                dve.wait_ge(S("values_turned"), b + 1)
                for e in range(2):
                    hs = slice(64 * e, 64 * e + 64)
                    got = ps[hs, 7, 4 * e:4 * e + 160].rearrange("p (c x) -> p c x", c=CT)[:, :, 0:TQ]
                    new = obase[hs, :, :].rearrange("p c (b e q) -> p e c b q", b=NB, e=2)[:, e, :, bass.ds(b, 1), :]
                    out = osbT[hs, :, SEQ:T].rearrange("p c (b q) -> p c b q", b=NB)[:, :, bass.ds(b, 1), :]
                    last = v.tensor_tensor(out, got.unsqueeze(2), new, ALU.add)
                last.then_inc(S("decoded"), 1)

            def before(b, g, lag):
                return (b, g - lag) if g >= lag else (b - 1, g - lag + NGRP)

            def decode_steps(b):
                chain.base, chain.n = chain_base(b), 0
                for g in range(NGRP):
                    turned_out(b, g)
                    if g >= 2 or not isinstance(b, int):
                        args(*before(b, g, 2))
                    if g >= 1 or not isinstance(b, int):
                        losses(*before(b, g, 1), sums_of=b - 1 if g == 2 and not isinstance(b, int) else None)
                    if g == 4 and not isinstance(b, int):
                        decoded(b - 1)
                per_loop.append(chain.n)

            per_loop = []
            chain_base = lambda b: chain.n + chain.base
            decode_steps(0)
            start = chain.base + chain.n
            steady = per_loop[0] + LOSS_STEPS
            chain_base = lambda b: start + (b - 1) * steady
            with dve.Fori(1, NB) as b:
                decode_steps(b)
            assert per_loop[1] == steady, per_loop
            chain.base, chain.n = start + (NB - 1) * steady, 0
            args(NB - 1, NGRP - 2)
            losses(NB - 1, NGRP - 1)
            args(NB - 1, NGRP - 1)
            values_out(NB - 1)
            decoded(NB - 1)

            for m in range(KD):
                dve.wait_ge(S("branch_products"), 4 * m + 3)
                dve.wait_ge(S("gates_read"), 2 * m + 2)
                v.tensor_tensor(each(mrg[:, m, :], 2), each(m_sa[:, m % 2, :], 2), ps[:, 4:6, 0:TH], ALU.mult
                                ).then_inc(S("branches_read"), 1)
                dve.wait_ge(S("branch_products"), 4 * m + 4)
                v.tensor_tensor(each(m_sb[:, m % 2, :], 2), each(m_sb[:, m % 2, :], 2), ps[:, 6:8, 0:TH], ALU.mult
                                ).then_inc(S("branches_read"), 1)
                dve.wait_ge(S("branches_read"), 2 * m + 2)
                v.tensor_tensor(mrg[:, m, :], mrg[:, m, :], m_sb[:, m % 2, :], ALU.add).then_inc(S("merged"), 1)
            dve.wait_ge(S("merged"), KD)
            v.memset(route, 0.0).then_inc(S("route_zero"), 1)
            dve.wait_ge(S("x_again"), 16 * NT)
            for i, r in enumerate(ROWS):
                dve.wait_ge(S("mixed"), i + 1)
                v.tensor_tensor(each(x2[0:r, i, :], 2), each(x2[0:r, i, :], 2), ps[0:r, 2 * (i % 2):2 * (i % 2) + 2, :],
                                ALU.add).then_inc(S("x2"), 1)
                dve.wait_ge(S("row_squares"), NT + i + 1)
                chain(v.tensor_scalar(rstd2[0:r, i:i + 1], ss2[0:r, i:i + 1], 1.0 / D, EPS, ALU.mult, ALU.add))
                chain.wait()
                v.reciprocal(rstd2[0:r, i:i + 1], rstd2[0:r, i:i + 1]).then_inc(S("row_inverses"), 1)
                dve.wait_ge(S("row_scales"), 2 + i)
                dve.wait_ge(S("w2_loaded"), 16)
                dve.wait_ge(S("x2"), i + 1)
                stt(out=h2[0:r, i, :], in0=x2[0:r, i, :], scalar=rstd2[0:r, i:i + 1], in1=w2r[0:r, :],
                    op0=ALU.mult, op1=ALU.mult).then_inc(S("h2"), 1)
            dve.wait_ge(S("b_router"), 32)
            dve.wait_ge(S("counters"), 2)
            for i, r in enumerate(ROWS):
                dve.wait_ge(S("h2_turned"), i + 1)
                if i >= 2:
                    dve.wait_ge(S("logits"), i - 1)
                v.tensor_copy(h2T[:, i % 2, :, 0:r], ps_h2[:, :, 0:r]).then_inc(S("h2_cols"), 1)
                dve.wait_ge(S("logits"), i + 1)

                def step(ins):
                    chain(ins)
                    chain.wait()

                g, x = slice(0, r), slice(NG, NG + NE)
                v.tensor_tensor(r_lg[g, :], ps[g, 6, 0:NG + NE], r_b36[g, :], ALU.add).then_inc(S("logits_read"), 1)
                dve.wait_ge(S("logits_read"), i + 1)
                chain(v.memset(r_gl[g, NG:8], -BIG))
                step(v.tensor_copy(r_gl[g, 0:NG], r_lg[g, 0:NG]))
                step(v.max(r_gm[g, :], r_gl[g, :]))
                chain(v.max_index(r_gi[g, :], r_gm[g, :], r_gl[g, :]))
                v.tensor_scalar(r_ng[g, :], r_gm[g, 0:1], -1.0, None, ALU.mult).then_inc(S("group_max"), 1)
                chain.wait()
                step(v.tensor_copy(r_gf[g, :], r_gi[g, 0:1]))
                step(v.tensor_scalar(r_m[g, :], gcol[g, :], r_gf[g, :], None, ALU.is_equal))
                chain(v.tensor_scalar(r_n[g, :], r_m[g, :], BIG, -BIG, ALU.mult, ALU.add))
                step(v.tensor_tensor(r_el[g, :], r_lg[g, x], r_m[g, :], ALU.mult))
                step(v.tensor_tensor(r_el[g, :], r_el[g, :], r_n[g, :], ALU.add))
                step(v.max(r_em[g, :], r_el[g, :]))
                chain(v.max_index(r_ei[g, :], r_em[g, :], r_el[g, :]))
                v.tensor_tensor(r_gap[g, :], r_em[g, 1:2], r_em[g, 0:1], ALU.subtract).then_inc(S("expert_gap"), 1)
                chain.wait()
                step(v.tensor_copy(r_EI[g, 2 * i:2 * i + 2], r_ei[g, 0:2]))
                for k in range(2):
                    chain(v.tensor_scalar(r_Ok[g, 2 * i + k, :], ecol[g, :], r_EI[g, 2 * i + k:2 * i + k + 1], None, ALU.is_equal))
                chain.wait()
                v.tensor_tensor(r_O[g, NE * i:NE * i + NE], r_Ok[g, 2 * i, :], r_Ok[g, 2 * i + 1, :], ALU.add
                                ).then_inc(S("chosen"), 1)
                dve.wait_ge(S("group_sum"), i + 1)
                dve.wait_ge(S("expert_ratio"), i + 1)
                step(v.tensor_scalar(r_t1[g, :], r_e2[g, :], 1.0, None, ALU.add))
                step(v.tensor_tensor(r_t1[g, :], r_t1[g, :], r_gs[g, :], ALU.mult))
                step(v.reciprocal(wts[g, 2 * i:2 * i + 1], r_t1[g, :]))
                step(v.tensor_tensor(wts[g, 2 * i + 1:2 * i + 2], wts[g, 2 * i:2 * i + 1], r_e2[g, :], ALU.mult))
            dve.wait_ge(S("list_sums"), 1)
            step(v.tensor_copy(r_cnt[0:NE, :], ps[0:NE, 6, 0:P]))
            step(v.tensor_scalar(r_ov[0:NE, :], r_cnt[0:NE, :], float(BLK), None, ALU.is_gt))
            for k in range(2, KMAX + 1):
                add = stt(out=r_ov[0:NE, :], in0=r_cnt[0:NE, :], scalar=float(BLK * k), in1=r_ov[0:NE, :],
                          op0=ALU.is_gt, op1=ALU.add)
                if k < KMAX:
                    step(add)
            add.then_inc(S("extra_blocks"), 1)
            chain(v.tensor_copy(r_rank[:, :], ps[:, 7, 0:NE * NT]) if False else v.tensor_copy(r_rank[:, 0:NE * 4], ps[:, 7, 0:NE * 4]))
            chain(v.tensor_copy(r_rank[0:TS, NE * 4:NE * 5], ps[0:TS, 7, NE * 4:NE * 5]))
            dve.wait_ge(S("list_sums"), 2)
            chain(v.tensor_copy(r_base[:, :], ps[:, 5, 0:NE]))
            chain(v.tensor_copy(r_incl[0:NE, :], ps[0:NE, 5, NE:NE + 1]))
            chain(v.tensor_copy(tab[0:1, NOVF:NOVF + 1], ps[0:1, 5, NE + 1:NE + 2]))
            chain.wait()
            v.tensor_scalar(r_ind[0:NE, :], ecol[0:NE, 0:NOVF], r_incl[0:NE, :], None, ALU.is_ge).then_inc(S("extra_after"), 1)
            for i, r in enumerate(ROWS):
                for k in range(2):
                    col = slice(2 * i + k, 2 * i + k + 1)
                    step(v.tensor_tensor_reduce(r_j[0:r, :], r_Ok[0:r, 2 * i + k, :], r_rank[0:r, NE * i:NE * i + NE], 1.0, 0.0,
                                                ALU.mult, ALU.add, r_RK[0:r, col]))
                    step(v.tensor_tensor_reduce(r_j[0:r, :], r_Ok[0:r, 2 * i + k, :], r_base[0:r, :], 1.0, 0.0,
                                                ALU.mult, ALU.add, r_BK[0:r, col]))
            step(v.tensor_tensor(r_BK, r_BK, r_EI, ALU.subtract))
            step(v.tensor_scalar(r_BK, r_BK, float(BLK), float((NE - 1) * BLK), ALU.mult, ALU.add))
            step(stt(out=r_BK, in0=r_RK, scalar=float(BLK), in1=r_BK, op0=ALU.is_ge, op1=ALU.mult))
            step(v.tensor_tensor(r_RK, r_RK, r_BK, ALU.add))
            step(stt(out=r_RK, in0=r_EI, scalar=float(BLK), in1=r_RK, op0=ALU.mult, op1=ALU.add))
            v.tensor_copy(slot_i[:, :], r_RK).then_inc(S("slots"), 1)
            dve.wait_ge(S("list_sums"), 3)
            step(v.tensor_scalar(r_ov[0:1, 0:NOVF], ps[0:1, 4, 0:NOVF], float(NE - 1), None, ALU.min))
            v.tensor_copy(tab[0:1, 0:NOVF], r_ov[0:1, 0:NOVF]).then_inc(S("extra_table"), 1)

            def cols_out(n, u):
                dve.wait_ge(S("rows_turned"), n + 1)
                if not (isinstance(n, int) and n < 2):
                    dve.wait_ge(S("gate_up"), n - 1)
                v.tensor_copy(flat(xgT[:, u]), ps[:, 0, :]).then_inc(S("xg_cols"), 1)

            def hidden(n, u):
                dve.wait_ge(S("silu"), n + 1)
                if not (isinstance(n, int) and n < 2):
                    dve.wait_ge(S("hidden_turned"), n - 1)
                v.tensor_tensor(m_hr[0:BLK, u, :], m_s[0:BLK, u, :], ps[0:BLK, 2 + 2 * u, :], ALU.mult
                                ).then_inc(S("hidden"), 1)

            def hidden_cols(n, u):
                dve.wait_ge(S("hidden_turned"), n + 1)
                v.tensor_copy(flat(m_h[:, u]), ps[:, 7, FJ * BLK * u:FJ * BLK * u + FJ * BLK]).then_inc(S("hidden_cols"), 1)

            def y_out(n, u):
                dve.wait_ge(S("down"), n + 1)
                if not (isinstance(n, int) and n < 2):
                    dve.wait_ge(S(f"out_stored_{u}"), (n - u) * 8)
                v.tensor_copy(m_y[0:BLK, u, 512:D], ps[0:BLK, 6, :]).then_inc(S("y_dve"), 1)

            cols_out(0, 0)
            hidden(0, 0)
            cols_out(1, 1)
            hidden_cols(0, 0)
            hidden(1, 1)
            cols_out(2, 0)
            y_out(0, 0)
            with dve.Fori(1, NE // 2 - 1) as it:
                for u in range(2):
                    hidden_cols(2 * it + u - 1, 1 - u)
                    hidden(2 * it + u, u)
                    cols_out(2 * it + u + 1, 1 - u)
                    y_out(2 * it + u - 1, 1 - u)
            hidden_cols(NE - 3, 1)
            hidden(NE - 2, 0)
            cols_out(NE - 1, 1)
            y_out(NE - 3, 1)
            hidden_cols(NE - 2, 0)
            hidden(NE - 1, 1)
            y_out(NE - 2, 0)
            hidden_cols(NE - 1, 1)
            y_out(NE - 1, 1)
            dve.wait_ge(S("extra_table"), 1)
            novf = dve.value_load(tab[0:1, NOVF:NOVF + 1], min_val=0, max_val=NOVF)
            with dve.Fori(0, NOVF) as i:
                with dve.If(i < novf):
                    dve.wait_ge(S("extra_products"), extra_stage(i, 1))
                    v.tensor_copy(flat(xgT[:, 0]), ps[:, 0, :]).then_inc(S("extra_dve"), 1)
                    dve.wait_ge(S("extra_act"), 2 * i + 1)
                    v.tensor_tensor(m_hr[0:BLK, 0, :], m_s[0:BLK, 0, :], ps[0:BLK, 2, :], ALU.mult).then_inc(S("extra_dve"), 1)
                    dve.wait_ge(S("extra_products"), extra_stage(i, 3))
                    v.tensor_copy(flat(m_h[:, 0]), ps[:, 7, 0:FJ * BLK]).then_inc(S("extra_dve"), 1)
                    dve.wait_ge(S("extra_products"), extra_stage(i, 4))
                    dve.wait_ge(S("extra_stored"), i * 16 + 16)
                    v.tensor_copy(m_y[0:BLK, 0, 512:D], ps[0:BLK, 6, :]).then_inc(S("extra_dve"), 1)
                with dve.Else():
                    dve.nop()
                dve.nop()
            for i, r in enumerate(ROWS):
                dve.wait_ge(S(f"y_gathered_{i % 2}"), 32 * (i // 2 + 1))
                step(stt(out=x2[0:r, i, :], in0=yg[0:r, 2 * (i % 2), :], scalar=wts[0:r, 2 * i:2 * i + 1], in1=x2[0:r, i, :],
                         op0=ALU.mult, op1=ALU.add))
                stt(out=x2[0:r, i, :], in0=yg[0:r, 2 * (i % 2) + 1, :], scalar=wts[0:r, 2 * i + 1:2 * i + 2], in1=x2[0:r, i, :],
                    op0=ALU.mult, op1=ALU.add).then_inc(S("y_rows"), 1)


_INS = ["x_prompt", "x_sample", "cache_k", "cache_v", "page_table", "state_hgrn", "norm1_w", "w_in", "q_norm_w",
        "k_norm_w", "sb_bias", "lb_logits", "hg_norm_w", "w_branch_a", "w_branch_b", "w_out", "norm2_w",
        "w_group_router", "b_group_router", "w_expert_router", "b_expert_router", "w_gate_exp", "w_up_exp",
        "w_down_exp"]
_OUTS = [("y_prompt", (1, SEQ, D)), ("y_sample", (NB, TQ, D)), ("new_k_prompt", (1, 1, SEQ, H, DH)),
         ("new_v_prompt", (1, 1, SEQ, H, DH)), ("new_hgrn_prompt", (1, 1, H, DH, DH)),
         ("new_k_sample", (1, NB, TQ, H, DH)), ("new_v_sample", (1, NB, TQ, H, DH)),
         ("new_hgrn_sample", (1, NB, H, DH, DH))]


def kernel(**inputs):
    import numpy as _np
    import concourse.bacc as _bacc
    from concourse import mybir as _mybir
    from concourse.bass_utils import run_bass_kernel_spmd as _run

    nc = _bacc.Bacc("TRN2", target_bir_lowering=False, num_devices=1)
    arrays, aps = {}, {}
    for name in _INS:
        x = _np.ascontiguousarray(inputs[name])
        arrays[f"in_{name}"] = x
        aps[name] = nc.dram_tensor(f"in_{name}", x.shape, _mybir.dt.from_np(x.dtype), kind="ExternalInput").ap()
    for name, shape in _OUTS:
        aps[name] = nc.dram_tensor(name, shape, F32, kind="ExternalOutput").ap()
    hybrid_step(nc, aps)
    r = _run(nc, [arrays], core_ids=[0])
    return tuple(r.results[0][name] for name, _ in _OUTS)
```

```python
from contextlib import ExitStack

import concourse.bass as bass
from concourse import mybir

F32 = mybir.dt.float32
F32R = mybir.dt.float32r
I32 = mybir.dt.int32
U32 = mybir.dt.uint32
ALU = mybir.AluOpType
ACT = mybir.ActivationFunctionType

P = 128
D = 1024
KD = D // P
SEQ = 512
NB = 8
TQ = 4
TS = NB * TQ
T = SEQ + TS
TH = T // 2
NT = 5
ROWS = [P] * 4 + [TS]
H = 8
DH = 64
CT = H * DH // P
W = H * DH
NPAGES = 32
GP = 4
NGRP = NPAGES // GP
CHUNK = 32
NE = 32
NG = 4
EG = NE // NG
FF = 512
FJ = FF // P
BLK = 64
KMAX = T // BLK
NOVF = 2 * T // BLK
NBLK = NE + NOVF
SCALE = float(DH) ** -0.5
EPS = 1e-6
BIG = 1e30
PARTS = 2 * KD * FF + KD * P
AZ = 1280
SB_OFF = [0, 512, 1024, 896]
SB_LEN = [512, 384, 256, 128]


def first(b):
    return isinstance(b, int) and b == 0


class Chain:

    def __init__(self, eng, sem):
        self.eng, self.sem, self.n, self.base = eng, sem, 0, 0

    def __call__(self, ins):
        ins.then_inc(self.sem, 1)
        self.n += 1

    def wait(self):
        self.eng.wait_ge(self.sem, self.base + self.n)


def hybrid_step(nc, a):
    ctx = ExitStack()
    with ctx:
        def sb(name, shape, dt=F32):
            return ctx.enter_context(nc.sbuf_tensor(name, shape, dt))

        signals = {}

        def S(name):
            if name not in signals:
                signals[name] = ctx.enter_context(nc.semaphore(name))
            return signals[name]

        ps = ctx.enter_context(nc.psum_tensor("ps", [P, 8, 512], F32))
        xg_dram = nc.dram_tensor("expert_rows", [NBLK * BLK, D], F32).ap()
        yg_dram = nc.dram_tensor("expert_outs", [NBLK * BLK, D], F32).ap()

        ident = sb("ident", [P, P])
        ones = sb("ones", [P, P])
        tri_ge = sb("tri_ge", [P, P])
        headones = sb("headones", [P, P])
        mask_lt = sb("mask_lt", [P, P])
        neg_lt = sb("neg_lt", [P, P])
        tri_le = sb("tri_le", [P, P])
        chk_le = sb("chk_le", [P, P])
        chk_gt = sb("chk_gt", [P, P])
        sq_le = sb("sq_le", [TS, TS])
        sq_gt = sb("sq_gt", [TS, TS])
        new_m = sb("new_m", [TS, 256])
        new_neg = sb("new_neg", [TS, 256])
        in_b = sb("in_b", [TS, NB])
        w1c = sb("w1c", [P, KD])
        qkg = sb("qkg", [P, 3])
        bias8 = sb("bias8", [P, H])
        bias32 = sb("bias32", [P, 32])
        fold = sb("fold", [P, BLK])
        eps = sb("eps", [P, 1])
        ss = sb("ss", [P, 8])
        rstd = sb("rstd", [P, 8])
        ss2 = sb("ss2", [P, 8])
        rstd2 = sb("rstd2", [P, 8])

        with ExitStack() as mixers:
            hT, osbT, ybT = (mixers.enter_context(nc.sbuf_tensor(name, [P, k, T], F32))
                             for name, k in (("hT", KD), ("osbT", CT), ("ybT", CT)))
            mixers.enter_context(nc.sbuf_tensor("mixers_rest", [P, PARTS - 2 * KD * T], F32))
        w_hi = sb("w_hi", [P, KD, FF], F32R)
        w_lo = sb("w_lo", [P, KD, FF], F32R)
        xg_parts = sb("xg_parts", [P, KD, P], F32R)
        ARENA = 40960
        arena = sb("arena", [P, ARENA])

        def carve(off, *dims):
            n = 1
            for d in dims:
                n *= d
            assert off + n <= ARENA, (off, dims)
            v = arena[:, off:off + n]
            if len(dims) == 2:
                v = v.rearrange("p (a b) -> p a b", a=dims[0])
            if len(dims) == 3:
                v = v.rearrange("p (a b c) -> p a b c", a=dims[0], b=dims[1])
            return v

        def flat(v):
            return v.rearrange("p a b -> p (a b)")

        wring = carve(0, 3, KD, 512)
        qT = carve(12288, CT, T)
        kT = carve(14464, CT, T)
        vtok = carve(16640, NT, W)
        hqT = carve(19200, CT, T)
        ftok = carve(21376, NT, W)
        itok = carve(23936, NT, W)
        gT = carve(26496, CT, T)
        A0 = 28672
        xt = carve(A0, NT, D)
        kout = carve(A0 + 5120, NT, W)
        sq = [carve(A0 + 7680, CT, T)] * 2 + [carve(A0, CT, T)]
        rs = [carve(A0 + 9856, CT, T)] * 2 + [carve(A0 + 2176, CT, T)]
        a_z = carve(A0, AZ)
        a_e = carve(A0 + 1280, AZ)
        a_ln = carve(A0 + 2560, AZ)
        a_t = carve(A0 + 3840, AZ)
        a_L = carve(A0 + 8960, AZ)
        a_A = carve(A0 + 5120, 2, AZ)

        state = carve(0, 8, CT, P)
        state0 = carve(4096, NB, CT, P)
        ib = carve(8192, NB, W)
        lbr = carve(A0 + 10240, 2, W)
        lb = carve(A0 + 11264, W)
        oml = carve(A0 + 11776, W)
        g0 = A0
        ktok = carve(g0 + 2048, W)
        g_e = carve(g0 + 2560, W)
        g_en = carve(g0 + 3072, W)
        g_e2 = carve(g0 + 3584, W)
        qd = carve(g0 + 4096, CT, P)
        kd = carve(g0 + 4608, CT, P)
        kdec = carve(g0 + 5120, W)
        scm = carve(g0 + 5632, H, P)

        d_kt = carve(0, 2, GP, 512)
        D0 = 4096
        d_z = carve(D0, 2, 128)
        d_e = carve(D0 + 256, 2, 128)
        d_ln = carve(D0 + 512, 2, 128)
        d_t = carve(D0 + 768, 2, 128)
        d_L = carve(D0 + 1024, 2, 128)
        d_R = carve(D0 + 1280, 4, 128)
        d_A = carve(D0 + 1792, 4, 128)
        qblk = carve(D0 + 2304, NB, 32)
        obase = carve(D0 + 2560, CT, 64)
        n_z = carve(D0 + 2816, 256)
        n_e = carve(D0 + 3072, 256)
        n_t = carve(D0 + 3328, 256)
        n_L = carve(D0 + 3584, 256)
        carry0 = carve(D0 + 3840, NB, 32)
        n_s = carve(D0 + 4096, 256)
        d_o = carve(D0 + 4352, 512)
        vring = carve(17664, 4, GP, 512)
        kring = carve(36864, 2, GP, 512)
        pages = carve(36352, NB * NPAGES).bitcast(I32)

        mrg = carve(0, KD, T)
        m_sa = carve(4352, 2, T)
        m_sb = carve(5440, 2, T)
        wab = [carve(9472, CT, D), carve(13568, CT, D)]
        x2 = carve(17664, NT, D)
        gw = [[carve(25856 + 4096 * i + 2048 * e, KD, 256) for e in range(2)] for i in range(2)]
        WO_PARTS = [(22784, 3), (34048, 4), (6528, 1)]
        wo = [arena[:, o + D * k:o + D * k + D] for o, n in WO_PARTS for k in range(n)]
        h2 = carve(12288, NT, D)
        h2T = carve(25856, 2, KD, P)
        w2r = carve(27904, D)
        wr = carve(28928, KD, 36)
        sqj = carve(29216, D)

        M0 = 22784
        xg = carve(M0, 2, D)
        xgT = carve(M0 + 2048, 2, KD, BLK)
        m_s = carve(M0 + 3072, 2, FF)
        m_hr = carve(M0 + 4096, 2, FF)
        m_h = carve(M0 + 5120, 2, FJ, BLK)
        m_y = carve(M0 + 5632, 2, D)
        wgv = [carve(0, KD, FF), carve(12288, KD, FF)]
        wuv = [carve(4096, KD, FF), carve(30464, KD, FF)]
        wdv = [carve(8192, FJ, D), carve(34560, FJ, D)]
        m_g = carve(40192, FF)
        yg = carve(0, 2 * NT, D)

        route = carve(38656, 1536)
        tab = sb("tab", [P, 32], I32)
        slot_i = sb("slot_i", [P, 2 * NT], I32)
        wts = sb("wts", [P, 2 * NT])

        x_tok = [a["x_prompt"][0, P * i:P * i + P, :] for i in range(4)] + [
            a["x_sample"].rearrange("b q d -> (b q) d")]
        w_in = a["w_in"][0].rearrange("(p k) n -> p k n", k=KD)
        w_br = [a[n][0].rearrange("(c p) n -> p c n", p=P) for n in ("w_branch_a", "w_branch_b")]

        CHUNKS = [("cols", qT), ("cols", kT), ("rows", vtok), ("cols", hqT), ("rows", ftok), ("rows", itok),
                  ("cols", gT)]
        JOBS = [(c, j) for c, (kind, _) in enumerate(CHUNKS) for j in range(4 if kind == "cols" else NT)]
        CHUNK_END = [max(n for n, (c, _) in enumerate(JOBS) if c == cc) + 1 for cc in range(len(CHUNKS))]
        QKV = CHUNK_END[2]
        KV_BANK = [5, 6, 7, 0]
        GATE_AT = [7 * 512, 9 * 512]

        def each(v, n):
            return v.rearrange("p (a b) -> p a b", a=n)

        def diag3(off):
            return each(arena[:, off:off + 1536], 3)[:, :, 0:P]

        ps_attn = ps[:, 0:3, :].rearrange("p b c -> p (b c)")[:, 0:AZ]
        ps_h2 = ps[:, 4:6, :].rearrange("p b (k m) -> p (b k) m", k=4)
        kout_flat = kout.rearrange("p a b -> p (a b)")
        a_z_off, a_L_off = A0, A0 + 8960
        LOSS_CHAIN = 7

        taken = [0]

        def small(n):
            o = taken[0]
            taken[0] += n
            assert taken[0] <= 1536
            return route[:, o:o + n]

        gcol_i, ecol_i = small(NE).bitcast(I32), small(NE).bitcast(I32)
        gcol, ecol, r_b36, r_lg = small(NE), small(NE), small(NG + NE), small(NG + NE)
        r_gl, r_gm, r_gi, r_em, r_ei = small(8), small(8), small(8).bitcast(U32), small(8), small(8).bitcast(U32)
        r_ng, r_gf, r_ge, r_gs, r_e2, r_gap, r_t1 = (small(k) for k in (1, 1, NG, 1, 1, 1, 1))
        r_m, r_n, r_el, r_j = small(NE), small(NE), small(NE), small(NE)
        r_O = small(NE * NT)
        r_Ok = small(2 * NT * NE).rearrange("p (a b) -> p a b", a=2 * NT)
        r_rank, r_ov, r_cnt, r_base, r_ind, r_incl = (small(k) for k in (NE * NT, P, P, NE, NOVF, 1))
        r_EI, r_RK, r_BK = small(2 * NT), small(2 * NT), small(2 * NT)

        def extra_stage(i, k):
            return 4 * i + 4 + k

        block = ctx.enter_context(nc.Block())

        @block.sync
        def _(sp):
            for i in range(NT):
                sp.dma_start(xt[0:ROWS[i], i, :], x_tok[i]).then_inc(S(f"x_loaded_{i}"), 16)
            for c in range(len(CHUNKS)):
                if c >= 3:
                    sp.wait_ge(S("projected"), CHUNK_END[c - 3])
                sp.dma_start(wring[:, c % 3], w_in[:, :, 512 * c:512 * c + 512]).then_inc(S(f"w_in_{c % 3}"), 16)
                if c == 5:
                    sp.wait_ge(S("projection_out"), QKV)
                    sp.dma_start(a["new_v_prompt"][0, 0].rearrange("(i p) h d -> p i (h d)", p=P),
                                 vtok[:, 0:4, :]).then_inc(S("rows_stored"), 16)
                    sp.dma_start(a["new_v_sample"][0].rearrange("b q h d -> (b q) (h d)"),
                                 vtok[0:TS, 4, :]).then_inc(S("rows_stored"), 16)
                    sp.wait_ge(S("k_rows"), NT)
                    sp.dma_start(a["new_k_prompt"][0, 0].rearrange("(i p) h d -> p i (h d)", p=P),
                                 kout[:, 0:4, :]).then_inc(S("rows_stored"), 16)
                    sp.dma_start(a["new_k_sample"][0].rearrange("b q h d -> (b q) (h d)"),
                                 kout[0:TS, 4, :]).then_inc(S("rows_stored"), 16)
            sp.wait_ge(S("projected"), len(JOBS))
            sp.wait_ge(S("states_zero"), 1)
            st_in = a["state_hgrn"][0].rearrange("b (c e) k v -> e k b c v", e=2)
            st_out = a["new_hgrn_sample"][0].rearrange("b (c e) k v -> e k b c v", e=2)
            for e in range(2):
                for b in range(NB):
                    sp.dma_start(state0[64 * e:64 * e + 64, b, :, 64 * e:64 * e + 64],
                                 st_in[e, :, b]).then_inc(S("states_loaded"), 16)
            def pages_of(b, g):
                return [sp.value_load(pages[0:1, bass.ds(b * NPAGES + NPAGES - 1 - GP * g - j, 1)],
                                      min_val=0, max_val=a["cache_k"].shape[1] - 1) for j in range(GP)]

            def key_loads(b, g):
                n = b * NGRP + g
                for j, page in enumerate(pages_of(b, g)):
                    if not (isinstance(n, int) and n < 2):
                        sp.wait_ge(S("page_turned"), GP * (n - 2) + j + 1)
                    sp.dma_start(kring[:, g % 2, j, :], a["cache_k"][0, bass.ds(page, 1)].rearrange("a s h d -> (a s) (h d)")
                                 ).then_inc(S(f"cache_k_{g % 2}"), 16)

            def value_loads(b, g):
                n = b * NGRP + g
                numbers = pages_of(b, g)
                if not (isinstance(n, int) and n < 4):
                    sp.wait_ge(S("values_summed"), n - 3)
                for j, page in enumerate(numbers):
                    sp.dma_start(vring[:, g % 4, j, :], a["cache_v"][0, bass.ds(page, 1)].rearrange("a s h d -> (a s) (h d)")
                                 ).then_inc(S(f"cache_v_{g % 4}"), 16)

            def before(b, g, lag):
                return (b, g - lag) if g >= lag else (b - 1, g - lag + NGRP)

            sp.dma_start(pages[0:1, :], a["page_table"].rearrange("(o b) n -> o (b n)", o=1)).then_inc(S("page_table"), 16)
            sp.wait_ge(S("page_table"), 16)
            sp.wait_ge(S("f"), NT)
            for g in range(2):
                key_loads(0, g)
            sp.wait_ge(S("chunk_states"), 16)
            p_out = a["new_hgrn_prompt"][0, 0].rearrange("(c e) k v -> e k c v", e=2)
            for e in range(2):
                sp.dma_start(p_out[e], state[64 * e:64 * e + 64, 0, :, 64 * e:64 * e + 64]
                             ).then_inc(S("states_stored"), 16)
            sp.wait_ge(S("sample_states"), NB)
            for e in range(2):
                for b in range(NB):
                    sp.dma_start(st_out[e, :, b], state0[64 * e:64 * e + 64, b, :, 64 * e:64 * e + 64]
                                 ).then_inc(S("states_stored"), 16)

            sp.wait_ge(S("yb"), 1)
            sp.wait_ge(S("new_rows"), 4)
            for g in range(2, NGRP):
                value_loads(0, g - 2)
                key_loads(0, g)

            def gate_loads(q):
                for e in range(2):
                    c0 = GATE_AT[e] + 256 * q
                    sp.dma_start(gw[q % 2][e], w_in[:, :, c0:c0 + 256]).then_inc(S(f"w_gate_{q % 2}"), 16)

            def sequence_loads(b):
                for g in range(NGRP):
                    value_loads(*before(b, g, 2))
                    key_loads(b, g)

            sequence_loads(1)
            with sp.Fori(1, NB // 2) as pair:
                for u in range(2):
                    sequence_loads(2 * pair + u)
            for g in (NGRP - 2, NGRP - 1):
                value_loads(NB - 1, g)
            gate_loads(0)
            for e in range(2):
                sp.dma_start(wab[e], w_br[e]).then_inc(S("w_branches"), 16)
            gate_loads(1)

            sp.wait_ge(S("values_summed"), NB * NGRP)
            for i in range(NT):
                sp.dma_start(x2[0:ROWS[i], i, :], x_tok[i]).then_inc(S("x_again"), 16)
            w_out = a["w_out"][0].rearrange("(k p) n -> p k n", p=P)
            k = 0
            for o, n in WO_PARTS:
                if o == WO_PARTS[-1][0]:
                    sp.wait_ge(S("decoded"), NB)
                sp.dma_start(each(arena[:, o:o + D * n], n), w_out[:, k:k + n]).then_inc(S("w_out"), 16)
                k += n
            for q in range(2, KD // 2):
                sp.wait_ge(S("branch_products"), 8 * (q - 1))
                gate_loads(q)
            def expert_rows(n, u):
                if not (isinstance(n, int) and n < 2):
                    sp.wait_ge(S("rows_turned"), n - 1)
                sp.dma_start(xg[0:BLK, u, :], xg_dram[bass.ds(n * BLK, BLK), :]).then_inc(S(f"rows_{u}"), 16)

            def gate_up_weights(n, u):
                late = not (isinstance(n, int) and n < 2)
                if late:
                    sp.wait_ge(S("w_low"), n - 1)
                sp.dma_start(wgv[u], a["w_gate_exp"][0, bass.ds(n, 1)].rearrange("a (p k) f -> (a p) k f", k=KD)
                             ).then_inc(S(f"w_gate_exp_{u}"), 16)
                if late:
                    sp.wait_ge(S("gate_up"), n - 1)
                sp.dma_start(wuv[u], a["w_up_exp"][0, bass.ds(n, 1)].rearrange("a (p k) f -> (a p) k f", k=KD)
                             ).then_inc(S(f"w_up_exp_{u}"), 16)

            def down_weights(n, u):
                if not (isinstance(n, int) and n < 2):
                    sp.wait_ge(S("down"), n - 1)
                sp.dma_start(wdv[u], a["w_down_exp"][0, bass.ds(n, 1)].rearrange("a (p j) d -> (a p) j d", j=FJ)
                             ).then_inc(S(f"w_down_exp_{u}"), 16)

            sp.wait_ge(S("mixed"), NT)
            gate_up_weights(0, 0)
            down_weights(0, 0)
            sp.wait_ge(S("h2_scattered"), 32 * NT)
            sp.wait_ge(S("logits"), NT)
            for n in range(4):
                expert_rows(n, n % 2)
                if n:
                    gate_up_weights(n, n % 2)
                if n >= 2:
                    down_weights(n - 1, 1 - n % 2)
            with sp.Fori(2, NE // 2) as it:
                for u in range(2):
                    expert_rows(2 * it + u, u)
                    gate_up_weights(2 * it + u, u)
                    down_weights(2 * it + u - 1, 1 - u)
            down_weights(NE - 1, 1)
            sp.wait_ge(S("down"), NE)
            novf = sp.value_load(tab[0:1, NOVF:NOVF + 1], min_val=0, max_val=NOVF)
            with sp.Fori(0, NOVF) as i:
                e = sp.value_load(tab[0:1, bass.ds(i, 1)], min_val=0, max_val=NE - 1)
                with sp.If(i < novf):
                    sp.wait_ge(S("extra_products"), extra_stage(i, 0))
                    sp.dma_start(wgv[0], a["w_gate_exp"][0, bass.ds(e, 1)].rearrange("a (p k) f -> (a p) k f", k=KD)
                                 ).then_inc(S("extra_loaded"), 16)
                    sp.dma_start(wuv[0], a["w_up_exp"][0, bass.ds(e, 1)].rearrange("a (p k) f -> (a p) k f", k=KD)
                                 ).then_inc(S("extra_loaded"), 16)
                    sp.dma_start(wdv[0], a["w_down_exp"][0, bass.ds(e, 1)].rearrange("a (p j) d -> (a p) j d", j=FJ)
                                 ).then_inc(S("extra_loaded"), 16)
                    sp.dma_start(xg[0:BLK, 0, :], xg_dram[bass.ds((NE + i) * BLK, BLK), :]).then_inc(S("extra_loaded"), 16)
                with sp.Else():
                    sp.nop()
                sp.nop()
            for i in range(NT):
                sp.wait_ge(S("y_rows"), i + 1)
                dst = a["y_prompt"][0, P * i:P * i + P, :] if i < 4 else a["y_sample"].rearrange("b q d -> (b q) d")
                sp.dma_start(dst, x2[0:ROWS[i], i, :]).then_inc(S("rows_stored"), 16)
            sp.wait_ge(S("rows_stored"), 64 + 16 * NT)
            sp.wait_ge(S("states_stored"), 16 * (2 + 2 * NB))

        @block.gpsimd
        def _(pool):
            chain = Chain(pool, S("pool_chain"))

            def select(v, pattern, op, fill, base, cm):
                chain(nc.gpsimd.affine_select(out=v, in_=v, compare_op=op, fill=fill, base=base, pattern=pattern,
                                              channel_multiplier=cm))

            for t, v in ((ident, 0.0), (ones, 1.0), (tri_ge, 1.0), (headones, 1.0), (mask_lt, 1.0), (neg_lt, 0.0),
                         (tri_le, 1.0), (chk_le, 1.0), (chk_gt, 1.0), (sq_le, 1.0), (sq_gt, 1.0), (new_m, 1.0),
                         (new_neg, 0.0), (in_b, 1.0), (eps, EPS), (fold, 0.0)):
                chain(nc.gpsimd.memset(t[:, :], v))
            chain(nc.gpsimd.memset(flat(ybT), 0.0))
            chain.wait()
            select(ident[:, :], [[-1, P]], ALU.not_equal, 1.0, 0, 1)
            select(fold[:, :], [[-1, BLK]], ALU.not_equal, 1.0, 0, 1)
            select(tri_ge[:, :], [[-1, P]], ALU.is_ge, 0.0, 0, 1)
            select(mask_lt[:, :], [[1, P]], ALU.is_gt, 0.0, 0, -1)
            select(neg_lt[:, :], [[1, P]], ALU.is_gt, -BIG, 0, -1)
            select(tri_le[:, :], [[1, P]], ALU.is_ge, 0.0, 0, -1)
            select(chk_le[:, :], [[1, P]], ALU.is_ge, 0.0, 0, -1)
            select(chk_gt[:, :], [[-1, P]], ALU.is_gt, 0.0, 0, 1)
            select(sq_le[:, :], [[1, TS]], ALU.is_ge, 0.0, 0, -1)
            select(sq_gt[:, :], [[-1, TS]], ALU.is_gt, 0.0, 0, 1)
            select(each(headones[:, :], 2), [[-64, 2], [0, 64]], ALU.is_ge, 0.0, 0, 1)
            select(in_b[:, :], [[-TQ, NB]], ALU.is_ge, 0.0, 0, 1)
            new4 = [v[:, :].rearrange("p (c b e q) -> p c b e q", c=CT, b=NB, e=2) for v in (new_m, new_neg)]
            for c in range(CT):
                for v, fill in zip(new4, (0.0, -BIG)):
                    select(v[:, c], [[-TQ, NB], [0, 2], [0, TQ]], ALU.is_ge, fill, 0, 1)
            chain.wait()
            select(fold[:, :], [[-1, BLK]], ALU.not_equal, 1.0, -BLK, 1)
            select(each(headones[:, :], 2), [[64, 2], [0, 64]], ALU.is_ge, 0.0, 63, -1)
            select(each(chk_le[:, :], 4), [[-CHUNK, 4], [0, CHUNK]], ALU.is_ge, 0.0, 0, 1)
            select(each(chk_gt[:, :], 4), [[CHUNK, 4], [0, CHUNK]], ALU.is_ge, 0.0, CHUNK - 1, -1)
            select(each(sq_le[:, :], NB), [[-TQ, NB], [0, TQ]], ALU.is_ge, 0.0, 0, 1)
            select(each(sq_gt[:, :], NB), [[TQ, NB], [0, TQ]], ALU.is_ge, 0.0, TQ - 1, -1)
            select(in_b[:, :], [[TQ, NB]], ALU.is_ge, 0.0, TQ - 1, -1)
            for c in range(CT):
                for v, fill in zip(new4, (0.0, -BIG)):
                    select(v[:, c], [[TQ, NB], [0, 2], [1, TQ]], ALU.is_gt, fill, 0, -1)
            chain.wait()
            nc.gpsimd.memset(ss[:, :], 0.0).then_inc(S("constants"), 1)
            pool.wait_ge(S("projected"), QKV)
            full = NBLK * BLK // P
            pool.dma_start(xg_dram[0:full * P, :].rearrange("(n p) d -> p n d", p=P),
                           flat(ybT)[:, 0:D].unsqueeze(1).to_broadcast([P, full, D])).then_inc(S("rows_zeroed"), 16)
            pool.dma_start(xg_dram[full * P:NBLK * BLK, :], flat(ybT)[0:NBLK * BLK - full * P, 0:D]
                           ).then_inc(S("rows_zeroed"), 16)
            extra = yg_dram[NE * BLK:NBLK * BLK, :].rearrange("(n p) d -> p n d", p=BLK)
            pool.dma_start(extra, flat(ybT)[0:BLK, 0:D].unsqueeze(1).to_broadcast([BLK, NOVF, D])
                           ).then_inc(S("rows_zeroed"), 16)
            pool.wait_ge(S("projected"), len(JOBS))
            nc.gpsimd.memset(arena[:, 0:8192], 0.0).then_inc(S("states_zero"), 1)
            pool.wait_ge(S("x2"), 1)
            chain(nc.gpsimd.iota(gcol_i, pattern=[[1, NG], [0, EG]], base=0, channel_multiplier=0))
            chain(nc.gpsimd.iota(ecol_i, pattern=[[1, NE]], base=0, channel_multiplier=0))
            chain.wait()
            nc.gpsimd.tensor_copy(gcol, gcol_i).then_inc(S("counters"), 1)
            nc.gpsimd.tensor_copy(ecol, ecol_i).then_inc(S("counters"), 1)
            pool.wait_ge(S("rows_zeroed"), 48)
            pool.wait_ge(S("slots"), 1)
            for i in range(NT):
                for k in range(2):
                    pool.indirect_dma_start(
                        out=xg_dram, out_offset=bass.IndirectOffsetOnAxis(
                            ap=slot_i[0:ROWS[i], 2 * i + k:2 * i + k + 1].bitcast(U32), axis=0),
                        in_=h2[0:ROWS[i], i, :], in_offset=None).then_inc(S("h2_scattered"), 16)
            pool.wait_ge(S("extra_table"), 1)
            novf = pool.value_load(tab[0:1, NOVF:NOVF + 1], min_val=0, max_val=NOVF)
            pool.wait_ge(S("out_stored_0"), 16 * NE // 2)
            pool.wait_ge(S("out_stored_1"), 16 * NE // 2)
            pool.wait_ge(S("extra_stored"), novf * 16 + 16)
            pool.sem_inc(S("pool_passed"), 1)
            for i in range(NT):
                for k in range(2):
                    pool.indirect_dma_start(
                        out=yg[0:ROWS[i], 2 * i + k, :], out_offset=None, in_=yg_dram,
                        in_offset=bass.IndirectOffsetOnAxis(
                            ap=slot_i[0:ROWS[i], 2 * i + k:2 * i + k + 1].bitcast(U32), axis=0)
                    ).then_inc(S(f"y_gathered_{i}"), 16)

        @block.tensor
        def _(pe):
            mm = nc.tensor.matmul
            turn = nc.tensor.transpose

            pe.wait_ge(S("constants"), 1)
            for i, r in enumerate(ROWS):
                pe.wait_ge(S("x_normed"), i + 1)
                for kk in range(2):
                    n = 2 * i + kk
                    if n >= 4:
                        pe.wait_ge(S("hT"), n - 3)
                    for c in range(4):
                        cols = xt[0:r, i, :].rearrange("p (m k) -> p k m", k=KD)[:, 4 * kk + c, :]
                        last = turn(ps[:, 4 + n % 4, P * c:P * c + r], cols, ident[0:r, 0:r])
                    last.then_inc(S("x_turned"), 1)
            pe.wait_ge(S("hT"), 2 * NT)

            def project(n):
                c, j = JOBS[n]
                bank = 4 + 2 * (n % 2)
                if j == 0:
                    pe.wait_ge(S(f"w_in_{c % 3}"), 16 * (c // 3 + 1))
                if n >= 2:
                    pe.wait_ge(S("projection_out"), n - 1)
                for k in range(KD):
                    if CHUNKS[c][0] == "cols":
                        for hf in range(2):
                            last = mm(ps[:, bank + hf, 0:TH], wring[:, c % 3, k, P * j:P * j + P],
                                      hT[:, k, TH * hf:TH * hf + TH], start=k == 0, stop=k == KD - 1)
                    else:
                        last = mm(ps[0:ROWS[j], bank, :], hT[:, k, P * j:P * j + ROWS[j]], wring[:, c % 3, k, :],
                                  start=k == 0, stop=k == KD - 1)
                last.then_inc(S("projected"), 1)

            def head_sums(m):
                pe.wait_ge(S("squares"), m + 1)
                for c in range(CT):
                    if m or c >= 2:
                        pe.wait_ge(S("head_roots"), 4 * m + max(c - 1, 0))
                    for hf in range(2):
                        last = mm(ps[:, 2 * (c % 2) + hf, 0:TH], headones[:, :], sq[m][:, c, TH * hf:TH * hf + TH],
                                  start=True, stop=True)
                    last.then_inc(S("head_sums"), 1)

            for n in range(8):
                project(n)
            head_sums(0)
            for n in range(8, QKV):
                project(n)
            head_sums(1)
            for n in range(QKV, QKV + 2):
                project(n)
            pe.wait_ge(S("heads_normed"), 2 * CT)
            for i, r in enumerate(ROWS):
                if i >= 4:
                    pe.wait_ge(S("k_rows"), i - 3)
                for c in range(CT):
                    last = turn(ps[0:r, i % 4, P * c:P * c + P], kT[:, c, P * i:P * i + r], ident[:, :])
                last.then_inc(S("k_turned_rows"), 1)

            def attn_scores(h):
                if h:
                    pe.wait_ge(S("attn_args"), h)
                else:
                    pe.wait_ge(S("k_rows"), NT)
                r0 = 64 * (h % 2)
                for s in range(4):
                    o = SB_OFF[s]
                    last = mm(ps[:, o // 512, o % 512:o % 512 + SB_LEN[s]], kT[r0:r0 + 64, h // 2, P * s:P * s + P],
                              qT[r0:r0 + 64, h // 2, P * s:SEQ], start=True, stop=True)
                last.then_inc(S("attn_scores"), 1)

            def attn_remain(h):
                pe.wait_ge(S("attn_losses"), h + 1)
                for s in (0, 1, 3, 2):
                    o = SB_OFF[s]
                    bank, c0 = o // 512, o % 512
                    last = mm(ps[:, bank, c0:c0 + SB_LEN[s]], tri_ge[:, :], a_L[:, o:o + SB_LEN[s]],
                              start=True, stop=s == 3)
                    for j in range(s + 1, 4):
                        skip = P * (j - s)
                        last = mm(ps[:, bank, c0 + skip:c0 + SB_LEN[s]], ones[:, :],
                                  a_L[:, SB_OFF[j]:SB_OFF[j] + SB_LEN[j]], start=False, stop=j == 3)
                last.then_inc(S("attn_remains"), 1)

            def attn_values(h):
                pe.wait_ge(S("attn_weights"), h + 1)
                r0 = 64 * (h % 2)
                if h % 2 == 0 and h:
                    pe.wait_ge(S("attn_out"), h // 2)
                for s in range(4):
                    last = mm(ps[r0:r0 + 64, 3, P * s:SEQ], vtok[:, s, DH * h:DH * h + DH],
                              a_A[:, h % 2, SB_OFF[s]:SB_OFF[s] + SB_LEN[s]], start=s == 0, stop=s == 3)
                last.then_inc(S("attn_values"), 1)

            n = QKV + 2
            for h in range(H):
                attn_scores(h)
                for _ in range(2 if h == 0 else 1):
                    if n < len(JOBS):
                        project(n)
                        n += 1
                attn_remain(h)
                if n < len(JOBS):
                    project(n)
                    n += 1
                attn_values(h)
            assert n == len(JOBS)

            for i in range(5):
                r, prompt = ROWS[i], i < 4
                le, gt = (chk_le, chk_gt) if prompt else (sq_le, sq_gt)
                pe.wait_ge(S("log_f"), i + 1)
                if i:
                    pe.wait_ge(S("chunk_states"), 4 * i)
                    pe.wait_ge(S("o_read"), i)
                    pe.wait_ge(S("decayed"), 3 * i)
                else:
                    pe.wait_ge(S("attn_args"), H)
                for c in range(CT):
                    mm(ps[:, 0, r * c:r * c + r], ftok[0:r, i, P * c:P * c + P], le[0:r, 0:r], start=True, stop=True)
                mm(ps[0:r, 1, :], gt[0:r, 0:r], ftok[0:r, i, :], start=True, stop=True)
                for c in range(CT):
                    last = turn(ps[:, 2, r * c:r * c + r], ktok[0:r, P * c:P * c + P], ident[0:r, 0:r])
                last.then_inc(S("decay_sums"), 1)
                pe.wait_ge(S("decayed"), 3 * i + 3)
                if i:
                    pe.wait_ge(S("hg_masked"), 2 * i)
                else:
                    pe.wait_ge(S("attn_out"), CT)
                    pe.wait_ge(S("projection_out"), len(JOBS))
                for e in range(2):
                    for c in range(CT):
                        last = mm(ps[0:r, 3 + e, r * c:r * c + r], kd[64 * e:64 * e + 64, c, 0:r],
                                  qd[64 * e:64 * e + 64, c, 0:r], start=True, stop=True)
                last.then_inc(S("hg_scores"), 1)
                if prompt:
                    for k in range(4):
                        for c in range(CT):
                            last = mm(ps[:, KV_BANK[k], P * c:P * c + P], kdec[CHUNK * k:CHUNK * k + CHUNK, P * c:P * c + P],
                                      itok[CHUNK * k:CHUNK * k + CHUNK, i, P * c:P * c + P], start=True, stop=True)
                        last.then_inc(S("chunk_kv"), 1)
                pe.wait_ge(S("hg_masked"), 2 * i + 2)
                for c in range(CT):
                    for e in range(2):
                        mm(ps[64 * e:64 * e + 64, 1, r * c:r * c + r], itok[0:r, i, P * c + 64 * e:P * c + 64 * e + 64],
                           scm[0:r, 4 * e + c, 0:r], start=c == 0, stop=False, skip_group_check=True)
                if prompt:
                    for k in range(4):
                        if i or k:
                            pe.wait_ge(S("chunk_states"), 4 * i + k)
                        else:
                            pe.wait_ge(S("states_zero"), 1)
                        for c in range(CT):
                            last = mm(ps[:, 1, P * c + CHUNK * k:P * c + CHUNK * k + CHUNK], state[:, (4 * i + k) % 8, c, :],
                                      qd[:, c, CHUNK * k:CHUNK * k + CHUNK], start=False, stop=True, skip_group_check=True)
                    last.then_inc(S("hg_out"), 1)
                else:
                    pe.wait_ge(S("states_loaded"), 32 * NB)
                    for b in range(NB):
                        for c in range(CT):
                            last = mm(ps[:, 1, TS * c + TQ * b:TS * c + TQ * b + TQ], state0[:, b, c, :],
                                      qd[:, c, TQ * b:TQ * b + TQ], start=False, stop=True, skip_group_check=True)
                    last.then_inc(S("hg_out"), 1)
                    pe.wait_ge(S("ib"), 1)
                    for b in range(NB):
                        if b >= 4:
                            pe.wait_ge(S("sample_states"), b - 3)
                        for c in range(CT):
                            last = mm(ps[:, KV_BANK[b % 4], P * c:P * c + P], kdec[0:r, P * c:P * c + P],
                                      ib[0:r, b, P * c:P * c + P], start=True, stop=True)
                        last.then_inc(S("sample_kv"), 1)
            pe.wait_ge(S("sample_states"), NB)
            head_sums(2)

            pe.wait_ge(S("q_blocks"), 1)
            for c in range(CT):
                last = mm(ps[0:TS, 4, 64 * c:64 * c + 64], kT[:, c, SEQ:T], qblk[:, :, 8 * c:8 * c + 8],
                          start=True, stop=True)
            last.then_inc(S("new_products"), 1)
            pe.wait_ge(S("new_rows"), 2)
            mm(ps[0:TS, 5, 0:256], tri_ge[0:TS, 0:TS], n_L[0:TS, :], start=True, stop=True).then_inc(S("new_products"), 1)
            pe.wait_ge(S("new_act"), 4)
            for c in range(CT):
                last = mm(ps[:, 6, 64 * c:64 * c + 64], vtok[0:TS, 4, P * c:P * c + P],
                          n_e[0:TS, 64 * c:64 * c + 64], start=True, stop=True)
            last.then_inc(S("new_products"), 1)

            def turn_keys(b, g, j):
                n = b * NGRP + g
                if j == 0:
                    pe.wait_ge(S(f"cache_k_{g % 2}"), (b * 4 + g // 2 + 1) * 16 * GP)
                if g or not first(b):
                    pe.wait_ge(S("kT_act" if j < 2 else "kT_dve"), 2 * n - 1 + j % 2)
                for c in range(CT):
                    last = turn(ps[:, j, P * c:P * c + P], kring[:, g % 2, j, P * c:P * c + P], ident[:, :])
                last.then_inc(S("page_turned"), 1)

            def page_scores(b, g, j):
                n = b * NGRP + g
                if j == 0:
                    pe.wait_ge(S("kT_act"), 2 * n + 2)
                    pe.wait_ge(S("kT_dve"), 2 * n + 2)
                    if not isinstance(n, int) or n >= 2:
                        pe.wait_ge(S("page_args"), n - 1)
                for c in range(CT):
                    last = mm(ps[:, 4 + g % 2, 32 * j + 8 * c:32 * j + 8 * c + 8], d_kt[:, g % 2, j, P * c:P * c + P],
                              qblk[:, bass.ds(b, 1), 8 * c:8 * c + 8], start=True, stop=True)
                if j == GP - 1:
                    last.then_inc(S("page_scores"), 1)

            def page_remains(b, g):
                n = b * NGRP + g
                pe.wait_ge(S("page_sums"), n + 1)
                mm(ps[:, 4 + g % 2, 128:256], tri_ge[:, :], d_L[:, g % 2, :], start=True, stop=False)
                mm(ps[:, 4 + g % 2, 128:256], ones[:, :], d_R[:, g % 4, :], start=False, stop=True
                   ).then_inc(S("page_remains"), 1)

            def page_values(b, g, j):
                n = b * NGRP + g
                if j == 0:
                    pe.wait_ge(S(f"cache_v_{g % 4}"), (b * 2 + g // 4 + 1) * 16 * GP)
                    pe.wait_ge(S("page_weights"), n + 1)
                    if g == 0 and first(b):
                        pe.wait_ge(S("new_rows"), 4)
                    elif g == 0:
                        pe.wait_ge(S("values_out"), b)
                last = mm(ps[0:32, 6, :], d_A[:, g % 4, 32 * j:32 * j + 32], vring[:, g % 4, j, :],
                          start=g == 0 and j == 0, stop=g == NGRP - 1 and j == GP - 1)
                if j == GP - 1:
                    last.then_inc(S("values_summed"), 1)

            def turn_values(b):
                pe.wait_ge(S("values_out"), b + 1)
                pe.sem_inc(S("pe_passed"), 1)
                for c in range(CT):
                    last = turn(ps[:, 7, 32 * c:32 * c + 32], d_o[0:32, P * c:P * c + P], ident[0:32, 0:32])
                last.then_inc(S("values_turned"), 1)

            def before(b, g, lag):
                return (b, g - lag) if g >= lag else (b - 1, g - lag + NGRP)

            def decode_steps(b):
                for g in range(NGRP):
                    if g == 4 and not first(b):
                        turn_values(b - 1)
                    for j in range(GP):
                        if j == 3 and (g >= 2 or not first(b)):
                            page_remains(*before(b, g, 2))
                        turn_keys(b, g, j)
                        for lag, part in ((1, page_scores), (3, page_values)):
                            if g >= lag or not first(b):
                                part(*before(b, g, lag), j)

            def branch_product(m, e):
                bank = 2 * e
                if m:
                    pe.wait_ge(S("gates_read" if e < 2 else "branches_read"), 2 * m - 1 + e % 2)
                if e == 0 and m % 2 == 0:
                    pe.wait_ge(S(f"w_gate_{m // 2 % 2}"), 32 * (m // 4 + 1))
                for k in range(KD if e < 2 else CT):
                    for hf in range(2):
                        cols = slice(TH * hf, TH * hf + TH)
                        if e < 2:
                            last = mm(ps[:, bank + hf, 0:TH], gw[m // 2 % 2][e][:, k, P * (m % 2):P * (m % 2) + P],
                                      hT[:, k, cols], start=k == 0, stop=k == KD - 1)
                        else:
                            last = mm(ps[:, bank + hf, 0:TH], wab[e - 2][:, k, P * m:P * m + P],
                                      (osbT, ybT)[e - 2][:, k, cols], start=k == 0, stop=k == CT - 1)
                last.then_inc(S("branch_products"), 1)

            pe.wait_ge(S("head_roots"), 3 * CT)
            decode_steps(0)
            decode_steps(1)
            with pe.Fori(1, NB // 2) as pair:
                for u in range(2):
                    decode_steps(2 * pair + u)
            page_remains(NB - 1, NGRP - 2)
            for j in range(GP):
                page_scores(NB - 1, NGRP - 1, j)
                page_values(NB - 1, NGRP - 3, j)
            branch_product(0, 0)
            page_remains(NB - 1, NGRP - 1)
            for j in range(GP):
                page_values(NB - 1, NGRP - 2, j)
            branch_product(0, 1)
            for j in range(GP):
                page_values(NB - 1, NGRP - 1, j)
            turn_values(NB - 1)

            pe.wait_ge(S("w_branches"), 32)
            pe.wait_ge(S("decoded"), NB)
            for m in range(KD):
                for e in range(0 if m else 2, 4):
                    branch_product(m, e)
            pe.wait_ge(S("merged"), KD)
            pe.wait_ge(S("w_out"), 16 * len(WO_PARTS))
            def mix(i):
                r = ROWS[i]
                if i >= 2:
                    pe.wait_ge(S("x2"), i - 1)
                for k in range(KD):
                    for hf in range(2):
                        last = mm(ps[0:r, 2 * (i % 2) + hf, :], mrg[:, k, P * i:P * i + r], wo[k][:, 512 * hf:512 * hf + 512],
                                  start=k == 0, stop=k == KD - 1)
                last.then_inc(S("mixed"), 1)
            def turn_h2(i):
                r = ROWS[i]
                pe.wait_ge(S("h2"), i + 1)
                if i:
                    pe.wait_ge(S("h2_cols"), i)
                for k in range(KD):
                    cols = h2[0:r, i, :].rearrange("p (m k) -> p k m", k=KD)[:, k, :]
                    last = turn(ps[:, 4 + k // 4, P * (k % 4):P * (k % 4) + r], cols, ident[0:r, 0:r])
                last.then_inc(S("h2_turned"), 1)

            def router(i):
                r = ROWS[i]
                pe.wait_ge(S("h2_cols"), i + 1)
                if i:
                    pe.wait_ge(S("logits_read"), i)
                for k in range(KD):
                    last = mm(ps[0:r, 6, 0:NG + NE], h2T[:, i % 2, k, 0:r], wr[:, k, :], start=k == 0, stop=k == KD - 1)
                last.then_inc(S("logits"), 1)

            for i in range(NT + 2):
                if i < NT:
                    mix(i)
                if i == 2:
                    pe.wait_ge(S("router_inputs"), 80)
                if i >= 2:
                    router(i - 2)
                if 1 <= i <= NT:
                    turn_h2(i - 1)
            pe.wait_ge(S("chosen"), NT)
            for i, r in enumerate(ROWS):
                for j in range(i + 1):
                    lhs = mask_lt[0:r, 0:r] if j == i else ones[0:ROWS[j], 0:r]
                    mm(ps[0:r, 7, NE * i:NE * i + NE], lhs, r_O[0:ROWS[j], NE * j:NE * j + NE], start=j == 0, stop=j == i)
            for j, r in enumerate(ROWS):
                last = mm(ps[0:NE, 6, 0:P], r_O[0:r, NE * j:NE * j + NE], ones[0:r, :], start=j == 0, stop=j == NT - 1)
            last.then_inc(S("list_sums"), 1)
            pe.wait_ge(S("extra_blocks"), 1)
            mm(ps[:, 5, 0:NE], r_ov[0:NE, :], mask_lt[0:NE, 0:NE], start=True, stop=True)
            mm(ps[0:NE, 5, NE:NE + 1], tri_le[0:NE, 0:NE], r_ov[0:NE, 0:1], start=True, stop=True)
            mm(ps[:, 5, NE + 1:NE + 2], ones[0:NE, :], r_ov[0:NE, 0:1], start=True, stop=True
               ).then_inc(S("list_sums"), 1)
            pe.wait_ge(S("extra_after"), 1)
            mm(ps[:, 4, 0:NOVF], ones[0:NE, :], r_ind[0:NE, :], start=True, stop=True).then_inc(S("list_sums"), 1)

            def rows_to_cols(n, u):
                pe.wait_ge(S(f"rows_{u}"), rows_count(n, u))
                if not (isinstance(n, int) and n < 1):
                    pe.wait_ge(S("xg_cols"), n)
                pe.sem_inc(S("pe_passed"), 1)
                for k in range(KD):
                    cols = xg[0:BLK, u, :].rearrange("p (m k) -> p k m", k=KD)[:, k, :]
                    last = turn(ps[:, 0, BLK * k:BLK * k + BLK], cols, ident[0:BLK, 0:BLK])
                last.then_inc(S("rows_turned"), 1)

            def rows_count(n, u):
                return 16 * (n // 2 + 1) if isinstance(n, int) else 16 + (n - u) * 8

            def gate_up(n, u):
                pe.wait_ge(S("xg_split"), n + 1)
                pe.wait_ge(S("w_low"), n + 1)
                if not (isinstance(n, int) and n < 2):
                    pe.wait_ge(S("hidden"), n - 1)
                for k in range(KD):
                    mm(ps[:, 1 + 2 * u, :], xg_parts[:, k, :], w_hi[:, k, :], start=k == 0, stop=False)
                    last = mm(ps[:, 1 + 2 * u, :], xg_parts[:, k, :], w_lo[:, k, :], start=False, stop=k == KD - 1)
                last.then_inc(S("gate"), 1)
                pe.wait_ge(S(f"w_up_exp_{u}"), rows_count(n, u))
                for k in range(KD):
                    last = mm(ps[0:BLK, 2 + 2 * u, :], xgT[:, u, k, :], wuv[u][:, k, :], start=k == 0, stop=k == KD - 1)
                last.then_inc(S("gate_up"), 1)
                pe.wait_ge(S("gate_copied"), n + 1)
                mm(ps[0:BLK, 1 + 2 * u, :], fold[:, :], m_g, start=True, stop=True).then_inc(S("gate_folded"), 1)

            def turn_hidden(n, u):
                pe.wait_ge(S("hidden"), n + 1)
                pe.sem_inc(S("pe_passed"), 1)
                cols = m_hr[0:BLK, u, :].rearrange("p (m j) -> p j m", j=FJ)
                for j in range(FJ):
                    last = turn(ps[:, 7, FJ * BLK * u + BLK * j:FJ * BLK * u + BLK * j + BLK], cols[:, j, :],
                                ident[0:BLK, 0:BLK])
                last.then_inc(S("hidden_turned"), 1)

            def down(n, u):
                pe.wait_ge(S("hidden_cols"), n + 1)
                pe.wait_ge(S(f"w_down_exp_{u}"), rows_count(n, u))
                if not (isinstance(n, int) and n < 1):
                    pe.wait_ge(S("y_act"), n)
                    pe.wait_ge(S("y_dve"), n)
                for hf in range(2):
                    for j in range(FJ):
                        last = mm(ps[0:BLK, 5 + hf, :], m_h[:, u, j, :], wdv[u][:, j, 512 * hf:512 * hf + 512],
                                  start=j == 0, stop=j == FJ - 1)
                last.then_inc(S("down"), 1)

            rows_to_cols(0, 0)
            gate_up(0, 0)
            rows_to_cols(1, 1)
            turn_hidden(0, 0)
            gate_up(1, 1)
            rows_to_cols(2, 0)
            down(0, 0)
            with pe.Fori(1, NE // 2 - 1) as it:
                for u in range(2):
                    turn_hidden(2 * it + u - 1, 1 - u)
                    gate_up(2 * it + u, u)
                    rows_to_cols(2 * it + u + 1, 1 - u)
                    down(2 * it + u - 1, 1 - u)
            turn_hidden(NE - 3, 1)
            gate_up(NE - 2, 0)
            rows_to_cols(NE - 1, 1)
            down(NE - 3, 1)
            turn_hidden(NE - 2, 0)
            gate_up(NE - 1, 1)
            down(NE - 2, 0)
            turn_hidden(NE - 1, 1)
            down(NE - 1, 1)
            pe.sem_inc(S("extra_products"), 4)
            novf = pe.value_load(tab[0:1, NOVF:NOVF + 1], min_val=0, max_val=NOVF)
            with pe.Fori(0, NOVF) as i:
                with pe.If(i < novf):
                    pe.wait_ge(S("extra_loaded"), (i + 1) * 64)
                    pe.sem_inc(S("pe_passed"), 1)
                    for k in range(KD):
                        cols = xg[0:BLK, 0, :].rearrange("p (m k) -> p k m", k=KD)[:, k, :]
                        last = turn(ps[:, 0, BLK * k:BLK * k + BLK], cols, ident[0:BLK, 0:BLK])
                    last.then_inc(S("extra_products"), 1)
                    pe.wait_ge(S("extra_dve"), 4 * i + 1)
                    for e, wv in enumerate((wgv[0], wuv[0])):
                        for k in range(KD):
                            last = mm(ps[0:BLK, 1 + e, :], xgT[:, 0, k, :], wv[:, k, :], start=k == 0, stop=k == KD - 1)
                    last.then_inc(S("extra_products"), 1)
                    pe.wait_ge(S("extra_dve"), 4 * i + 2)
                    pe.sem_inc(S("pe_passed"), 1)
                    cols = m_hr[0:BLK, 0, :].rearrange("p (m j) -> p j m", j=FJ)
                    for j in range(FJ):
                        last = turn(ps[:, 7, BLK * j:BLK * j + BLK], cols[:, j, :], ident[0:BLK, 0:BLK])
                    last.then_inc(S("extra_products"), 1)
                    pe.wait_ge(S("extra_dve"), 4 * i + 3)
                    for hf in range(2):
                        for j in range(FJ):
                            last = mm(ps[0:BLK, 5 + hf, :], m_h[:, 0, j, :], wdv[0][:, j, 512 * hf:512 * hf + 512],
                                      start=j == 0, stop=j == FJ - 1)
                    last.then_inc(S("extra_products"), 1)
                with pe.Else():
                    pe.nop()
                pe.nop()

        @block.scalar
        def _(act):
            fn = nc.scalar.activation

            def load(dst, src, signal):
                act.dma_start(dst, src).then_inc(S(signal), 16)

            load(w1c[:, :], a["norm1_w"][0].rearrange("(p k) -> p k", k=KD), "w1_loaded")
            for j, name in enumerate(("q_norm_w", "k_norm_w", "hg_norm_w")):
                for e in range(2):
                    load(qkg[64 * e:64 * e + 64, j:j + 1], a[name][0].rearrange("(p o) -> p o", o=1), "small_loaded")
            load(bias8[:, :], a["sb_bias"].to_broadcast([P, H]), "small_loaded")

            act.wait_ge(S("constants"), 1)
            for i, r in enumerate(ROWS):
                act.wait_ge(S(f"x_loaded_{i}"), 16)
                if i:
                    act.wait_ge(S("row_squares"), i)
                fn(kout_flat[0:r, 0:D], xt[0:r, i, :], ACT.Square, accum_out=ss[0:r, i:i + 1]).then_inc(S("row_squares"), 1)
                act.wait_ge(S("row_squares"), i + 1)
                fn(rstd[0:r, i:i + 1], ss[0:r, i:i + 1], ACT.Sqrt, scale=1.0 / D, bias=eps[0:r, :]).then_inc(S("row_roots"), 1)

            def projection_out(n):
                c, j = JOBS[n]
                kind, dst = CHUNKS[c]
                bank = 4 + 2 * (n % 2)
                act.wait_ge(S("projected"), n + 1)
                if kind == "cols":
                    fn(each(dst[:, j, :], 2), ps[:, bank:bank + 2, 0:TH], ACT.Copy).then_inc(S("projection_out"), 1)
                else:
                    r = ROWS[j]
                    func, scale = (ACT.Exp, -1.0) if dst is ftok else (ACT.Copy, 1.0)
                    fn(dst[0:r, j, :], ps[0:r, bank, :], func, scale=scale).then_inc(S("projection_out"), 1)

            def head_roots(m):
                for c in range(CT):
                    act.wait_ge(S("head_sums"), 4 * m + c + 1)
                    if m == 1:
                        act.wait_ge(S("heads_normed"), c + 1)
                    fn(each(rs[m][:, c, :], 2), ps[:, 2 * (c % 2):2 * (c % 2) + 2, 0:TH], ACT.Sqrt,
                       scale=1.0 / DH, bias=eps[:, :]).then_inc(S("head_roots"), 1)

            for n in range(8):
                projection_out(n)
            head_roots(0)
            for n in range(8, QKV):
                projection_out(n)
            head_roots(1)
            for n in range(QKV, QKV + 2):
                projection_out(n)

            act.wait_ge(S("heads_normed"), 2 * CT)
            load(lbr[:, :, :], a["lb_logits"].rearrange("(o r) c -> o r c", o=1).to_broadcast([P, 2, W]), "lb_loaded")
            n = QKV + 2
            for h in range(H):
                if h == 2:
                    act.wait_ge(S("lb_shifted"), 1)
                    fn(lbr[:, :, :], lbr[:, :, :], ACT.Exp).then_inc(S("lb_exp"), 1)
                act.wait_ge(S("attn_scores"), h + 1)
                if h:
                    act.wait_ge(S("attn_losses"), h)
                    act.wait_ge(S("attn_weights"), h)
                fn(a_z, ps_attn, ACT.Identity, scale=SCALE, bias=bias8[:, h:h + 1]).then_inc(S("attn_z"), 1)
                act.wait_ge(S("attn_z"), h + 1)
                fn(a_e, a_z, ACT.Abs).then_inc(S("attn_softplus"), 1)
                act.wait_ge(S("attn_softplus"), 3 * h + 1)
                fn(a_e, a_e, ACT.Exp, scale=-1.0).then_inc(S("attn_softplus"), 1)
                act.wait_ge(S("attn_softplus"), 3 * h + 2)
                fn(a_ln, a_e, ACT.Ln, bias=1.0).then_inc(S("attn_softplus"), 1)
                for _ in range(2 if h == 0 else 1):
                    if n < len(JOBS):
                        projection_out(n)
                        n += 1
                act.wait_ge(S("attn_args"), h + 1)
                if h < 2:
                    act.wait_ge(S("rows_stored"), 64)
                else:
                    act.wait_ge(S("attn_values"), h - 1)
                fn(a_A[:, h % 2, :], a_z, ACT.Exp).then_inc(S("attn_weights"), 1)
                if n < len(JOBS):
                    projection_out(n)
                    n += 1

            for i, r in enumerate(ROWS):
                act.wait_ge(S("f"), i + 1)
                fn(ftok[0:r, i, :], ftok[0:r, i, :], ACT.Ln).then_inc(S("log_f"), 1)
                act.wait_ge(S("decay_sums"), i + 1)
                fn(g_e[:, 0:CT * r], ps[:, 0, 0:CT * r], ACT.Exp).then_inc(S("decays"), 1)
                fn(g_en[:, 0:CT * r], ps[:, 0, 0:CT * r], ACT.Exp, scale=-1.0).then_inc(S("decays"), 1)
                fn(g_e2[0:r, :], ps[0:r, 1, :], ACT.Exp).then_inc(S("decays"), 1)
            act.wait_ge(S("decayed"), 3 * NT)
            fn(flat(hqT), flat(gT), ACT.Sigmoid).then_inc(S("g_sigmoid"), 1)
            head_roots(2)

            act.wait_ge(S("new_rows"), 1)
            fn(n_e[0:TS, :], n_z[0:TS, :], ACT.Abs).then_inc(S("new_act"), 1)
            act.wait_ge(S("new_act"), 1)
            fn(n_e[0:TS, :], n_e[0:TS, :], ACT.Exp, scale=-1.0).then_inc(S("new_act"), 1)
            act.wait_ge(S("new_act"), 2)
            fn(n_s[0:TS, :], n_e[0:TS, :], ACT.Ln, bias=1.0).then_inc(S("new_act"), 1)
            act.wait_ge(S("new_rows"), 3)
            fn(n_e[0:TS, :], n_z[0:TS, :], ACT.Exp).then_inc(S("new_act"), 1)

            def turned_out(b, g):
                n = b * NGRP + g
                for j in range(2):
                    act.wait_ge(S("page_turned"), 4 * n + j + 1)
                    if not isinstance(n, int) or n >= 2:
                        act.wait_ge(S("page_scores"), n - 1)
                    fn(d_kt[:, g % 2, j, :], ps[:, j, :], ACT.Copy).then_inc(S("kT_act"), 1)

            def softplus_parts(b, g):
                n = b * NGRP + g
                act.wait_ge(S("page_z"), n + 1)
                fn(d_e[:, g % 2, :], d_z[:, g % 2, :], ACT.Abs).then_inc(S("page_softplus"), 1)
                act.wait_ge(S("page_softplus"), 3 * n + 1)
                fn(d_e[:, g % 2, :], d_e[:, g % 2, :], ACT.Exp, scale=-1.0).then_inc(S("page_softplus"), 1)
                act.wait_ge(S("page_softplus"), 3 * n + 2)
                fn(d_ln[:, g % 2, :], d_e[:, g % 2, :], ACT.Ln, bias=1.0).then_inc(S("page_softplus"), 1)

            def page_weights(b, g):
                n = b * NGRP + g
                act.wait_ge(S("page_args"), n + 1)
                if not isinstance(n, int) or n >= 4:
                    act.wait_ge(S("values_summed"), n - 3)
                fn(d_A[:, g % 4, :], d_z[:, g % 2, :], ACT.Exp).then_inc(S("page_weights"), 1)

            def before(b, g, lag):
                return (b, g - lag) if g >= lag else (b - 1, g - lag + NGRP)

            def decode_steps(b):
                for g in range(NGRP):
                    turned_out(b, g)
                    for lag, part in ((2, page_weights), (1, softplus_parts)):
                        if g >= lag or not first(b):
                            part(*before(b, g, lag))

            decode_steps(0)
            decode_steps(1)
            with act.Fori(1, NB // 2) as pair:
                for u in range(2):
                    decode_steps(2 * pair + u)
            page_weights(NB - 1, NGRP - 2)
            softplus_parts(NB - 1, NGRP - 1)
            page_weights(NB - 1, NGRP - 1)

            for m in range(KD):
                for e, dst in enumerate((m_sa, m_sb)):
                    act.wait_ge(S("branch_products"), 4 * m + e + 1)
                    if m >= 2:
                        act.wait_ge(S("merged"), m - 1)
                    elif m == 0:
                        act.wait_ge(S("decoded"), NB)
                    fn(each(dst[:, m % 2, :], 2), ps[:, 2 * e:2 * e + 2, 0:TH], ACT.Sigmoid).then_inc(S("gates_read"), 1)
            act.wait_ge(S("branch_products"), 4 * KD)
            load(w2r[:, :], a["norm2_w"].to_broadcast([P, D]), "router_inputs")
            act.wait_ge(S("merged"), KD)
            load(wr[:, :, 0:NG], a["w_group_router"][0].rearrange("(p k) n -> p k n", k=KD), "router_inputs")
            load(wr[:, :, NG:NG + NE], a["w_expert_router"][0].rearrange("(p k) n -> p k n", k=KD), "router_inputs")
            act.wait_ge(S("route_zero"), 1)
            load(r_b36[:, 0:NG], a["b_group_router"].to_broadcast([P, NG]), "router_inputs")
            load(r_b36[:, NG:NG + NE], a["b_expert_router"].to_broadcast([P, NE]), "router_inputs")
            def norm2(i):
                r = ROWS[i]
                act.wait_ge(S("x2"), i + 1)
                if i:
                    act.wait_ge(S("row_squares"), NT + i)
                fn(sqj[0:r, :], x2[0:r, i, :], ACT.Square, accum_out=ss2[0:r, i:i + 1]).then_inc(S("row_squares"), 1)
                act.wait_ge(S("row_inverses"), 1 + i)
                fn(rstd2[0:r, i:i + 1], rstd2[0:r, i:i + 1], ACT.Sqrt).then_inc(S("row_scales"), 1)

            def router_exps(i):
                r = ROWS[i]
                act.wait_ge(S("group_max"), i + 1)
                fn(r_ge[0:r, :], r_gl[0:r, 0:NG], ACT.Exp, bias=r_ng[0:r, :], accum_out=r_gs[0:r, :]
                   ).then_inc(S("group_sum"), 1)
                act.wait_ge(S("expert_gap"), i + 1)
                fn(r_e2[0:r, :], r_gap[0:r, :], ACT.Exp).then_inc(S("expert_ratio"), 1)

            for i in range(NT + 2):
                if i < NT:
                    norm2(i)
                if i >= 2:
                    router_exps(i - 2)

            def slot_count(n, u):
                return 16 * (n // 2 + 1) if isinstance(n, int) else 16 + (n - u) * 8

            def w_high(n, u):
                act.wait_ge(S(f"w_gate_exp_{u}"), slot_count(n, u))
                if not (isinstance(n, int) and n < 1):
                    act.wait_ge(S("gate"), n)
                for hf in range(2):
                    k = slice(4 * hf, 4 * hf + 4)
                    fn(w_hi[:, k, :], wgv[u][:, k, :], ACT.Copy).then_inc(S("w_high"), 1)

            def gate_out(n, u):
                act.wait_ge(S("gate"), n + 1)
                if not (isinstance(n, int) and n < 1):
                    act.wait_ge(S("gate_folded"), n)
                fn(m_g, ps[:, 1 + 2 * u, :], ACT.Copy).then_inc(S("gate_copied"), 1)

            def silu(n, u):
                act.wait_ge(S("gate_folded"), n + 1)
                if not (isinstance(n, int) and n < 2):
                    act.wait_ge(S("hidden"), n - 1)
                fn(m_s[0:BLK, u, :], ps[0:BLK, 1 + 2 * u, :], ACT.Silu).then_inc(S("silu"), 1)

            def y_out(n, u):
                act.wait_ge(S("down"), n + 1)
                if not (isinstance(n, int) and n < 2):
                    act.wait_ge(S(f"out_stored_{u}"), slot_count(n, u) - 16)
                fn(m_y[0:BLK, u, 0:512], ps[0:BLK, 5, :], ACT.Copy).then_inc(S("y_act"), 1)
                act.wait_ge(S("y_act"), n + 1)
                act.wait_ge(S("y_dve"), n + 1)
                act.dma_start(yg_dram[bass.ds(n * BLK, BLK), :], m_y[0:BLK, u, :]).then_inc(S(f"out_stored_{u}"), 16)

            w_high(0, 0)
            gate_out(0, 0)
            w_high(1, 1)
            silu(0, 0)
            gate_out(1, 1)
            w_high(2, 0)
            silu(1, 1)
            y_out(0, 0)
            with act.Fori(1, NE // 2 - 1) as it:
                for u in range(2):
                    gate_out(2 * it + u, u)
                    w_high(2 * it + u + 1, 1 - u)
                    silu(2 * it + u, u)
                    y_out(2 * it + u - 1, 1 - u)
            gate_out(NE - 2, 0)
            w_high(NE - 1, 1)
            silu(NE - 2, 0)
            y_out(NE - 3, 1)
            gate_out(NE - 1, 1)
            silu(NE - 1, 1)
            y_out(NE - 2, 0)
            y_out(NE - 1, 1)
            for u in range(2):
                act.wait_ge(S(f"out_stored_{u}"), 8 * NE)
            act.sem_inc(S("extra_stored"), 16)
            novf = act.value_load(tab[0:1, NOVF:NOVF + 1], min_val=0, max_val=NOVF)
            with act.Fori(0, NOVF) as i:
                with act.If(i < novf):
                    act.wait_ge(S("extra_products"), extra_stage(i, 2))
                    fn(m_s[0:BLK, 0, :], ps[0:BLK, 1, :], ACT.Silu).then_inc(S("extra_act"), 1)
                    act.wait_ge(S("extra_products"), extra_stage(i, 4))
                    act.wait_ge(S("extra_stored"), i * 16 + 16)
                    fn(m_y[0:BLK, 0, 0:512], ps[0:BLK, 5, :], ACT.Copy).then_inc(S("extra_act"), 1)
                    act.wait_ge(S("extra_act"), 2 * i + 2)
                    act.wait_ge(S("extra_dve"), 4 * i + 4)
                    act.dma_start(yg_dram[bass.ds((NE + i) * BLK, BLK), :], m_y[0:BLK, 0, :]).then_inc(S("extra_stored"), 16)
                with act.Else():
                    act.nop()
                act.nop()

        @block.vector
        def _(dve):
            v = nc.vector
            chain = Chain(dve, S("vector_chain"))
            stt = v.scalar_tensor_tensor

            def over(m, r, n, k):
                return m[0:r, 0:k].unsqueeze(1).to_broadcast([r, n, k])

            def turned_x(i, r):
                for kk in range(2):
                    n = 2 * i + kk
                    dve.wait_ge(S("x_turned"), n + 1)
                    v.tensor_tensor(hT[:, 4 * kk:4 * kk + 4, P * i:P * i + r], each(ps[:, 4 + n % 4, :], 4)[:, :, 0:r],
                                    w1c[:, 4 * kk:4 * kk + 4].unsqueeze(2).to_broadcast([P, 4, r]), ALU.mult
                                    ).then_inc(S("hT"), 1)

            for i, r in enumerate(ROWS):
                dve.wait_ge(S("row_roots"), i + 1)
                chain(v.reciprocal(rstd[0:r, i:i + 1], rstd[0:r, i:i + 1]))
                chain.wait()
                v.tensor_scalar(xt[0:r, i, :], xt[0:r, i, :], rstd[0:r, i:i + 1], None, ALU.mult).then_inc(S("x_normed"), 1)
                if i == 1:
                    dve.wait_ge(S("w1_loaded"), 16)
                if i:
                    turned_x(i - 1, ROWS[i - 1])
            turned_x(NT - 1, ROWS[NT - 1])
            dve.wait_ge(S("small_loaded"), 112)
            chain(v.tensor_copy(bias32[:, :].rearrange("p (h q) -> p h q", q=TQ), bias8[:, :].unsqueeze(2).to_broadcast([P, H, TQ])))

            def head_squares(m, xT):
                if m:
                    dve.wait_ge(S("head_sums"), 4 * m)
                v.tensor_tensor(flat(sq[m]), flat(xT), flat(xT), ALU.mult).then_inc(S("squares"), 1)

            def head_scaled(m, xT, c):
                dve.wait_ge(S("head_roots"), 4 * m + c + 1)
                chain(v.reciprocal(rs[m][:, c, :], rs[m][:, c, :]))
                chain.wait()
                stt(out=xT[:, c, :], in0=xT[:, c, :], scalar=qkg[:, m:m + 1], in1=rs[m][:, c, :],
                    op0=ALU.mult, op1=ALU.mult).then_inc(S("heads_normed"), 1)

            def head_norm(m, xT):
                head_squares(m, xT)
                for c in range(CT):
                    head_scaled(m, xT, c)

            dve.wait_ge(S("projection_out"), 4)
            head_norm(0, qT)
            dve.wait_ge(S("projection_out"), 8)
            head_norm(1, kT)
            for i, r in enumerate(ROWS):
                dve.wait_ge(S("k_turned_rows"), i + 1)
                v.tensor_copy(kout[0:r, i, :], ps[0:r, i % 4, :]).then_inc(S("k_rows"), 1)

            def rounding(e, t):
                chain(v.tensor_scalar(t, e, 1.0, -1.0, ALU.add, ALU.add))
                chain.wait()
                chain(v.tensor_tensor(t, e, t, ALU.subtract))

            def attn_pair_out(p):
                dve.wait_ge(S("attn_values"), 2 * p + 2)
                v.tensor_copy(osbT[:, p, 0:SEQ], ps[:, 3, :]).then_inc(S("attn_out"), 1)

            def bounds_shifted():
                dve.wait_ge(S("lb_loaded"), 16)
                chain(v.tensor_tensor(oml, lbr[:, 0, :], lbr[:, 1, :], ALU.max))
                chain.wait()
                chain(v.tensor_tensor(lbr[:, 0, :], lbr[:, 0, :], oml, ALU.subtract))
                v.tensor_tensor(lbr[:, 1, :], lbr[:, 1, :], oml, ALU.subtract).then_inc(S("lb_shifted"), 1)

            def bounds():
                dve.wait_ge(S("lb_exp"), 1)
                chain(v.tensor_tensor(oml, lbr[:, 0, :], lbr[:, 1, :], ALU.add))
                chain.wait()
                chain(v.reciprocal(oml, oml))
                chain.wait()
                chain(v.tensor_tensor(lb, lbr[:, 0, :], oml, ALU.mult))
                chain.wait()
                chain(v.tensor_scalar(oml, lb, -1.0, 1.0, ALU.mult, ALU.add))

            def forget(i):
                r = ROWS[i]
                f = ftok[0:r, i, :]
                dve.wait_ge(S("projection_out"), CHUNK_END[3] + i + 1)
                chain.wait()
                chain(v.tensor_scalar(f, f, 1.0, None, ALU.add))
                chain.wait()
                chain(v.reciprocal(f, f))
                chain.wait()
                chain(v.tensor_tensor(f, f, oml[0:r, :], ALU.mult))
                chain.wait()
                chain(v.tensor_tensor(f, f, lb[0:r, :], ALU.add))

            for h in range(H):
                dve.wait_ge(S("attn_softplus"), 3 * h + 2)
                rounding(a_e, a_t)
                dve.wait_ge(S("attn_softplus"), 3 * h + 3)
                chain(stt(out=a_L, in0=a_z, scalar=0.0, in1=a_ln, op0=ALU.max, op1=ALU.add))
                chain.wait()
                chain(v.tensor_tensor(a_L, a_L, a_t, ALU.add))
                chain.wait()
                chain(v.tensor_tensor(diag3(a_L_off), diag3(a_L_off), over(mask_lt, P, 3, P), ALU.mult))
                v.tensor_tensor(a_L[:, 896:1024], a_L[:, 896:1024], mask_lt[:, :], ALU.mult).then_inc(S("attn_losses"), 1)
                dve.wait_ge(S("attn_remains"), h + 1)
                chain(v.tensor_tensor(a_z, a_z, ps_attn, ALU.subtract))
                chain.wait()
                chain(v.tensor_tensor(diag3(a_z_off), diag3(a_z_off), over(neg_lt, P, 3, P), ALU.add))
                v.tensor_tensor(a_z[:, 896:1024], a_z[:, 896:1024], neg_lt[:, :], ALU.add).then_inc(S("attn_args"), 1)
                if h == 1:
                    bounds_shifted()
                elif h == 2:
                    bounds()
                elif h >= 3:
                    forget(h - 3)
                if h % 2 == 0 and h:
                    attn_pair_out(h // 2 - 1)
            attn_pair_out(CT - 1)
            chain.wait()

            dve.wait_ge(S("states_zero"), 1)
            for b in range(NB):
                last = v.tensor_scalar(ib[0:TS, b, :], itok[0:TS, 4, :], in_b[:, b:b + 1], None, ALU.mult)
            last.then_inc(S("ib"), 1)

            def keys_of_f(i):
                r = ROWS[i]
                if i:
                    dve.wait_ge(S("decay_sums"), i)
                    dve.wait_ge(S("decayed"), 3 * i)
                v.tensor_scalar(ktok[0:r, :], ftok[0:r, i, :], -1.0, 1.0, ALU.mult, ALU.add).then_inc(S("f"), 1)

            def state_update(dst, src, bank, col):
                for c in range(CT):
                    for e in range(2):
                        hs = slice(64 * e, 64 * e + 64)
                        last = stt(out=dst[hs, c, hs], in0=src[hs, c, hs], scalar=g_e[hs, col(c):col(c) + 1],
                                   in1=ps[hs, bank, P * c + 64 * e:P * c + 64 * e + 64], op0=ALU.mult, op1=ALU.add)
                return last

            for i, r in enumerate(ROWS):
                keys_of_f(i)
                dve.wait_ge(S("decays"), 3 * i + 3)
                if i:
                    dve.wait_ge(S("hg_out"), i)
                cols = slice(P * i, P * i + r)
                v.tensor_tensor(qd[:, :, 0:r], hqT[:, :, cols], each(g_e[:, 0:CT * r], CT), ALU.mult).then_inc(S("decayed"), 1)
                v.tensor_tensor(kd[:, :, 0:r], each(ps[:, 2, 0:CT * r], CT), each(g_en[:, 0:CT * r], CT), ALU.mult
                                ).then_inc(S("decayed"), 1)
                dve.wait_ge(S("f"), i + 1)
                v.tensor_tensor(kdec[0:r, :], ktok[0:r, :], g_e2[0:r, :], ALU.mult).then_inc(S("decayed"), 1)
                dve.wait_ge(S("hg_scores"), i + 1)
                for e in range(2):
                    v.tensor_tensor(scm[0:r, 4 * e:4 * e + 4, 0:r], each(ps[0:r, 3 + e, 0:CT * r], CT),
                                    over(chk_le if i < 4 else sq_le, r, CT, r), ALU.mult).then_inc(S("hg_masked"), 1)
                if i < 4:
                    for k in range(4):
                        x = 4 * i + k
                        dve.wait_ge(S("chunk_kv"), x + 1)
                        if x:
                            dve.wait_ge(S("chunk_states"), x)
                        state_update(state[:, (x + 1) % 8], state[:, x % 8], KV_BANK[k],
                                     lambda c: P * c + CHUNK * k + CHUNK - 1).then_inc(S("chunk_states"), 1)
                dve.wait_ge(S("hg_out"), i + 1)
                if i == 0:
                    dve.wait_ge(S("rows_zeroed"), 48)
                v.tensor_copy(ybT[:, :, cols], each(ps[:, 1, 0:CT * r], CT)).then_inc(S("o_read"), 1)
            for b in range(NB):
                dve.wait_ge(S("sample_kv"), b + 1)
                state_update(state0[:, b], state0[:, b], KV_BANK[b % 4], lambda c: TS * c + TQ * b + TQ - 1
                             ).then_inc(S("sample_states"), 1)
            dve.wait_ge(S("o_read"), NT)
            head_squares(2, ybT)

            dve.wait_ge(S("states_stored"), 16 * (2 + 2 * NB))
            chain(v.memset(flat(qblk), 0.0))
            chain(v.memset(flat(carry0), 0.0))
            chain.wait()
            for e in range(2):
                hs = slice(64 * e, 64 * e + 64)
                for c in range(CT):
                    dst = qblk[hs, :, :].rearrange("p b (c e q) -> p c e b q", c=CT, e=2)[:, c, e]
                    last = v.tensor_copy(dst, qT[hs, c, SEQ:T].rearrange("p (b q) -> p b q", b=NB))
            last.then_inc(S("q_blocks"), 1)
            head_scaled(2, ybT, 0)
            dve.wait_ge(S("new_products"), 1)
            for c in range(CT):
                z4 = n_z[0:TS, 64 * c:64 * c + 64].rearrange("p (b x) -> p b x", b=NB)
                last = stt(out=z4, in0=ps[0:TS, 4, 64 * c:64 * c + 64].rearrange("p (b x) -> p b x", b=NB), scalar=SCALE,
                           in1=bias32[0:TS, 8 * c:8 * c + 8].unsqueeze(1).to_broadcast([TS, NB, 8]),
                           op0=ALU.mult, op1=ALU.add)
            last.then_inc(S("new_rows"), 1)
            head_scaled(2, ybT, 1)
            dve.wait_ge(S("new_act"), 3)
            rounding(n_e[0:TS, :], n_t[0:TS, :])
            dve.wait_ge(S("new_rows"), 1)
            chain(stt(out=n_L[0:TS, :], in0=n_z[0:TS, :], scalar=0.0, in1=n_s[0:TS, :], op0=ALU.max, op1=ALU.add))
            chain.wait()
            chain(v.tensor_tensor(n_L[0:TS, :], n_L[0:TS, :], n_t[0:TS, :], ALU.add))
            chain.wait()
            v.tensor_tensor(n_L[0:TS, :], n_L[0:TS, :], new_m[:, :], ALU.mult).then_inc(S("new_rows"), 1)
            dve.wait_ge(S("new_rows"), 2)
            for b in range(NB):
                chain(v.tensor_copy(carry0[0:TS, b, :].rearrange("p (c x) -> p c x", c=CT),
                                    n_L[0:TS, :].rearrange("p (c b x) -> p b c x", c=CT, b=NB)[:, b]))
            head_scaled(2, ybT, 2)
            dve.wait_ge(S("new_products"), 2)
            chain(v.tensor_tensor(n_z[0:TS, :], n_z[0:TS, :], ps[0:TS, 5, 0:256], ALU.subtract))
            chain.wait()
            v.tensor_tensor(n_z[0:TS, :], n_z[0:TS, :], new_neg[:, :], ALU.add).then_inc(S("new_rows"), 1)
            head_scaled(2, ybT, 3)
            dve.wait_ge(S("new_products"), 3)
            v.tensor_copy(flat(obase), ps[:, 6, 0:256]).then_inc(S("new_rows"), 1)
            dve.wait_ge(S("new_rows"), 4)
            dve.wait_ge(S("g_sigmoid"), 1)
            chain(v.tensor_tensor(flat(gT), flat(gT), flat(hqT), ALU.mult))
            chain.wait()
            dve.wait_ge(S("heads_normed"), 3 * CT)
            v.tensor_tensor(flat(ybT), flat(ybT), flat(gT), ALU.mult).then_inc(S("yb"), 1)

            def turned_out(b, g):
                n = b * NGRP + g
                for j in range(2, GP):
                    dve.wait_ge(S("page_turned"), 4 * n + j + 1)
                    if not isinstance(n, int) or n >= 2:
                        dve.wait_ge(S("page_scores"), n - 1)
                    v.tensor_copy(d_kt[:, g % 2, j, :], ps[:, j, :]).then_inc(S("kT_dve"), 1)

            def values_out(b):
                dve.wait_ge(S("values_summed"), (b + 1) * NGRP)
                v.tensor_copy(d_o[0:32, :], ps[0:32, 6, :]).then_inc(S("values_out"), 1)

            def losses(b, g, sums_of=None):
                n = b * NGRP + g
                z, e, t, L = (x[:, g % 2, :] for x in (d_z, d_e, d_t, d_L))
                dve.wait_ge(S("page_scores"), n + 1)
                if not isinstance(n, int) or n >= 2:
                    dve.wait_ge(S("page_weights"), n - 1)
                stt(out=each(z, GP), in0=each(ps[:, 4 + g % 2, 0:128], GP), scalar=SCALE,
                    in1=bias32[:, :].unsqueeze(1).to_broadcast([P, GP, 32]), op0=ALU.mult, op1=ALU.add
                    ).then_inc(S("page_z"), 1)
                if sums_of is not None:
                    values_out(sums_of)
                if g == 0:
                    chain(v.tensor_copy(d_R[:, 0, 0:32], carry0[:, bass.ds(b, 1), :].rearrange("p o c -> p (o c)")))
                dve.wait_ge(S("page_softplus"), 3 * n + 2)
                rounding(e, t)
                dve.wait_ge(S("page_softplus"), 3 * n + 3)
                chain(stt(out=L, in0=z, scalar=0.0, in1=d_ln[:, g % 2, :], op0=ALU.max, op1=ALU.add))
                chain.wait()
                chain(v.tensor_tensor(L, L, t, ALU.add))
                chain.wait()
                R = d_R[:, g % 4, :]
                for j in range(GP - 1):
                    add = v.tensor_tensor(R[:, 32 * j + 32:32 * j + 64], R[:, 32 * j:32 * j + 32], L[:, 32 * j:32 * j + 32],
                                          ALU.add)
                    if j < GP - 2:
                        chain(add)
                        chain.wait()
                add.then_inc(S("page_sums"), 1)
                dve.wait_ge(S("page_sums"), n + 1)
                if g < NGRP - 1:
                    chain(v.tensor_tensor(d_R[:, (g + 1) % 4, 0:32], R[:, 96:128], L[:, 96:128], ALU.add))

            def args(b, g):
                n = b * NGRP + g
                dve.wait_ge(S("page_remains"), n + 1)
                v.tensor_tensor(d_z[:, g % 2, :], d_z[:, g % 2, :], ps[:, 4 + g % 2, 128:256], ALU.subtract
                                ).then_inc(S("page_args"), 1)

            def decoded(b):
                dve.wait_ge(S("values_turned"), b + 1)
                for e in range(2):
                    hs = slice(64 * e, 64 * e + 64)
                    got = ps[hs, 7, 4 * e:4 * e + 160].rearrange("p (c x) -> p c x", c=CT)[:, :, 0:TQ]
                    new = obase[hs, :, :].rearrange("p c (b e q) -> p e c b q", b=NB, e=2)[:, e, :, bass.ds(b, 1), :]
                    out = osbT[hs, :, SEQ:T].rearrange("p c (b q) -> p c b q", b=NB)[:, :, bass.ds(b, 1), :]
                    last = v.tensor_tensor(out, got.unsqueeze(2), new, ALU.add)
                last.then_inc(S("decoded"), 1)

            def before(b, g, lag):
                return (b, g - lag) if g >= lag else (b - 1, g - lag + NGRP)

            def decode_steps(b):
                for g in range(NGRP):
                    turned_out(b, g)
                    if g >= 2 or not first(b):
                        args(*before(b, g, 2))
                    if g >= 1 or not first(b):
                        losses(*before(b, g, 1), sums_of=b - 1 if g == 2 and not first(b) else None)
                    if g == 4 and not first(b):
                        decoded(b - 1)

            decode_steps(0)
            start, per_sequence = chain.base + chain.n, LOSS_CHAIN * NGRP
            decode_steps(1)
            with dve.Fori(1, NB // 2) as pair:
                for u in range(2):
                    b = 2 * pair + u
                    chain.base, chain.n = start + (b - 1) * per_sequence, 0
                    decode_steps(b)
            assert chain.n == per_sequence
            chain.base, chain.n = start + (NB - 1) * per_sequence, 0
            args(NB - 1, NGRP - 2)
            losses(NB - 1, NGRP - 1)
            args(NB - 1, NGRP - 1)
            values_out(NB - 1)
            decoded(NB - 1)

            for m in range(KD):
                dve.wait_ge(S("branch_products"), 4 * m + 3)
                dve.wait_ge(S("gates_read"), 2 * m + 2)
                v.tensor_tensor(each(mrg[:, m, :], 2), each(m_sa[:, m % 2, :], 2), ps[:, 4:6, 0:TH], ALU.mult
                                ).then_inc(S("branches_read"), 1)
                dve.wait_ge(S("branch_products"), 4 * m + 4)
                v.tensor_tensor(each(m_sb[:, m % 2, :], 2), each(m_sb[:, m % 2, :], 2), ps[:, 6:8, 0:TH], ALU.mult
                                ).then_inc(S("branches_read"), 1)
                dve.wait_ge(S("branches_read"), 2 * m + 2)
                v.tensor_tensor(mrg[:, m, :], mrg[:, m, :], m_sb[:, m % 2, :], ALU.add).then_inc(S("merged"), 1)
            dve.wait_ge(S("merged"), KD)
            v.memset(route, 0.0).then_inc(S("route_zero"), 1)
            dve.wait_ge(S("x_again"), 16 * NT)

            def norm2(i):
                r = ROWS[i]
                dve.wait_ge(S("mixed"), i + 1)
                v.tensor_tensor(each(x2[0:r, i, :], 2), each(x2[0:r, i, :], 2), ps[0:r, 2 * (i % 2):2 * (i % 2) + 2, :],
                                ALU.add).then_inc(S("x2"), 1)
                dve.wait_ge(S("row_squares"), NT + i + 1)
                chain(v.tensor_scalar(rstd2[0:r, i:i + 1], ss2[0:r, i:i + 1], 1.0 / D, EPS, ALU.mult, ALU.add))
                chain.wait()
                v.reciprocal(rstd2[0:r, i:i + 1], rstd2[0:r, i:i + 1]).then_inc(S("row_inverses"), 1)
                dve.wait_ge(S("row_scales"), 1 + i)
                dve.wait_ge(S("router_inputs"), 80)
                dve.wait_ge(S("x2"), i + 1)
                stt(out=h2[0:r, i, :], in0=x2[0:r, i, :], scalar=rstd2[0:r, i:i + 1], in1=w2r[0:r, :],
                    op0=ALU.mult, op1=ALU.mult).then_inc(S("h2"), 1)

            def step(ins):
                chain(ins)
                chain.wait()

            def h2_cols(i):
                r = ROWS[i]
                dve.wait_ge(S("h2_turned"), i + 1)
                if i >= 2:
                    dve.wait_ge(S("logits"), i - 1)
                v.tensor_copy(h2T[:, i % 2, :, 0:r], ps_h2[:, :, 0:r]).then_inc(S("h2_cols"), 1)

            def choose(i):
                r = ROWS[i]
                dve.wait_ge(S("logits"), i + 1)
                g, x = slice(0, r), slice(NG, NG + NE)
                v.tensor_tensor(r_lg[g, :], ps[g, 6, 0:NG + NE], r_b36[g, :], ALU.add).then_inc(S("logits_read"), 1)
                dve.wait_ge(S("logits_read"), i + 1)
                chain(v.memset(r_gl[g, NG:8], -BIG))
                step(v.tensor_copy(r_gl[g, 0:NG], r_lg[g, 0:NG]))
                step(v.max(r_gm[g, :], r_gl[g, :]))
                chain(v.max_index(r_gi[g, :], r_gm[g, :], r_gl[g, :]))
                v.tensor_scalar(r_ng[g, :], r_gm[g, 0:1], -1.0, None, ALU.mult).then_inc(S("group_max"), 1)
                chain.wait()
                step(v.tensor_copy(r_gf[g, :], r_gi[g, 0:1]))
                step(v.tensor_scalar(r_m[g, :], gcol[g, :], r_gf[g, :], None, ALU.is_equal))
                chain(v.tensor_scalar(r_n[g, :], r_m[g, :], BIG, -BIG, ALU.mult, ALU.add))
                step(v.tensor_tensor(r_el[g, :], r_lg[g, x], r_m[g, :], ALU.mult))
                step(v.tensor_tensor(r_el[g, :], r_el[g, :], r_n[g, :], ALU.add))
                step(v.max(r_em[g, :], r_el[g, :]))
                chain(v.max_index(r_ei[g, :], r_em[g, :], r_el[g, :]))
                v.tensor_tensor(r_gap[g, :], r_em[g, 1:2], r_em[g, 0:1], ALU.subtract).then_inc(S("expert_gap"), 1)
                chain.wait()
                step(v.tensor_copy(r_EI[g, 2 * i:2 * i + 2], r_ei[g, 0:2]))
                for k in range(2):
                    chain(v.tensor_scalar(r_Ok[g, 2 * i + k, :], ecol[g, :], r_EI[g, 2 * i + k:2 * i + k + 1], None, ALU.is_equal))
                chain.wait()
                v.tensor_tensor(r_O[g, NE * i:NE * i + NE], r_Ok[g, 2 * i, :], r_Ok[g, 2 * i + 1, :], ALU.add
                                ).then_inc(S("chosen"), 1)
                dve.wait_ge(S("group_sum"), i + 1)
                dve.wait_ge(S("expert_ratio"), i + 1)
                step(v.tensor_scalar(r_t1[g, :], r_e2[g, :], 1.0, None, ALU.add))
                step(v.tensor_tensor(r_t1[g, :], r_t1[g, :], r_gs[g, :], ALU.mult))
                step(v.reciprocal(wts[g, 2 * i:2 * i + 1], r_t1[g, :]))
                step(v.tensor_tensor(wts[g, 2 * i + 1:2 * i + 2], wts[g, 2 * i:2 * i + 1], r_e2[g, :], ALU.mult))

            for i in range(NT + 2):
                if i < NT:
                    norm2(i)
                if 1 <= i <= NT:
                    h2_cols(i - 1)
                if i == 2:
                    dve.wait_ge(S("router_inputs"), 80)
                    dve.wait_ge(S("counters"), 2)
                if i >= 2:
                    choose(i - 2)
            dve.wait_ge(S("list_sums"), 1)
            step(v.tensor_copy(r_cnt[0:NE, :], ps[0:NE, 6, 0:P]))
            step(v.tensor_scalar(r_ov[0:NE, :], r_cnt[0:NE, :], float(BLK), None, ALU.is_gt))
            for k in range(2, KMAX + 1):
                add = stt(out=r_ov[0:NE, :], in0=r_cnt[0:NE, :], scalar=float(BLK * k), in1=r_ov[0:NE, :],
                          op0=ALU.is_gt, op1=ALU.add)
                if k < KMAX:
                    step(add)
            add.then_inc(S("extra_blocks"), 1)
            chain(v.tensor_copy(r_rank[:, 0:NE * 4], ps[:, 7, 0:NE * 4]))
            chain(v.tensor_copy(r_rank[0:TS, NE * 4:NE * 5], ps[0:TS, 7, NE * 4:NE * 5]))
            dve.wait_ge(S("list_sums"), 2)
            chain(v.tensor_copy(r_base[:, :], ps[:, 5, 0:NE]))
            chain(v.tensor_copy(r_incl[0:NE, :], ps[0:NE, 5, NE:NE + 1]))
            chain(v.tensor_copy(tab[0:1, NOVF:NOVF + 1], ps[0:1, 5, NE + 1:NE + 2]))
            chain.wait()
            v.tensor_scalar(r_ind[0:NE, :], ecol[0:NE, 0:NOVF], r_incl[0:NE, :], None, ALU.is_ge).then_inc(S("extra_after"), 1)
            for i, r in enumerate(ROWS):
                for k in range(2):
                    col = slice(2 * i + k, 2 * i + k + 1)
                    step(v.tensor_tensor_reduce(r_j[0:r, :], r_Ok[0:r, 2 * i + k, :], r_rank[0:r, NE * i:NE * i + NE], 1.0, 0.0,
                                                ALU.mult, ALU.add, r_RK[0:r, col]))
                    step(v.tensor_tensor_reduce(r_j[0:r, :], r_Ok[0:r, 2 * i + k, :], r_base[0:r, :], 1.0, 0.0,
                                                ALU.mult, ALU.add, r_BK[0:r, col]))
            step(v.tensor_tensor(r_BK, r_BK, r_EI, ALU.subtract))
            step(v.tensor_scalar(r_BK, r_BK, float(BLK), float((NE - 1) * BLK), ALU.mult, ALU.add))
            step(stt(out=r_BK, in0=r_RK, scalar=float(BLK), in1=r_BK, op0=ALU.is_ge, op1=ALU.mult))
            step(v.tensor_tensor(r_RK, r_RK, r_BK, ALU.add))
            step(stt(out=r_RK, in0=r_EI, scalar=float(BLK), in1=r_RK, op0=ALU.mult, op1=ALU.add))
            v.tensor_copy(slot_i[:, :], r_RK).then_inc(S("slots"), 1)
            dve.wait_ge(S("list_sums"), 3)
            step(v.tensor_scalar(r_ov[0:1, 0:NOVF], ps[0:1, 4, 0:NOVF], float(NE - 1), None, ALU.min))
            v.tensor_copy(tab[0:1, 0:NOVF], r_ov[0:1, 0:NOVF]).then_inc(S("extra_table"), 1)

            def cols_out(n, u):
                dve.wait_ge(S("rows_turned"), n + 1)
                if not (isinstance(n, int) and n < 2):
                    dve.wait_ge(S("gate_up"), n - 1)
                v.tensor_copy(flat(xgT[:, u]), ps[:, 0, :]).then_inc(S("xg_cols"), 1)
                dve.wait_ge(S("xg_cols"), n + 1)
                if not (isinstance(n, int) and n < 1):
                    dve.wait_ge(S("gate"), n)
                v.tensor_copy(xg_parts[:, :, 0:BLK], xgT[:, u]).then_inc(S("xg_high"), 1)
                dve.wait_ge(S("xg_high"), n + 1)
                v.tensor_tensor(xg_parts[:, :, BLK:P], xgT[:, u], xg_parts[:, :, 0:BLK], ALU.subtract
                                ).then_inc(S("xg_split"), 1)

            def w_low(n, u):
                for hf in range(2):
                    k = slice(4 * hf, 4 * hf + 4)
                    dve.wait_ge(S("w_high"), 2 * n + hf + 1)
                    last = v.tensor_tensor(w_lo[:, k, :], wgv[u][:, k, :], w_hi[:, k, :], ALU.subtract)
                last.then_inc(S("w_low"), 1)

            def hidden(n, u):
                dve.wait_ge(S("silu"), n + 1)
                if not (isinstance(n, int) and n < 2):
                    dve.wait_ge(S("hidden_turned"), n - 1)
                v.tensor_tensor(m_hr[0:BLK, u, :], m_s[0:BLK, u, :], ps[0:BLK, 2 + 2 * u, :], ALU.mult
                                ).then_inc(S("hidden"), 1)

            def hidden_cols(n, u):
                dve.wait_ge(S("hidden_turned"), n + 1)
                v.tensor_copy(flat(m_h[:, u]), ps[:, 7, FJ * BLK * u:FJ * BLK * u + FJ * BLK]).then_inc(S("hidden_cols"), 1)

            def y_out(n, u):
                dve.wait_ge(S("down"), n + 1)
                if not (isinstance(n, int) and n < 2):
                    dve.wait_ge(S(f"out_stored_{u}"), (n - u) * 8)
                v.tensor_copy(m_y[0:BLK, u, 512:D], ps[0:BLK, 6, :]).then_inc(S("y_dve"), 1)

            w_low(0, 0)
            cols_out(0, 0)
            w_low(1, 1)
            hidden(0, 0)
            cols_out(1, 1)
            hidden_cols(0, 0)
            w_low(2, 0)
            hidden(1, 1)
            cols_out(2, 0)
            y_out(0, 0)
            with dve.Fori(1, NE // 2 - 1) as it:
                for u in range(2):
                    hidden_cols(2 * it + u - 1, 1 - u)
                    w_low(2 * it + u + 1, 1 - u)
                    hidden(2 * it + u, u)
                    cols_out(2 * it + u + 1, 1 - u)
                    y_out(2 * it + u - 1, 1 - u)
            hidden_cols(NE - 3, 1)
            w_low(NE - 1, 1)
            hidden(NE - 2, 0)
            cols_out(NE - 1, 1)
            y_out(NE - 3, 1)
            hidden_cols(NE - 2, 0)
            hidden(NE - 1, 1)
            y_out(NE - 2, 0)
            hidden_cols(NE - 1, 1)
            y_out(NE - 1, 1)
            dve.wait_ge(S("extra_table"), 1)
            novf = dve.value_load(tab[0:1, NOVF:NOVF + 1], min_val=0, max_val=NOVF)
            with dve.Fori(0, NOVF) as i:
                with dve.If(i < novf):
                    dve.wait_ge(S("extra_products"), extra_stage(i, 1))
                    v.tensor_copy(flat(xgT[:, 0]), ps[:, 0, :]).then_inc(S("extra_dve"), 1)
                    dve.wait_ge(S("extra_act"), 2 * i + 1)
                    v.tensor_tensor(m_hr[0:BLK, 0, :], m_s[0:BLK, 0, :], ps[0:BLK, 2, :], ALU.mult).then_inc(S("extra_dve"), 1)
                    dve.wait_ge(S("extra_products"), extra_stage(i, 3))
                    v.tensor_copy(flat(m_h[:, 0]), ps[:, 7, 0:FJ * BLK]).then_inc(S("extra_dve"), 1)
                    dve.wait_ge(S("extra_products"), extra_stage(i, 4))
                    dve.wait_ge(S("extra_stored"), i * 16 + 16)
                    v.tensor_copy(m_y[0:BLK, 0, 512:D], ps[0:BLK, 6, :]).then_inc(S("extra_dve"), 1)
                with dve.Else():
                    dve.nop()
                dve.nop()
            for i, r in enumerate(ROWS):
                dve.wait_ge(S(f"y_gathered_{i}"), 32)
                step(stt(out=x2[0:r, i, :], in0=yg[0:r, 2 * i, :], scalar=wts[0:r, 2 * i:2 * i + 1], in1=x2[0:r, i, :],
                         op0=ALU.mult, op1=ALU.add))
                stt(out=x2[0:r, i, :], in0=yg[0:r, 2 * i + 1, :], scalar=wts[0:r, 2 * i + 1:2 * i + 2], in1=x2[0:r, i, :],
                    op0=ALU.mult, op1=ALU.add).then_inc(S("y_rows"), 1)


_INS = ["x_prompt", "x_sample", "cache_k", "cache_v", "page_table", "state_hgrn", "norm1_w", "w_in", "q_norm_w",
        "k_norm_w", "sb_bias", "lb_logits", "hg_norm_w", "w_branch_a", "w_branch_b", "w_out", "norm2_w",
        "w_group_router", "b_group_router", "w_expert_router", "b_expert_router", "w_gate_exp", "w_up_exp",
        "w_down_exp"]
_OUTS = [("y_prompt", (1, SEQ, D)), ("y_sample", (NB, TQ, D)), ("new_k_prompt", (1, 1, SEQ, H, DH)),
         ("new_v_prompt", (1, 1, SEQ, H, DH)), ("new_hgrn_prompt", (1, 1, H, DH, DH)),
         ("new_k_sample", (1, NB, TQ, H, DH)), ("new_v_sample", (1, NB, TQ, H, DH)),
         ("new_hgrn_sample", (1, NB, H, DH, DH))]


def kernel(**inputs):
    import numpy as _np
    import concourse.bacc as _bacc
    from concourse import mybir as _mybir
    from concourse.bass_utils import run_bass_kernel_spmd as _run

    nc = _bacc.Bacc("TRN2", target_bir_lowering=False, num_devices=1)
    arrays, aps = {}, {}
    for name in _INS:
        x = _np.ascontiguousarray(inputs[name])
        arrays[f"in_{name}"] = x
        aps[name] = nc.dram_tensor(f"in_{name}", x.shape, _mybir.dt.from_np(x.dtype), kind="ExternalInput").ap()
    for name, shape in _OUTS:
        aps[name] = nc.dram_tensor(name, shape, F32, kind="ExternalOutput").ap()
    hybrid_step(nc, aps)
    r = _run(nc, [arrays], core_ids=[0])
    return tuple(r.results[0][name] for name, _ in _OUTS)
```
